# Optimizing a Trainium2 kernel written in Bass

```python
import math
import jax, jax.numpy as jnp
from jax import lax
import numpy as np

D_MODEL = 1024
BATCH = 1
SEQ = 256
DEPTH = 1

ATT_HEADS = 8
ATT_HEAD_DIM = 64
ATT_QK_WIDTH = ATT_HEADS * 2 * ATT_HEAD_DIM
ATT_V_WIDTH = ATT_HEADS * 2 * ATT_HEAD_DIM
BLOCK_Q = 128
SSM_WIDTH = 512
SSM_GROUP = 16
SSM_GROUPS = SSM_WIDTH // SSM_GROUP
SSM_STATE = 64
DT_MIN = 0.001
DT_MAX = 0.1
N_BRANCH = 2
IN_WIDTH = 2 * ATT_QK_WIDTH + ATT_V_WIDTH + SSM_WIDTH + N_BRANCH * D_MODEL
N_GROUPS = 4
EXPERTS_PER_GROUP = 8
N_EXPERTS = N_GROUPS * EXPERTS_PER_GROUP
EXPERT_FF = 256
TOP_K_INNER = 2
PLE_DIM = 256
EPS = 1e-6

kernel_name = 'hybrid_s5_diffattn_hiermoe_ple'

def rms_norm(x, g):
    xf = x.astype(jnp.float32)
    y = xf * lax.rsqrt(jnp.mean(xf * xf, axis=-1, keepdims=True) + EPS)
    return (y * g.astype(jnp.float32)).astype(x.dtype)

def lambda_init_for(layer_idx):
    return 0.8 - 0.6 * math.exp(-0.3 * layer_idx)

def diff_attention(q, k, v, lam):
    s = q.shape[1]
    scale = ATT_HEAD_DIM ** -0.5
    outs = []
    for blk in range(s // BLOCK_Q):
        q0 = blk * BLOCK_Q
        kv_len = q0 + BLOCK_Q
        qb = q[:, q0:kv_len]
        kb = k[:, :kv_len]
        vb = v[:, :kv_len]
        scores = jnp.einsum('bqhmd,bkhmd->bhmqk', qb, kb).astype(jnp.float32) * scale
        q_pos = q0 + jnp.arange(BLOCK_Q)[:, None]
        k_pos = jnp.arange(kv_len)[None, :]
        scores = jnp.where(k_pos <= q_pos, scores, -jnp.inf)
        probs = jax.nn.softmax(scores, axis=-1)
        w = probs[:, :, 0] - lam * probs[:, :, 1]
        outs.append(jnp.einsum('bhqk,bkhe->bqhe', w.astype(v.dtype), vb))
    return jnp.concatenate(outs, axis=1)

def _complex_linear_combine(e1, e2):
    a1r, a1i, b1r, b1i = e1
    a2r, a2i, b2r, b2i = e2
    ar = a2r * a1r - a2i * a1i
    ai = a2r * a1i + a2i * a1r
    br = a2r * b1r - a2i * b1i + b2r
    bi = a2r * b1i + a2i * b1r + b2i
    return (ar, ai, br, bi)

def s5_ssm(u, lam_re, lam_im, log_step, b_re, b_im, c_re, c_im, d_skip):
    f32 = jnp.float32
    bsz, s, _ = u.shape
    uf = u.astype(f32).reshape(bsz, s, SSM_GROUPS, SSM_GROUP)
    lr = lam_re.astype(f32)
    li = lam_im.astype(f32)
    dt = jnp.exp(log_step.astype(f32))[:, None]
    mag = jnp.exp(lr * dt)
    ab_re = mag * jnp.cos(li * dt)
    ab_im = mag * jnp.sin(li * dt)
    den = lr * lr + li * li
    nr = ab_re - 1.0
    coef_re = (nr * lr + ab_im * li) / den
    coef_im = (ab_im * lr - nr * li) / den
    br = b_re.astype(f32)
    bi = b_im.astype(f32)
    bb_re = coef_re[..., None] * br - coef_im[..., None] * bi
    bb_im = coef_re[..., None] * bi + coef_im[..., None] * br
    bu_re = jnp.einsum('bsgh,gph->bsgp', uf, bb_re)
    bu_im = jnp.einsum('bsgh,gph->bsgp', uf, bb_im)
    a_re = jnp.broadcast_to(ab_re, bu_re.shape)
    a_im = jnp.broadcast_to(ab_im, bu_im.shape)
    _, _, st_re, st_im = lax.associative_scan(_complex_linear_combine, (a_re, a_im, bu_re, bu_im), axis=1)
    y = (jnp.einsum('bsgp,ghp->bsgh', st_re, c_re.astype(f32))
         - jnp.einsum('bsgp,ghp->bsgh', st_im, c_im.astype(f32))
         + d_skip.astype(f32) * uf)
    return y.reshape(bsz, s, SSM_WIDTH).astype(u.dtype)

def hier_moe(h, w_rg, b_rg, w_re, b_re, w_g, w_u, w_d):
    f32 = jnp.float32
    bsz, s, d = h.shape
    t = h.reshape(-1, d)
    logits_grp = (t @ w_rg + b_rg).astype(f32)
    probs_grp = jax.nn.softmax(logits_grp, axis=-1)
    grp = jnp.argmax(logits_grp, axis=-1)
    p_grp = jnp.take_along_axis(probs_grp, grp[:, None], axis=-1)
    logits_exp = (jnp.einsum('td,nde->tne', t, w_re) + b_re).astype(f32)
    logits_sel = jnp.take_along_axis(logits_exp, grp[:, None, None], axis=1)[:, 0]
    top_vals, top_idx = lax.top_k(logits_sel, TOP_K_INNER)
    top_w = jax.nn.softmax(top_vals, axis=-1) * p_grp
    w_local = jnp.einsum('tk,tke->te', top_w, jax.nn.one_hot(top_idx, EXPERTS_PER_GROUP, dtype=f32))
    out = jnp.zeros_like(t)
    for n in range(N_GROUPS):
        w_n = jnp.where((grp == n)[:, None], w_local, 0.0).astype(t.dtype)
        hg = jnp.einsum('td,edf->tef', t, w_g[n])
        hu = jnp.einsum('td,edf->tef', t, w_u[n])
        act = jax.nn.silu(hg) * hu * w_n[:, :, None]
        out = out + jnp.einsum('tef,efd->td', act, w_d[n])
    return out.reshape(bsz, s, d)

def setup_inputs(seed: int = 0) -> dict:
    key = jax.random.key(seed)
    ks = jax.random.split(key, 40)
    f32 = jnp.float32

    def nrm(k, shape, scale):
        return jax.random.normal(k, shape, f32) * scale

    def gain(k, shape):
        return 1.0 + 0.02 * jax.random.normal(k, shape, f32)

    G, P, H = SSM_GROUPS, SSM_STATE, SSM_GROUP
    lam_im_base = jnp.pi * jnp.arange(P, dtype=f32)
    return {
        'x': nrm(ks[0], (BATCH, SEQ, D_MODEL), 1.0),
        'p': nrm(ks[1], (DEPTH, BATCH, SEQ, PLE_DIM), 1.0),
        'attn_norm_g': gain(ks[2], (DEPTH, D_MODEL)),
        'w_in': nrm(ks[3], (DEPTH, D_MODEL, IN_WIDTH), D_MODEL ** -0.5),
        'b_gate': nrm(ks[4], (DEPTH, N_BRANCH * D_MODEL), 0.01),
        'q_norm_g': gain(ks[5], (DEPTH, 2, ATT_HEAD_DIM)),
        'k_norm_g': gain(ks[6], (DEPTH, 2, ATT_HEAD_DIM)),
        'lam_qk': nrm(ks[7], (DEPTH, 4, ATT_HEAD_DIM), 0.1),
        'subln_g': gain(ks[8], (DEPTH, 2 * ATT_HEAD_DIM)),
        'w_attn_up': nrm(ks[9], (DEPTH, ATT_V_WIDTH, D_MODEL), ATT_V_WIDTH ** -0.5),
        'ssm_lam_re': -0.5 + 0.01 * jax.random.normal(ks[10], (DEPTH, G, P), f32),
        'ssm_lam_im': lam_im_base + 0.01 * jax.random.normal(ks[11], (DEPTH, G, P), f32),
        'ssm_log_step': jax.random.uniform(ks[12], (DEPTH, G), f32, math.log(DT_MIN), math.log(DT_MAX)),
        'ssm_b_re': nrm(ks[13], (DEPTH, G, P, H), (2 * H) ** -0.5),
        'ssm_b_im': nrm(ks[14], (DEPTH, G, P, H), (2 * H) ** -0.5),
        'ssm_c_re': nrm(ks[15], (DEPTH, G, H, P), (2 * P) ** -0.5),
        'ssm_c_im': nrm(ks[16], (DEPTH, G, H, P), (2 * P) ** -0.5),
        'ssm_d': nrm(ks[17], (DEPTH, G, H), 1.0),
        'w_glu': nrm(ks[18], (DEPTH, SSM_WIDTH, SSM_WIDTH), SSM_WIDTH ** -0.5),
        'b_glu': nrm(ks[19], (DEPTH, SSM_WIDTH), 0.01),
        'w_ssm_up': nrm(ks[20], (DEPTH, SSM_WIDTH, D_MODEL), SSM_WIDTH ** -0.5),
        'w_out': nrm(ks[21], (DEPTH, D_MODEL, D_MODEL), D_MODEL ** -0.5),
        'ffn_norm_g': gain(ks[22], (DEPTH, D_MODEL)),
        'w_router_group': nrm(ks[23], (DEPTH, D_MODEL, N_GROUPS), D_MODEL ** -0.5),
        'b_router_group': nrm(ks[24], (DEPTH, N_GROUPS), 0.01),
        'w_router_expert': nrm(ks[25], (DEPTH, N_GROUPS, D_MODEL, EXPERTS_PER_GROUP), D_MODEL ** -0.5),
        'b_router_expert': nrm(ks[26], (DEPTH, N_GROUPS, EXPERTS_PER_GROUP), 0.01),
        'w_exp_gate': nrm(ks[27], (DEPTH, N_GROUPS, EXPERTS_PER_GROUP, D_MODEL, EXPERT_FF), D_MODEL ** -0.5),
        'w_exp_up': nrm(ks[28], (DEPTH, N_GROUPS, EXPERTS_PER_GROUP, D_MODEL, EXPERT_FF), D_MODEL ** -0.5),
        'w_exp_down': nrm(ks[29], (DEPTH, N_GROUPS, EXPERTS_PER_GROUP, EXPERT_FF, D_MODEL), EXPERT_FF ** -0.5),
        'ple_norm_g': gain(ks[30], (DEPTH, D_MODEL)),
        'w_ple_gate': nrm(ks[31], (DEPTH, D_MODEL, D_MODEL), D_MODEL ** -0.5),
        'w_ple': nrm(ks[32], (DEPTH, PLE_DIM, D_MODEL), PLE_DIM ** -0.5),
    }

def reference(x, p, attn_norm_g, w_in, b_gate, q_norm_g, k_norm_g, lam_qk, subln_g, w_attn_up,
              ssm_lam_re, ssm_lam_im, ssm_log_step, ssm_b_re, ssm_b_im, ssm_c_re, ssm_c_im, ssm_d,
              w_glu, b_glu, w_ssm_up, w_out, ffn_norm_g, w_router_group, b_router_group,
              w_router_expert, b_router_expert, w_exp_gate, w_exp_up, w_exp_down,
              ple_norm_g, w_ple_gate, w_ple):
    bsz, s, _ = x.shape
    split_points = [ATT_QK_WIDTH, 2 * ATT_QK_WIDTH, 2 * ATT_QK_WIDTH + ATT_V_WIDTH,
                    2 * ATT_QK_WIDTH + ATT_V_WIDTH + SSM_WIDTH]
    for i in range(DEPTH):
        lam_init = lambda_init_for(i)
        h = rms_norm(x, attn_norm_g[i])
        proj = h @ w_in[i]
        q, k, v, u, g = jnp.split(proj, split_points, axis=-1)
        q = rms_norm(q.reshape(bsz, s, ATT_HEADS, 2, ATT_HEAD_DIM), q_norm_g[i])
        k = rms_norm(k.reshape(bsz, s, ATT_HEADS, 2, ATT_HEAD_DIM), k_norm_g[i])
        v = v.reshape(bsz, s, ATT_HEADS, 2 * ATT_HEAD_DIM)
        lq = lam_qk[i].astype(jnp.float32)
        lam = jnp.exp(jnp.sum(lq[0] * lq[1])) - jnp.exp(jnp.sum(lq[2] * lq[3])) + lam_init
        o = diff_attention(q, k, v, lam)
        o = rms_norm(o, subln_g[i]) * (1.0 - lam_init)
        y_att = o.reshape(bsz, s, ATT_V_WIDTH) @ w_attn_up[i]

        y_s = s5_ssm(u, ssm_lam_re[i], ssm_lam_im[i], ssm_log_step[i], ssm_b_re[i], ssm_b_im[i],
                     ssm_c_re[i], ssm_c_im[i], ssm_d[i])
        z = jax.nn.gelu(y_s)
        z = z * jax.nn.sigmoid(z @ w_glu[i] + b_glu[i])
        y_ssm = z @ w_ssm_up[i]

        gates = jax.nn.sigmoid(g + b_gate[i]).reshape(bsz, s, N_BRANCH, D_MODEL)
        mixed = gates[:, :, 0] * y_att + gates[:, :, 1] * y_ssm
        x = x + mixed @ w_out[i]
        x = x + hier_moe(rms_norm(x, ffn_norm_g[i]), w_router_group[i], b_router_group[i],
                         w_router_expert[i], b_router_expert[i], w_exp_gate[i], w_exp_up[i],
                         w_exp_down[i])
        ple_gate = jax.nn.sigmoid(rms_norm(x, ple_norm_g[i]) @ w_ple_gate[i])
        x = x + ple_gate * (p[i] @ w_ple[i])
    return x


_drawn_inputs = setup_inputs


def setup_inputs(seed=0):
    import zlib

    import numpy as np

    out = dict(_drawn_inputs(seed))
    spreads = {}
    factors = {'b_gate': 8.0,
     'q_norm_g': 4.198,
     'k_norm_g': 3.327,
     'subln_g': 2.875,
     'ssm_lam_re': 64.0,
     'ssm_log_step': 33.928,
     'ssm_b_re': 23.728,
     'ssm_b_im': 29.92,
     'ssm_c_re': 46.048,
     'ssm_c_im': 29.168,
     'b_glu': 8.0,
     'ffn_norm_g': 3.384,
     'b_router_group': 5.972,
     'b_router_expert': 4.328,
     'ple_norm_g': 64.0,
     'ssm_lam_im': 8.0}
    for name, (base, spread) in spreads.items():
        noise = np.random.default_rng([zlib.crc32(name.encode()), seed]).standard_normal(out[name].shape)
        drawn = base * np.exp(spread * noise) if base else spread * noise
        out[name] = __import__('jax').numpy.asarray(drawn.astype(out[name].dtype))
    for name, factor in factors.items():
        out[name] = (out[name] * factor).astype(out[name].dtype)
    return out
```

```python
from contextlib import ExitStack
import math

import numpy as np
import concourse.bass as bass
from concourse import mybir

F32 = mybir.dt.float32
F32R = mybir.dt.float32r
I32 = mybir.dt.int32
ALU = mybir.AluOpType
ACT = mybir.ActivationFunctionType
AX = mybir.AxisListType.X

P = 128
S = 256
T = S // P
D = 1024
KC = D // P
HEADS = 8
DH = 64
SSMW = 512
SG = 32
NST = 64
SH = 16
ST = SG * NST // P
HALF = 128
NG = 4
NE = 8
FF = 256
EPS = 1e-6
LAM_INIT = 0.8 - 0.6 * math.exp(-0.3 * 0)
SCALE = DH ** -0.5
NEG = -1e30
GELU_C = 2.0 * math.sqrt(2.0 / math.pi)
ROUND = 1.5 * 2.0 ** 23
PI2_HI = 6.28125
PI2_MID = 0.0019350051879882812
PI2_LO = 2 * math.pi - PI2_HI - PI2_MID

NRAW = 8
NSPL = 4
AHEAD = 3
PIECE = 2048

P_U = 0
P_QKV = 2
P_G = 14
P_GLU = 22
P_PLE = 23
P_UP = 24
P_AT = 26
P_WO = 30
N_PRE = 34
PER_BLOCK = 3 * NE
TILE_AT = {6 + j: j for j in range(ST)}
YT_AT = {k + 3: j for k, j in TILE_AT.items()}
HALF_PIECES = 2 * (P_G - P_QKV)
QN_AT = {4 * i + 5: i for i in range(4)}
QT_AT = {4 * i + 8 + h: (i, h) for i in range(4) for h in range(2)}
G_U, G_Q, G_K, G_V, G_G, G_GLU, G_PLE, G_UP, G_AT, G_WO = 0, 1, 3, 5, 7, 11, 12, 14, 16, 18
C_BG, C_LR, C_LI, C_BGLU, C_D, C_SUB, C_QG, C_KG, C_LS = 0, 16, 32, 48, 52, 56, 57, 58, 64


def moe_order():
    order = [("g", 0, 0), ("g", 0, 1)]
    for e in range(NE):
        if e + 1 < NE:
            order += [("g", e + 1, 0), ("g", e + 1, 1)]
        order.append(("d", e, 0))
    return order


MOE = moe_order()


class Steps:

    def __init__(self, eng, sem):
        self.eng, self.sem, self.n, self.base = eng, sem, 0, 0

    def add(self, ins):
        ins.then_inc(self.sem, 1)
        self.n += 1
        return ins

    def wait(self):
        self.eng.wait_ge(self.sem, self.base + self.n)

    def do(self, ins):
        self.add(ins)
        self.wait()


def build(nc, a, out):
    ctx = ExitStack()
    with ctx:
        def sb(name, shape, dt=F32, stack=None):
            return (stack or ctx).enter_context(nc.sbuf_tensor(name, shape, dt))

        def sem(name):
            return ctx.enter_context(nc.semaphore(name))

        ring = ExitStack()
        raw = sb("raw", [P, NRAW, PIECE], stack=ring)
        ring.close()
        wlo = sb("wlo", [P, NRAW, PIECE], F32R)
        whi = sb("whi", [P, NSPL, PIECE], F32R)
        ah = sb("ah", [P, KC, S], F32R)
        al = sb("al", [P, KC, S], F32R)
        pst = sb("pst", [P, T, 256])
        pth = sb("pth", [P, 2, S], F32R)
        ptl = sb("ptl", [P, 2, S], F32R)
        ident = sb("ident", [P, P])
        ones = sb("ones", [P, P])
        upper = sb("upper", [P, P])
        iota = sb("iota", [P, P])
        mask = sb("mask", [P, 2 * P])
        mk = sb("mk", [P, 4])
        half_c = sb("half_c", [P, 64])
        smt = sb("smt", [80, P])
        lst = sb("lst", [80, 2])
        col = sb("col", [P, 80])
        gains = sb("gains", [P, 3, KC])
        subg = sb("subg", [P, 1])
        lamq = sb("lamq", [1, 4 * DH])
        lamp = sb("lamp", [1, 2 * DH])
        lams = sb("lams", [1, 4])
        lam = sb("lam", [P, 1])
        nrm = sb("nrm", [P, 64])
        wr = sb("wr", [P, KC, 36])
        wrb = sb("wrb", [P, 36])
        ss = sb("ss", [P, 24, 16])
        rt = sb("rt", [P, 2, 160])
        slotc = sb("slotc", [P, T, 8])
        ohc = sb("ohc", [P, T, 8])
        wl8 = sb("wl8", [P, T, NE])
        wc = sb("wc", [P, NE])
        cnt = sb("cnt", [P, 8])
        plan = sb("plan", [P, 2], I32)
        att = sb("att", [P, 32])
        oss = sb("oss", [P, 4])
        osq = sb("osq", [P, 2, P])
        desc = sb("desc", [P, NE])

        ph = ExitStack()
        qT = sb("qT", [P, HEADS, S], stack=ph)
        kT = sb("kT", [P, HEADS, S], stack=ph)
        v = sb("v", [P, T, D], stack=ph)
        y = sb("y", [P, 4, S], stack=ph)
        p1 = ExitStack()
        qsq = sb("qsq", [P, T, 512], stack=p1)
        qn = sb("qn", [P, T, 512], stack=p1)
        ptab = sb("ptab", [P, 2, ST, HALF], stack=p1)
        bT = sb("bT", [P, 2, 4, P], stack=p1)
        cm = sb("cm", [P, 2, ST, 32], stack=p1)
        uT = sb("uT", [P, 4, S], stack=p1)
        tt = sb("tt", [P, 2, 512], stack=p1)
        rr = sb("rr", [P, 2, 512], stack=p1)
        so = sb("so", [P, 2, 512], stack=p1)
        pp2 = sb("pp2", [P, 512], stack=p1)
        ini = sb("ini", [P, 4], stack=p1)
        p1.close()
        p2 = ExitStack()
        zh = sb("zh", [P, 4, S], F32R, stack=p2)
        zl = sb("zl", [P, 4, S], F32R, stack=p2)
        gT = sb("gT", [P, 16, S], stack=p2)
        oh = sb("oh", [P, HEADS, S], F32R, stack=p2)
        ol = sb("ol", [P, HEADS, S], F32R, stack=p2)
        sm = sb("sm", [P, 2, 384], stack=p2)
        ee = sb("ee", [P, 2, 384], stack=p2)
        ww = sb("ww", [P, 384], stack=p2)
        wT = sb("wT", [P, 384], stack=p2)
        on = sb("on", [P, 2, P], stack=p2)
        p2.close()
        ph.close()
        p3 = ExitStack()
        f8 = sb("f8", [P, KC, S], stack=p3)
        pp = sb("pp", [P, T, D], stack=p3)
        x1 = sb("x1", [P, T, D], stack=p3)
        xnh = sb("xnh", [P, T, D], F32R, stack=p3)
        xnl = sb("xnl", [P, T, D], F32R, stack=p3)
        xn2 = sb("xn2", [P, T, D], stack=p3)
        hgh = sb("hgh", [P, KC, P], F32R, stack=p3)
        hgl = sb("hgl", [P, KC, P], F32R, stack=p3)
        yh = sb("yh", [P, D], F32R, stack=p3)
        yl = sb("yl", [P, D], F32R, stack=p3)
        pm = sb("pm", [P, T, P], F32R, stack=p3)
        pT = sb("pT", [P, S], F32R, stack=p3)
        sg = sb("sg", [P, FF], stack=p3)
        a1 = sb("a1", [P, FF], stack=p3)
        ac = sb("ac", [P, 2, FF], stack=p3)
        ach = sb("ach", [P, 2, 2, P], F32R, stack=p3)
        acl = sb("acl", [P, 2, 2, P], F32R, stack=p3)
        p3.close()
        xin, xn = qT[:].rearrange("p a b -> p (a b)").rearrange("p (t d) -> p t d", t=T), \
            kT[:].rearrange("p a b -> p (a b)").rearrange("p (t d) -> p t d", t=T)
        cst = v[:, 0, :].rearrange("p (r k n) -> p r k n", r=2, k=4)
        bm = v[:, 1, :].rearrange("p (r j g h) -> p r j g h", r=2, j=ST, g=2)
        hgf = f8[:, 0:4].rearrange("p a b -> p (a b)").rearrange("p (c s) -> p c s", c=KC)
        bst = qsq[:].rearrange("p t n -> p (t n)").rearrange("p (r j h) -> p r j h", r=4, j=ST)

        def psum(name, shape):
            return ctx.enter_context(nc.psum_tensor(name, shape, F32))
        pj = psum("pj", [P, 2, 1024])
        sc = psum("sc", [P, 2, 512])
        tp = psum("tp", [P, 512])
        ov = psum("ov", [P, 512])

        raw_in = [sem(f"raw_in{i}") for i in range(NRAW)]
        hi_done = sem("hi_done")
        lo_done = sem("lo_done")
        piece_used = sem("piece_used")
        x_in, small_in, vec_in, p_in, xres_in, bc_in, router_in = (
            sem(n) for n in ("x_in", "small_in", "vec_in", "p_in", "xres_in", "bc_in", "router_in"))
        pool_step, act_step, dve_step = sem("pool_step"), sem("act_step"), sem("dve_step")
        moe_step = sem("moe_step")
        consts = sem("consts")
        xsq = sem("xsq")
        xrs = sem("xrs")
        xnd = sem("xnd")
        xt_pe = sem("xt_pe")
        ah_done = sem("ah_done")
        al_done = sem("al_done")
        pj_read = [sem(f"pj_read{i}") for i in range(2)]
        ls_done = sem("ls_done")
        small_pe = sem("small_pe")
        col_done = sem("col_done")
        lam_row, lam_exp, lam_sum, lam_pe, lam_done = (
            sem(n) for n in ("lam_row", "lam_exp", "lam_sum", "lam_pe", "lam_done"))
        dt_done = sem("dt_done")
        th_done = sem("th_done")
        trig = sem("trig")
        bm_done = sem("bm_done")
        b_pe, c_pe = sem("b_pe"), sem("c_pe")
        bT_done, cm_done = sem("bT_done"), sem("cm_done")
        bu_full = sem("bu_full")
        bu_read = sem("bu_read")
        scan_done = sem("scan_done")
        rot_done = sem("rot_done")
        y_pe = sem("y_pe")
        y_read = sem("y_read")
        qsq_done = sem("qsq_done")
        ssq_done = sem("ssq_done")
        qk_rs = sem("qk_rs")
        qt_pe = sem("qt_pe")
        qt_done = sem("qt_done")
        gelu_in, gelu_sig, z_done, z_hi, z_lo = (
            sem(n) for n in ("gelu_in", "gelu_sig", "z_done", "z_hi", "z_lo"))
        s_full = sem("s_full")
        max_done = sem("max_done")
        e_done = sem("e_done")
        w_done = sem("w_done")
        wt_pe, wt_done = sem("wt_pe"), sem("wt_done")
        o_full = sem("o_full")
        o_sq, o_rs, o_done = sem("o_sq"), sem("o_rs"), sem("o_done")
        ot_pe, oh_done, ol_done = sem("ot_pe"), sem("oh_done"), sem("ol_done")
        g_sig = sem("g_sig")
        glu_sig = sem("glu_sig")
        pt_pe, pth_done, ptl_done = sem("pt_pe"), sem("pth_done"), sem("ptl_done")
        mix_done = sem("mix_done")
        xnh_done, xnl_done = sem("xnh_done"), sem("xnl_done")
        wr_done = sem("wr_done")
        lg_pe, lg_in, lg_exp = sem("lg_pe"), sem("lg_in"), sem("lg_exp")
        grp_done, rank_pe, plan_done = sem("grp_done"), sem("rank_pe"), sem("plan_done")
        m_pm = sem("m_pm")
        m_gat = sem("m_gat")
        m_hgf = sem("m_hgf")
        m_hgh, m_hgl = sem("m_hgh"), sem("m_hgl")
        m_ptp = sem("m_ptp")
        m_pt, m_wc = sem("m_pt"), sem("m_wc")
        m_sig, m_act = sem("m_sig"), sem("m_act")
        m_tp, m_ach, m_acl = sem("m_tp"), sem("m_ach"), sem("m_acl")
        m_yh, m_yl = sem("m_yh"), sem("m_yl")
        m_sc, m_add = sem("m_sc"), sem("m_add")
        wl_done = sem("wl_done")
        xt3, pl_sig = sem("xt3"), sem("pl_sig")
        o_ready, o_out = sem("o_ready"), sem("o_out")

        last_piece = {G_U: P_U + 1, G_GLU: P_GLU, G_PLE: P_PLE, G_PLE + 1: P_PLE, G_UP: P_UP, G_UP + 1: P_UP + 1}
        last_piece.update({G_Q + i: P_QKV + 2 * i + 1 for i in range(6)})
        last_piece.update({G_G + i: P_G + 2 * i + 1 for i in range(4)})
        last_piece.update({G_AT + i: P_AT + 2 * i + 1 for i in range(2)})
        last_piece.update({G_WO + i: P_WO + 2 * i + 1 for i in range(2)})

        def full(eng, G):
            eng.wait_ge(piece_used, last_piece[G] + 1)

        def read_count(G):
            return G // 2 + 2

        w_in = a["w_in"][0].rearrange("(p h c) n -> h p c n", h=2, c=4)

        def cols(w, c0):
            return [w[h, :, :, c0:c0 + 512] for h in range(2)]
        glu_w = a["w_glu"][0].rearrange("(c p) n -> p c n", p=P)
        up_w = a["w_ssm_up"][0].rearrange("(c p) n -> p c n", p=P)
        at_w = a["w_attn_up"][0].rearrange("(h c p) n -> h p c n", h=2, p=P)
        wo_w = a["w_out"][0].rearrange("(h c p) n -> h p c n", h=2, p=P)
        pg_w = a["w_ple_gate"][0].rearrange("(p h c) n -> h p c n", h=2, c=4)
        pl_w = a["w_ple"][0].rearrange("(p c) n -> p c n", c=2)
        pre = cols(w_in, 3072)
        for c0 in (0, 512, 1024, 1536, 2048, 2560):
            pre += cols(w_in, c0)
        for g in range(4):
            pre += cols(w_in, 3584 + 512 * g)
        pre += [glu_w, pl_w, up_w[:, :, 0:512], up_w[:, :, 512:1024]]
        pre += cols(at_w, 0) + cols(at_w, 512) + cols(wo_w, 0) + cols(wo_w, 512)
        assert len(pre) == N_PRE
        ple = cols(pg_w, 0) + cols(pg_w, 512)
        wg_e = a["w_exp_gate"][0].rearrange("n e (p h c) f -> (n e) h p (c f)", h=2, c=4)
        wu_e = a["w_exp_up"][0].rearrange("n e (p h c) f -> (n e) h p (c f)", h=2, c=4)
        wd_e = a["w_exp_down"][0].rearrange("n e (p c) d -> (n e) p (c d)", c=2)
        xd = a["x"][0].rearrange("(t p) d -> p t d", p=P)
        outd = out[0].rearrange("(t p) d -> p t d", p=P)

        block = ctx.enter_context(nc.Block())

        @block.sync
        def _(sp):
            def load(i, halves, b=0):
                if i >= NRAW:
                    sp.wait_ge(piece_used, b * PER_BLOCK + (i - NRAW + 1))
                for dst, src in halves(raw[:, i % NRAW, :]):
                    sp.dma_start(dst, src).then_inc(raw_in[i % NRAW], 16)

            def plain(src):
                k = src.shape[1]

                def halves(slot):
                    d = slot.rearrange("p (c n) -> p c n", c=k)
                    return [(d[:, 0:k // 2], src[:, 0:k // 2]), (d[:, k // 2:], src[:, k // 2:])]
                return halves
            for t in range(T):
                sp.dma_start(xin[:, t], xd[:, t]).then_inc(x_in, 16)
            for n in range(N_PRE):
                load(n, plain(pre[n]))
                if n == 2:
                    sp.dma_start(pst[:], a["p"][0, 0].rearrange("(t p) d -> p t d", p=P)).then_inc(p_in, 16)
            sp.wait_ge(o_full, HEADS)
            sp.dma_start(x1[:], xd).then_inc(xres_in, 16)

            def block_loads(b, group):
                for i, (kind, e, h) in enumerate(MOE):
                    ex = group * NE + e

                    def halves(slot):
                        d = slot.rearrange("p (w n) -> p w n", w=2)
                        if kind == "g":
                            return [(d[:, w], m[bass.ds(ex, 1), h].rearrange("a p n -> (a p) n"))
                                    for w, m in enumerate((wg_e, wu_e))]
                        s = wd_e[bass.ds(ex, 1)].rearrange("a p (w n) -> (a p) w n", w=2)
                        return [(d[:, w], s[:, w]) for w in range(2)]
                    load(N_PRE + i, halves, b)
            with sp.Fori(0, NG) as b:
                block_loads(b, b)
            sp.wait_ge(plan_done, 1)
            nb = sp.value_load(plan[0:1, 0:1], min_val=NG, max_val=NG + 1)
            gx = sp.value_load(plan[0:1, 1:2], min_val=0, max_val=NG - 1)
            with sp.If(nb > NG):
                block_loads(NG, gx)
            for j in range(4):
                load(N_PRE + j, plain(ple[j]), nb)
            for i in range(2):
                sp.wait_ge(o_ready, i + 1)
                sp.dma_start(outd[:, :, 512 * i:512 * i + 512], x1[:, :, 512 * i:512 * i + 512]).then_inc(o_out, 16)
            sp.wait_ge(o_out, 32)

        @block.gpsimd
        def _(pool):
            g = nc.gpsimd
            st = Steps(pool, pool_step)
            for buf, val in ((ones, 1.0), (half_c, -0.5), (mask, 0.0), (mk, -1.0), (slotc, -1.0), (ohc, 0.0)):
                st.add(g.memset(buf[:], val))
            st.wait()
            g.affine_select(out=ident[:], in_=ones[:], compare_op=ALU.is_equal, fill=0.0, base=0,
                            pattern=[[-1, P]], channel_multiplier=1).then_inc(consts, 1)
            g.affine_select(out=upper[:], in_=ones[:], compare_op=ALU.is_gt, fill=0.0, base=0,
                            pattern=[[1, P]], channel_multiplier=-1).then_inc(consts, 1)
            g.affine_select(out=mask[:, P:], in_=mask[:, P:], compare_op=ALU.is_ge, fill=NEG, base=0,
                            pattern=[[-1, P]], channel_multiplier=1).then_inc(consts, 1)
            g.iota(iota[:], pattern=[[1, P]], base=0, channel_multiplier=0,
                   allow_small_or_imprecise_dtypes=True).then_inc(consts, 1)
            for i, src in enumerate((ones[:, 0:1], ones[:, 0:1], mk[:, 2:3], mk[:, 3:4])):
                sign, cmp = ((-1, ALU.is_gt), (1, ALU.is_ge))[i % 2]
                g.affine_select(out=mk[:, i:i + 1], in_=src, compare_op=cmp, fill=0.0, base=-64 * sign,
                                pattern=[[0, 1]], channel_multiplier=sign).then_inc(consts, 1)
            def rload(dst, src):
                pool.dma_start(dst, src).then_inc(router_in, 16)
            rload(wr[:, :, 0:NG], a["w_router_group"][0].rearrange("(p c) n -> p c n", c=KC))
            for n in range(NG):
                rload(wr[:, :, NG + NE * n:NG + NE * n + NE],
                      a["w_router_expert"][0, n].rearrange("(p c) e -> p c e", c=KC))
            rload(wrb[:, 0:NG], a["b_router_group"][0].partition_broadcast(P))
            rload(wrb[:, NG:36], a["b_router_expert"][0].rearrange("n e -> (n e)").partition_broadcast(P))

            def inv_root(ap, width, dim, done):
                st.do(g.tensor_scalar(ap, ap, 1.0 / dim, EPS, ALU.mult, ALU.add))
                g.tensor_tensor(ap, ap, half_c[:, 0:width], ALU.pow).then_inc(done, 1)
            pool.wait_ge(xsq, 1)
            inv_root(nrm[:, 0:2], 2, D, xrs)

            def rotate_back(j):
                b = j % 2
                pool.wait_ge(scan_done, j + 1)
                if j >= 2:
                    pool.wait_ge(y_pe, j - 1)
                c, s = (ptab[:, i, j, :].unsqueeze(1).to_broadcast([P, 4, HALF]) for i in range(2))
                r4 = rr[:, b, :].rearrange("p (a t) -> p a t", a=4)
                st.add(g.tensor_tensor(so[:, b, :].rearrange("p (a t) -> p a t", a=4), r4, c, ALU.mult))
                st.do(g.tensor_tensor(pp2[:].rearrange("p (a t) -> p a t", a=4), r4, s, ALU.mult))
                g.tensor_tensor(so[:, b, 0:256], so[:, b, 0:256], pp2[:, 256:512], ALU.subtract)
                g.tensor_tensor(so[:, b, 256:512], so[:, b, 256:512], pp2[:, 0:256], ALU.add).then_inc(rot_done, 1)
                pool.wait_ge(rot_done, j + 1)

            for k in range(HALF_PIECES):
                if k in QN_AT:
                    pool.wait_ge(ssq_done, QN_AT[k] + 1)
                    inv_root(nrm[:, 16:32], 16, DH, qk_rs)
                if k in TILE_AT:
                    rotate_back(TILE_AT[k])
            for h in range(HEADS):
                pool.wait_ge(o_sq, h + 1)
                inv_root(oss[:, 0:2], 2, P, o_rs)
            for i in (1, 2):
                pool.wait_ge(xsq, i + 1)
                inv_root(nrm[:, 2 * i:2 * i + 2], 2, D, xrs)
                if i == 1:
                    zeros = mask[:, 0:P]
                    for buf, done in ((yh, m_yh), (yl, m_yl)):
                        g.tensor_copy(buf[:].rearrange("p (c n) -> p c n", c=KC),
                                      zeros.unsqueeze(1).to_broadcast([P, KC, P])).then_inc(done, 1)
                    g.tensor_copy(pT[:].rearrange("p (t n) -> p t n", t=T),
                                  zeros.unsqueeze(1).to_broadcast([P, T, P])).then_inc(m_pt, 1)

        @block.scalar
        def _(act):
            e = nc.scalar
            st = Steps(act, act_step)

            def split_hi(i, b=0):
                act.wait_ge(raw_in[i % NRAW], b * (32 * PER_BLOCK // NRAW) + 32 * (i // NRAW + 1))
                if i >= NSPL:
                    act.wait_ge(piece_used, b * PER_BLOCK + (i - NSPL + 1))
                e.activation(whi[:, i % NSPL, :], raw[:, i % NRAW, :], ACT.Copy).then_inc(hi_done, 1)

            bg = a["b_gate"][0].rearrange("(r n) -> r n", n=P)
            for r0, src in ((C_BG, bg),
                            (C_LR, a["ssm_lam_re"][0].rearrange("(j g) s -> j (g s)", g=2)),
                            (C_LI, a["ssm_lam_im"][0].rearrange("(j g) s -> j (g s)", g=2)),
                            (C_BGLU, a["b_glu"][0].rearrange("(r n) -> r n", n=P)),
                            (C_D, a["ssm_d"][0].rearrange("(r g) h -> r (g h)", g=8)),
                            (C_SUB, a["subln_g"]),
                            (C_QG, a["q_norm_g"].rearrange("o m d -> o (m d)")),
                            (C_KG, a["k_norm_g"].rearrange("o m d -> o (m d)")),
                            (C_KG + 1, bg[0:C_LS - C_KG - 1])):
                act.dma_start(smt[r0:r0 + src.shape[0], :], src).then_inc(small_in, 16)
            act.dma_start(lst[64:80, :], a["ssm_log_step"][0].rearrange("(j g) -> j g", g=2)).then_inc(small_in, 16)
            for i, nm in enumerate(("attn_norm_g", "ffn_norm_g", "ple_norm_g")):
                act.dma_start(gains[:, i, :], a[nm][0].rearrange("(p c) -> p c", c=KC)).then_inc(vec_in, 16)
            act.dma_start(lamq[:], a["lam_qk"].rearrange("o m d -> o (m d)")).then_inc(vec_in, 16)
            for i, nm in enumerate(("ssm_b_re", "ssm_b_im")):
                act.dma_start(bst[:, i], a[nm][0].rearrange("(j g) s h -> (g s) j h", g=2)).then_inc(bc_in, 16)
            for i, nm in enumerate(("ssm_c_re", "ssm_c_im")):
                for d in range(2):
                    act.dma_start(cst[:, i, :, NST * d:NST * d + NST],
                                  a[nm][0].rearrange("(k g) h s -> (g h) k s", g=8)).then_inc(bc_in, 16)

            def square_sums(dst, src, k, done):
                for t in range(T):
                    ins = e.activation(dst[:, t], src[:, t], ACT.Square, accum_out=nrm[:, k + t:k + t + 1])
                ins.then_inc(done, 1)
            act.wait_ge(x_in, 32)
            square_sums(xn, xin, 0, xsq)
            split_hi(0)
            act.wait_ge(small_pe, 1)
            e.activation(col[:], ov[:, 0:80], ACT.Copy).then_inc(col_done, 1)
            act.wait_ge(col_done, 1)
            e.activation(subg[:], col[:, C_SUB:C_SUB + 1], ACT.Copy, scale=1.0 - LAM_INIT)
            e.activation(ss[:, 0, :], col[:, C_LS:C_LS + 16], ACT.Exp).then_inc(dt_done, 1)
            act.wait_ge(lam_row, 1)
            e.activation(lams[0:1, 2:4], lams[0:1, 0:2], ACT.Exp).then_inc(lam_exp, 1)
            act.wait_ge(vec_in, 64)

            def chunks_hi(bank_full, gain):
                for k in range(4):
                    bank_full(k)
                    for c in (2 * k, 2 * k + 1):
                        e.activation(ah[:, c, :], pj[:, k // 2, (c % 4) * S:(c % 4) * S + S], ACT.Copy,
                                     scale=gains[:, gain, c:c + 1]).then_inc(ah_done, 1)
            chunks_hi(lambda k: act.wait_ge(xt_pe, k + 1), 0)
            split_hi(1)
            act.wait_ge(th_done, 1)
            e.activation(ss[:, 3, :], ss[:, 1, :], ACT.Exp)
            e.activation(ss[:, 5, :], ss[:, 4, :], ACT.Sin)
            e.activation(ss[:, 7, :], ss[:, 6, :], ACT.Sin).then_inc(trig, 1)
            act.wait_ge(pt_pe, 1)
            e.activation(pth[:], tp[:].rearrange("p (c s) -> p c s", c=2), ACT.Copy).then_inc(pth_done, 1)

            def u_evac():
                full(act, G_U)
                e.activation(uT[:].rearrange("p k s -> p (k s)"), pj[:, G_U % 2, :], ACT.Copy)\
                    .then_inc(pj_read[G_U % 2], 1)

            def qk_squares(i):
                full(act, G_Q + i)
                if i:
                    act.wait_ge(ssq_done, i)
                else:
                    act.wait_ge(bm_done, 1)
                e.activation(qsq[:].rearrange("p t n -> p (t n)"), pj[:, (G_Q + i) % 2, :], ACT.Square)\
                    .then_inc(qsq_done, 1)

            def qk_norm(i):
                act.wait_ge(qk_rs, i + 1)
                if i:
                    act.wait_ge(qt_pe, 2 * i)
                src, dst = pj[:, (G_Q + i) % 2, :], qn[:].rearrange("p t n -> p (t n)")
                for q in range(16):
                    ins = e.activation(dst[:, DH * q:DH * q + DH], src[:, DH * q:DH * q + DH], ACT.Copy,
                                       scale=nrm[:, 16 + q:17 + q])
                ins.then_inc(pj_read[(G_Q + i) % 2], 1)

            def qt_evac(i, half):
                act.wait_ge(qt_pe, 2 * i + half + 1)
                h0 = 4 * (i % 2) + 2 * half
                gc = C_QG if i < 2 else C_KG
                e.activation((qT if i < 2 else kT)[:, h0:h0 + 2, :].rearrange("p h s -> p (h s)"), tp[:], ACT.Copy,
                             scale=col[:, gc:gc + 1]).then_inc(qt_done, 1)

            def v_evac(i):
                G = G_V + i
                full(act, G)
                e.activation(v[:, :, 512 * i:512 * i + 512], pj[:, G % 2, :].rearrange("p (t n) -> p t n", t=2),
                             ACT.Copy).then_inc(pj_read[G % 2], 1)

            def g_evac(i):
                G = G_G + i
                full(act, G)
                for b in range(4):
                    ins = e.activation(gT[:, 4 * i + b, :], pj[:, G % 2, b * S:b * S + S], ACT.Identity,
                                       bias=col[:, C_BG + 4 * i + b:C_BG + 4 * i + b + 1])
                ins.then_inc(pj_read[G % 2], 1)

            split_hi(2)
            split_hi(3)
            u_evac()
            split_hi(4)
            for n in range(P_QKV, P_G):
                split_hi(n + AHEAD)
                if n == P_QKV + 1:
                    act.wait_ge(b_pe, 1)
                    for r in range(2):
                        e.activation(bT[:, r], sc[:, r, :].rearrange("p (k n) -> p k n", k=4), ACT.Copy)\
                            .then_inc(bT_done, 1)
                i = (n - P_QKV) // 2
                if n % 2 == 1:
                    if 1 <= i <= 4:
                        qk_norm(i - 1)
                    qk_squares(i) if i < 4 else v_evac(i - 4)
                for k in (2 * (n - P_QKV), 2 * (n - P_QKV) + 1):
                    if k in QT_AT:
                        qt_evac(*QT_AT[k])

            for j in range(HEADS + 3):
                split_hi(P_G + j + AHEAD)
                if j >= 3:
                    act.wait_ge(ot_pe, j - 2)
                    e.activation(oh[:, j - 3, :], tp[:, 0:S], ACT.Copy, scale=subg[:, 0:1]).then_inc(oh_done, 1)
                if 1 <= j <= HEADS:
                    act.wait_ge(wt_pe, j)
                    e.activation(wT[:], tp[:, 0:384], ACT.Copy).then_inc(wt_done, 1)
                if j < HEADS:
                    act.wait_ge(max_done, j + 1)
                    for m in range(2):
                        for qb, (k0, k1) in enumerate(((0, P), (P, 3 * P))):
                            i = 2 * m + qb
                            ins = e.activation(ee[:, m, k0:k1], sm[:, m, k0:k1], ACT.Exp, scale=SCALE,
                                               bias=att[:, 4 + i:5 + i], accum_out=att[:, 8 + i:9 + i])
                    ins.then_inc(e_done, 1)
                if j < HEADS and j % 2 == 1:
                    g_evac(j // 2)
                if j == 1:
                    act.wait_ge(gelu_in, 1)
                    e.activation(tt[:], tt[:], ACT.Sigmoid, scale=GELU_C).then_inc(gelu_sig, 1)
                if j == 2:
                    act.wait_ge(z_done, 1)
                    e.activation(zh[:], y[:], ACT.Copy).then_inc(z_hi, 1)
                if 1 <= j <= HEADS:
                    act.wait_ge(o_full, j)
                    if j >= 2:
                        act.wait_ge(o_done, j - 1)
                    for qb in range(2):
                        ins = e.activation(osq[:, qb], ov[:, qb * P:qb * P + P], ACT.Square, accum_out=oss[:, qb:qb + 1])
                    ins.then_inc(o_sq, 1)
                if j == HEADS:
                    e.activation(gT[:, 8:16], gT[:, 8:16], ACT.Sigmoid).then_inc(g_sig, 1)
                    full(act, G_GLU)
                    for b in range(4):
                        ins = e.activation(f8[:, b, :], pj[:, G_GLU % 2, b * S:b * S + S], ACT.Sigmoid,
                                           bias=col[:, C_BGLU + b:C_BGLU + b + 1])
                    ins.then_inc(pj_read[G_GLU % 2], 1)
                    e.activation(gT[:, 0:8], gT[:, 0:8], ACT.Sigmoid).then_inc(g_sig, 1)
                    act.wait_ge(z_done, 2)
                    e.activation(zh[:], y[:], ACT.Copy).then_inc(z_hi, 1)
                if j == HEADS + 1:
                    for i in range(2):
                        full(act, G_PLE + i)
                        e.activation(pp[:, i, :], pj[:, (G_PLE + i) % 2, :], ACT.Copy)\
                            .then_inc(pj_read[(G_PLE + i) % 2], 1)
            for n in range(P_UP + 1, N_PRE):
                split_hi(n + AHEAD)
                if n in (P_AT + 2, P_WO):
                    i = 0 if n < P_WO else 1
                    act.wait_ge(mix_done, i + 1)
                    e.activation(ah[:, 4 * i:4 * i + 4, :], gT[:, 4 * i:4 * i + 4, :], ACT.Copy).then_inc(ah_done, 1)

            act.wait_ge(pj_read[0], read_count(G_WO))
            act.wait_ge(pj_read[1], read_count(G_WO + 1))
            square_sums(xn2, x1, 2, xsq)
            act.wait_ge(xnd, 2)
            e.activation(xnh[:], xn2[:], ACT.Copy).then_inc(xnh_done, 1)
            for k in range(2):
                act.wait_ge(xt_pe, 4 + 2 * (k + 1))
                e.activation(f8[:, 4 * k:4 * k + 4].rearrange("p c s -> p (c s)"), pj[:, k, :], ACT.Copy)\
                    .then_inc(pj_read[k], 1)
            act.wait_ge(lg_in, 1)
            e.activation(rt[:, :, 48:52], rt[:, :, 44:48], ACT.Exp).then_inc(lg_exp, 1)
            act.wait_ge(lg_in, 2)
            e.activation(rt[:, :, 90:91], rt[:, :, 89:90], ACT.Exp).then_inc(lg_exp, 1)

            def tokens_hi():
                e.activation(hgh[:], hgf, ACT.Copy).then_inc(m_hgh, 1)
            act.wait_ge(m_hgf, 1)
            tokens_hi()
            act.wait_ge(plan_done, 1)
            nb = act.value_load(plan[0:1, 0:1], min_val=NG, max_val=NG + 1)
            with act.Fori(0, nb) as b:
                def act_hi(x):
                    act.wait_ge(m_tp, b * NE + (x + 1))
                    e.activation(ach[:, x % 2], tp[:, 0:FF].rearrange("p (r n) -> p r n", r=2), ACT.Copy).then_inc(m_ach, 1)
                for i, (kind, x, h) in enumerate(MOE):
                    if kind == "g" and h == 1 and x >= 1:
                        act_hi(x - 1)
                    split_hi(N_PRE + i + AHEAD, b)
                    if i == 4:
                        act.wait_ge(m_ptp, b + 1)
                        act.wait_ge(m_sc, (b + 1) * T)
                        e.activation(pT[:], ov[:, 0:S], ACT.Copy).then_inc(m_pt, 1)
                    if kind == "g" and h == 1:
                        act.wait_ge(piece_used, b * PER_BLOCK + (N_PRE + i + 1))
                        e.activation(sg[:], pj[:, 0, 512 * (x % 2):512 * (x % 2) + FF], ACT.Sigmoid)\
                            .then_inc(m_sig, 1)
                    if kind == "d" and x == NE - 2:
                        act_hi(NE - 1)
                        act.wait_ge(m_hgf, b + 2)
                        tokens_hi()
                act.wait_ge(piece_used, b * PER_BLOCK + (N_PRE + PER_BLOCK))
                e.activation(yh[:], sc[:].rearrange("p a n -> p (a n)"), ACT.Copy).then_inc(m_yh, 1)

            act.wait_ge(m_add, (nb + 1) * T)
            square_sums(xn2, x1, 4, xsq)
            chunks_hi(lambda k: act.wait_ge(xt3, k + 1), 2)
            split_hi(N_PRE + 3, nb)
            for i in range(2):
                act.wait_ge(piece_used, nb * PER_BLOCK + (N_PRE + 2 * i + 2))
                e.activation(f8[:, 4 * i:4 * i + 4].rearrange("p c s -> p (c s)"), pj[:, i, :], ACT.Sigmoid)\
                    .then_inc(pl_sig, 1)

        @block.vector
        def _(dve):
            w = nc.vector
            st = Steps(dve, dve_step)

            def split_lo(i, b=0):
                dve.wait_ge(hi_done, b * PER_BLOCK + (i + 1))
                w.tensor_tensor(wlo[:, i % NRAW, :], raw[:, i % NRAW, :], whi[:, i % NSPL, :].bitcast(F32),
                                ALU.subtract).then_inc(lo_done, 1)
            dve.wait_ge(small_in, 160)
            w.tensor_copy(smt[64:80, :].rearrange("p (g s) -> p g s", g=2),
                          lst[64:80, :].unsqueeze(2).to_broadcast([16, 2, NST])).then_inc(ls_done, 1)
            dve.wait_ge(vec_in, 64)
            lq = lamq[:].rearrange("o (a b d) -> o a b d", a=2, b=2)
            lp = lamp[:].rearrange("o (a d) -> o a d", a=2)
            st.do(w.tensor_tensor(lp, lq[:, :, 0], lq[:, :, 1], ALU.mult))
            w.reduce_sum(lams[0:1, 0:2], lp, AX).then_inc(lam_row, 1)

            def normalise(dst, src, k, i):
                dve.wait_ge(xrs, i)
                for t in range(T):
                    ins = w.tensor_scalar(dst[:, t], src[:, t], nrm[:, k + t:k + t + 1], None, ALU.mult)
                ins.then_inc(xnd, 1)
            normalise(xn, xin, 0, 1)
            split_lo(0)
            dve.wait_ge(lam_exp, 1)
            st.do(w.tensor_tensor(lams[0:1, 0:1], lams[0:1, 2:3], lams[0:1, 3:4], ALU.subtract))
            w.tensor_scalar(lams[0:1, 0:1], lams[0:1, 0:1], LAM_INIT, None, ALU.add).then_inc(lam_sum, 1)

            def chunks_lo(base, gain):
                for k in range(4):
                    dve.wait_ge(ah_done, base + 2 * k + 2)
                    for c in (2 * k, 2 * k + 1):
                        ins = w.scalar_tensor_tensor(
                            out=al[:, c, :], in0=pj[:, k // 2, (c % 4) * S:(c % 4) * S + S],
                            scalar=gains[:, gain, c:c + 1], in1=ah[:, c, :].bitcast(F32),
                            op0=ALU.mult, op1=ALU.subtract)
                    if k % 2:
                        ins.then_inc(pj_read[k // 2], 1)
            chunks_lo(0, 0)
            split_lo(1)

            def V(i):
                return ss[:, i, :]

            def tt_(o, x, z, op):
                return w.tensor_tensor(o, x, z, op)
            dve.wait_ge(dt_done, 1)
            lr, li = col[:, C_LR:C_LR + 16], col[:, C_LI:C_LI + 16]
            st.add(tt_(V(1), lr, V(0), ALU.mult))
            st.do(tt_(V(2), li, V(0), ALU.mult))
            st.do(w.tensor_scalar(V(8), V(2), 1.0 / (2 * math.pi), None, ALU.mult))
            st.do(w.tensor_scalar(V(8), V(8), ROUND, None, ALU.add))
            st.do(w.tensor_scalar(V(8), V(8), -ROUND, None, ALU.add))
            for part in (PI2_HI, PI2_MID, PI2_LO):
                st.do(w.scalar_tensor_tensor(out=V(2), in0=V(8), scalar=-part, in1=V(2), op0=ALU.mult, op1=ALU.add))
            st.do(w.tensor_scalar(V(4), V(2), 3.1415925, -3.1415925, ALU.min, ALU.max))
            st.do(w.tensor_scalar(V(6), V(4), -1.0, None, ALU.mult))
            st.do(tt_(V(6), V(6), V(4), ALU.max))
            w.tensor_scalar(V(6), V(6), -1.0, math.pi / 2, ALU.mult, ALU.add).then_inc(th_done, 1)
            st.add(tt_(V(8), lr, lr, ALU.mult))
            st.do(tt_(V(9), li, li, ALU.mult))
            st.do(tt_(V(8), V(8), V(9), ALU.add))
            st.do(w.reciprocal(V(8), V(8)))
            dve.wait_ge(trig, 1)
            st.add(tt_(V(10), V(3), V(7), ALU.mult))
            st.do(tt_(V(11), V(3), V(5), ALU.mult))
            st.do(w.tensor_scalar(V(10), V(10), -1.0, None, ALU.add))
            st.add(tt_(V(12), V(10), lr, ALU.mult))
            st.add(tt_(V(13), V(11), li, ALU.mult))
            st.add(tt_(V(14), V(11), lr, ALU.mult))
            st.do(tt_(V(15), V(10), li, ALU.mult))
            st.add(tt_(V(12), V(12), V(13), ALU.add))
            st.do(tt_(V(14), V(14), V(15), ALU.subtract))
            st.add(tt_(V(12), V(12), V(8), ALU.mult))
            st.do(tt_(V(14), V(14), V(8), ALU.mult))

            dve.wait_ge(bc_in, 96)
            dve.wait_ge(consts, 8)

            def spread(col_):
                return col_.unsqueeze(2).to_broadcast([P, ST, SH])
            st.add(tt_(bst[:, 2], bst[:, 0], spread(V(12)), ALU.mult))
            st.add(tt_(bm[:, 0, :, 0, :], bst[:, 1], spread(V(14)), ALU.mult))
            st.add(tt_(bst[:, 3], bst[:, 1], spread(V(12)), ALU.mult))
            st.do(tt_(bm[:, 0, :, 1, :], bst[:, 0], spread(V(14)), ALU.mult))
            st.add(tt_(bst[:, 2], bst[:, 2], bm[:, 0, :, 0, :], ALU.subtract))
            st.do(tt_(bst[:, 3], bst[:, 3], bm[:, 0, :, 1, :], ALU.add))
            for r in range(2):
                for gl in range(2):
                    ins = w.tensor_scalar(bm[:, r, :, gl, :], bst[:, 2 + r], mk[:, gl:gl + 1], None, ALU.mult)
            ins.then_inc(bm_done, 1)
            dve.wait_ge(pth_done, 1)
            tt_(ptl[:], tp[:].rearrange("p (c s) -> p c s", c=2), pth[:].bitcast(F32), ALU.subtract)\
                .then_inc(ptl_done, 1)
            split_lo(2)

            st.add(w.memset(ptab[:, 0, :, 0:1], 1.0))
            st.add(w.memset(ptab[:, 1, :, 0:1], 0.0))
            st.add(w.tensor_copy(V(16), V(7)))
            st.do(w.tensor_copy(V(17), V(5)))
            sc1 = tt[:].rearrange("p a n -> p (a n)")
            sc2 = rr[:].rearrange("p a n -> p (a n)")
            L = 1
            while L < HALF:
                c_, s_ = (V(i).unsqueeze(2).to_broadcast([P, ST, L]) for i in (16, 17))
                old = [ptab[:, r, :, 0:L] for r in range(2)]
                new = [ptab[:, r, :, L:2 * L] for r in range(2)]
                t1, t2 = (s[:, 0:ST * L].rearrange("p (j l) -> p j l", j=ST) for s in (sc1, sc2))
                st.add(tt_(new[0], old[0], c_, ALU.mult))
                st.add(tt_(t1, old[1], s_, ALU.mult))
                st.add(tt_(new[1], old[0], s_, ALU.mult))
                st.do(tt_(t2, old[1], c_, ALU.mult))
                st.add(tt_(new[0], new[0], t1, ALU.subtract))
                st.add(tt_(new[1], new[1], t2, ALU.add))
                st.add(tt_(V(18), V(16), V(16), ALU.mult))
                st.add(tt_(V(19), V(17), V(17), ALU.mult))
                st.do(tt_(V(20), V(16), V(17), ALU.mult))
                st.add(tt_(V(16), V(18), V(19), ALU.subtract))
                st.do(w.tensor_scalar(V(17), V(20), 2.0, None, ALU.mult))
                if L in (2, 8, 16, 32, 64):
                    split_lo({2: 3, 8: 4, 16: 5, 32: 6, 64: 7}[L])
                L *= 2

            dve.wait_ge(c_pe, 1)
            for r, bank in enumerate((ov, tp)):
                src = bank[:].rearrange("p (j g h) -> p j g h", j=ST, g=2)
                dst = cm[:, r].rearrange("p j (g h) -> p j g h", g=2)
                for gl in range(2):
                    ins = w.tensor_scalar(dst[:, :, gl, :], src[:, :, gl, :], mk[:, 2 * r + gl:2 * r + gl + 1],
                                          None, ALU.mult)
            ins.then_inc(cm_done, 1)
            dve.wait_ge(lam_pe, 1)
            w.tensor_copy(lam[:], sc[:, 1, 0:1]).then_inc(lam_done, 1)

            def scan_tile(j):
                b = j % 2
                dve.wait_ge(bu_full, j + 1)
                if j >= 2:
                    dve.wait_ge(rot_done, j - 1)
                c, s = (ptab[:, i, j, :].unsqueeze(1).to_broadcast([P, 4, HALF]) for i in range(2))
                bank = sc[:, b, :].rearrange("p (a t) -> p a t", a=4)
                t1, t2 = tt[:, 0, :], tt[:, 1, :]
                w.tensor_tensor(t1.rearrange("p (a t) -> p a t", a=4), bank, c, ALU.mult)
                w.tensor_tensor(t2.rearrange("p (a t) -> p a t", a=4), bank, s, ALU.mult).then_inc(bu_read, 1)
                dve.wait_ge(bu_read, j + 1)
                st.add(tt_(t1[:, 0:256], t1[:, 0:256], t2[:, 256:512], ALU.add))
                st.do(tt_(t1[:, 256:512], t1[:, 256:512], t2[:, 0:256], ALU.subtract))
                mag = ss[:, 3, j:j + 1].to_broadcast([P, HALF])
                r = rr[:, b, :]
                for k in (0, 256):
                    ins = st.add(w.tensor_tensor_scan(r[:, k:k + HALF], mag, t1[:, k:k + HALF], 0.0, ALU.mult, ALU.add))
                st.wait()
                c1, s1 = V(16)[:, j:j + 1], V(17)[:, j:j + 1]
                re, im = r[:, HALF - 1:HALF], r[:, 256 + HALF - 1:256 + HALF]
                st.add(tt_(ini[:, 0:1], im, s1, ALU.mult))
                st.do(tt_(ini[:, 1:2], re, s1, ALU.mult))
                st.add(w.scalar_tensor_tensor(out=ini[:, 2:3], in0=re, scalar=c1, in1=ini[:, 0:1],
                                              op0=ALU.mult, op1=ALU.subtract))
                st.do(w.scalar_tensor_tensor(out=ini[:, 3:4], in0=im, scalar=c1, in1=ini[:, 1:2],
                                             op0=ALU.mult, op1=ALU.add))
                for n, k in enumerate((0, 256)):
                    ins = w.tensor_tensor_scan(r[:, k + HALF:k + 2 * HALF], mag, t1[:, k + HALF:k + 2 * HALF],
                                               ini[:, 2 + n:3 + n], ALU.mult, ALU.add)
                ins.then_inc(scan_done, 1)
                dve.wait_ge(scan_done, j + 1)

            def y_evac(c):
                dve.wait_ge(y_pe, 4 * c + 4)
                dve.wait_ge(pj_read[G_U % 2], read_count(G_U))
                w.scalar_tensor_tensor(out=y[:, c, :], in0=uT[:, c, :], scalar=col[:, C_D + c:C_D + c + 1],
                                       in1=ov[:, 0:S], op0=ALU.mult, op1=ALU.add).then_inc(y_read, 1)

            for k in range(4, max(YT_AT) + 1):
                if k % 4 == 0 and 1 <= k // 4 <= 4:
                    i = k // 4 - 1
                    dve.wait_ge(qsq_done, i + 1)
                    if i:
                        dve.wait_ge(pj_read[(G_Q + i - 1) % 2], read_count(G_Q + i - 1))
                    w.reduce_sum(nrm[:, 16:32], qsq[:].rearrange("p t (s d) -> p (t s) d", d=DH), AX)\
                        .then_inc(ssq_done, 1)
                if k in TILE_AT:
                    scan_tile(TILE_AT[k])
                if YT_AT.get(k, 0) % 4 == 3:
                    y_evac(YT_AT[k] // 4)
                if k % 2 == 0 and 6 <= k < HALF_PIECES:
                    split_lo(P_QKV + k // 2 + AHEAD)

            yf, tf = y[:].rearrange("p k s -> p (k s)"), tt[:].rearrange("p a n -> p (a n)")

            def gelu_argument():
                dve.wait_ge(y_read, 4)
                st.do(tt_(tf, yf, yf, ALU.mult))
                st.do(w.tensor_scalar(tf, tf, 0.044715, 1.0, ALU.mult, ALU.add))
                tt_(tf, tf, yf, ALU.mult).then_inc(gelu_in, 1)

            def gelu_product():
                dve.wait_ge(gelu_sig, 1)
                tt_(yf, yf, tf, ALU.mult).then_inc(z_done, 1)

            for j in range(HEADS + 3):
                if j >= 3:
                    dve.wait_ge(oh_done, j - 2)
                    w.scalar_tensor_tensor(out=ol[:, j - 3, :], in0=tp[:, 0:S], scalar=subg[:, 0:1],
                                           in1=oh[:, j - 3, :].bitcast(F32), op0=ALU.mult, op1=ALU.subtract)\
                        .then_inc(ol_done, 1)
                if j < HEADS:
                    dve.wait_ge(s_full, j + 1)
                    for m in range(2):
                        for qb, (k0, k1) in enumerate(((0, P), (P, 3 * P))):
                            ins = st.add(w.tensor_tensor_reduce(
                                out=sm[:, m, k0:k1], in0=sc[:, m, k0:k1], in1=mask[:, 2 * P - (k1 - k0):2 * P],
                                scale=1.0, scalar=-3e38, op0=ALU.add, op1=ALU.max,
                                accum_out=att[:, 2 * m + qb:2 * m + qb + 1]))
                    st.wait()
                    w.tensor_scalar(att[:, 4:8], att[:, 0:4], -SCALE, None, ALU.mult).then_inc(max_done, 1)
                split_lo(P_G + j + AHEAD)
                if j < HEADS:
                    dve.wait_ge(e_done, j + 1)
                    if j == 0:
                        dve.wait_ge(lam_done, 1)
                    st.do(w.reciprocal(att[:, 12:16], att[:, 8:12]))
                    st.do(w.tensor_scalar(att[:, 16:18], att[:, 14:16], lam[:, 0:1], -1.0, ALU.mult, ALU.mult))
                    if j:
                        dve.wait_ge(wt_pe, j)
                    for qb, (k0, k1) in enumerate(((0, P), (P, 3 * P))):
                        st.add(w.tensor_scalar(ww[:, k0:k1], ee[:, 0, k0:k1], att[:, 12 + qb:13 + qb], None, ALU.mult))
                    st.wait()
                    for qb, (k0, k1) in enumerate(((0, P), (P, 3 * P))):
                        ins = w.scalar_tensor_tensor(out=ww[:, k0:k1], in0=ee[:, 1, k0:k1],
                                                     scalar=att[:, 16 + qb:17 + qb], in1=ww[:, k0:k1],
                                                     op0=ALU.mult, op1=ALU.add)
                    ins.then_inc(w_done, 1)
                if 1 <= j <= HEADS:
                    dve.wait_ge(o_rs, j)
                    if j >= 2:
                        dve.wait_ge(ot_pe, j - 1)
                    for qb in range(2):
                        ins = w.tensor_scalar(on[:, qb, :], ov[:, qb * P:qb * P + P], oss[:, qb:qb + 1], None, ALU.mult)
                    ins.then_inc(o_done, 1)
                if j == 0:
                    gelu_argument()
                elif j == 1:
                    gelu_product()
                elif j == 2:
                    dve.wait_ge(z_hi, 1)
                    tt_(zl[:], y[:], zh[:].bitcast(F32), ALU.subtract).then_inc(z_lo, 1)
                if j == HEADS:
                    dve.wait_ge(pj_read[G_GLU % 2], read_count(G_GLU))
                    tt_(y[:], y[:], f8[:, 0:4, :], ALU.mult).then_inc(z_done, 1)
                    dve.wait_ge(z_hi, 2)
                    tt_(zl[:], y[:], zh[:].bitcast(F32), ALU.subtract).then_inc(z_lo, 1)

            def pair(i, G):
                full(dve, G)
                return pj[:, G % 2, :].rearrange("p (c s) -> p c s", c=4)
            for n in range(P_UP + 1, N_PRE):
                split_lo(n + AHEAD)
                if n in (P_UP + 1, P_UP + 2):
                    i = n - P_UP - 1
                    dve.wait_ge(g_sig, 2)
                    tt_(gT[:, 8 + 4 * i:12 + 4 * i], gT[:, 8 + 4 * i:12 + 4 * i], pair(i, G_UP + i), ALU.mult)\
                        .then_inc(pj_read[(G_UP + i) % 2], 1)
                if n in (P_AT + 2, P_WO):
                    i = 0 if n < P_WO else 1
                    tt_(gT[:, 4 * i:4 * i + 4], gT[:, 4 * i:4 * i + 4], pair(i, G_AT + i), ALU.mult)\
                        .then_inc(pj_read[(G_AT + i) % 2], 1)
                    dve.wait_ge(pj_read[(G_AT + i) % 2], read_count(G_AT + i))
                    dve.wait_ge(pj_read[(G_UP + i) % 2], read_count(G_UP + i))
                    tt_(gT[:, 4 * i:4 * i + 4], gT[:, 4 * i:4 * i + 4], gT[:, 8 + 4 * i:12 + 4 * i], ALU.add)\
                        .then_inc(mix_done, 1)
                    dve.wait_ge(ah_done, 9 + i)
                    tt_(al[:, 4 * i:4 * i + 4], gT[:, 4 * i:4 * i + 4], ah[:, 4 * i:4 * i + 4].bitcast(F32),
                        ALU.subtract).then_inc(al_done, 1)
                if n == P_WO:
                    dve.wait_ge(router_in, 16 * 7)
                    tt_(wr[:], wr[:], gains[:, 1, :].unsqueeze(2).to_broadcast([P, KC, 36]), ALU.mult)\
                        .then_inc(wr_done, 1)
            dve.wait_ge(xres_in, 16)
            for i in range(2):
                G = G_WO + i
                full(dve, G)
                xs = x1[:, :, 512 * i:512 * i + 512]
                tt_(xs, xs, pj[:, G % 2, :].rearrange("p (t n) -> p t n", t=T), ALU.add).then_inc(pj_read[G % 2], 1)

            normalise(xn2, x1, 2, 2)
            dve.wait_ge(xnh_done, 1)
            tt_(xnl[:], xn2[:], xnh[:].bitcast(F32), ALU.subtract).then_inc(xnl_done, 1)
            dve.wait_ge(lg_pe, 1)

            def R(k0, k1):
                return rt[:, :, k0:k1]

            def wide(k, n):
                return rt[:, :, k:k + 1].to_broadcast([P, T, n])
            logits = ov[:, 0:128].rearrange("p (t n) -> p t n", t=T)[:, :, 0:36]
            st.do(tt_(R(0, 36), logits, wrb[:].unsqueeze(1).to_broadcast([P, T, 36]), ALU.add))
            st.add(w.tensor_scalar(desc[:], iota[:, 0:NE], -1.0, float(NE), ALU.mult, ALU.add))
            st.do(w.reduce_max(R(36, 37), R(0, 4), AX))

            def first_max(vals, k_max, n, dst):
                st.do(tt_(dst, vals, wide(k_max, n), ALU.is_equal))
                st.do(tt_(dst, dst, desc[:, 0:n].unsqueeze(1).to_broadcast([P, T, n]), ALU.mult))
                st.do(w.reduce_max(R(37, 38), dst, AX))
                return tt_(dst, dst, wide(37, n), ALU.is_equal)
            tt_(R(44, 48), R(0, 4), wide(36, 4), ALU.subtract).then_inc(lg_in, 1)
            first_max(R(0, 4), 36, NG, R(56, 60)).then_inc(grp_done, 1)
            dve.wait_ge(grp_done, 1)
            le = R(4, 36).rearrange("p t (n e) -> p t n e", n=NG)
            prod = R(96, 128).rearrange("p t (n e) -> p t n e", n=NG)
            st.do(tt_(prod, le, R(56, 60).unsqueeze(3).to_broadcast([P, T, NG, NE]), ALU.mult))
            st.do(w.reduce_sum(R(60, 68), prod.rearrange("p t n e -> p t e n"), AX))
            st.do(w.reduce_max(R(68, 69), R(60, 68), AX))
            st.do(first_max(R(60, 68), 68, NE, R(72, 80)))
            st.do(w.scalar_tensor_tensor(out=R(60, 68), in0=R(72, 80), scalar=NEG, in1=R(60, 68),
                                         op0=ALU.mult, op1=ALU.add))
            st.do(w.reduce_max(R(69, 70), R(60, 68), AX))
            st.do(first_max(R(60, 68), 69, NE, R(80, 88)))
            tt_(R(89, 90), R(69, 70), R(68, 69), ALU.subtract).then_inc(lg_in, 1)

            dve.wait_ge(rank_pe, 1)
            ranks = ov[:, 128:136].rearrange("p (t n) -> p t n", t=T)
            st.do(tt_(R(40, 44), ranks, R(56, 60), ALU.mult))
            st.add(w.tensor_scalar(cnt[:, 0:4], ov[:, 136:140], float(P), None, ALU.is_gt))
            st.do(w.reduce_sum(R(95, 96), R(40, 44), AX))
            st.add(w.tensor_copy(slotc[:, :, 0:NG], wide(95, NG)))
            st.add(w.tensor_copy(ohc[:, :, 0:NG], R(56, 60)))
            st.add(w.tensor_scalar(slotc[:, :, NG:NG + 1], R(95, 96), -float(P), None, ALU.add))
            st.add(w.tensor_scalar(ohc[:, :, NG:NG + 1], R(95, 96), float(P), None, ALU.is_ge))
            st.add(w.reduce_sum(cnt[:, 4:5], cnt[:, 0:4], AX))
            st.do(tt_(cnt[:, 0:4], cnt[:, 0:4], iota[:, 0:4], ALU.mult))
            st.add(w.tensor_scalar(cnt[:, 4:5], cnt[:, 4:5], float(NG), None, ALU.add))
            st.do(w.reduce_sum(cnt[:, 5:6], cnt[:, 0:4], AX))
            w.tensor_copy(plan[:], cnt[:, 4:6]).then_inc(plan_done, 1)

            def one_hot(b):
                for t in range(T):
                    ins = w.tensor_scalar(pm[:, t, :], iota[:], slotc[:, t, bass.ds(b, 1)], ohc[:, t, bass.ds(b, 1)],
                                          ALU.is_equal, ALU.mult)
                ins.then_inc(m_pm, 1)

            def tokens_scaled():
                tt_(hgf, pj[:, 1, :].rearrange("p (c s) -> p c s", c=KC),
                    gains[:, 1, :].unsqueeze(2).to_broadcast([P, KC, P]), ALU.mult).then_inc(m_hgf, 1)

            def tokens_lo():
                tt_(hgl[:], hgf, hgh[:].bitcast(F32), ALU.subtract).then_inc(m_hgl, 1)
            one_hot(0)
            dve.wait_ge(lg_exp, 2)
            st.do(w.reduce_sum(R(52, 53), R(48, 52), AX))
            st.add(w.reciprocal(R(53, 54), R(52, 53)))
            st.do(w.tensor_scalar(R(91, 92), R(90, 91), 1.0, None, ALU.add))
            st.do(w.reciprocal(R(92, 93), R(91, 92)))
            st.do(tt_(R(93, 94), R(92, 93), R(53, 54), ALU.mult))
            st.do(tt_(R(94, 95), R(93, 94), R(90, 91), ALU.mult))
            for t in range(T):
                st.add(w.tensor_scalar(wl8[:, t, :], rt[:, t, 72:80], rt[:, t, 93:94], None, ALU.mult))
            st.wait()
            for t in range(T):
                ins = w.scalar_tensor_tensor(out=wl8[:, t, :], in0=rt[:, t, 80:88], scalar=rt[:, t, 94:95],
                                             in1=wl8[:, t, :], op0=ALU.mult, op1=ALU.add)
            ins.then_inc(wl_done, 1)
            dve.wait_ge(m_gat, 1)
            tokens_scaled()
            dve.wait_ge(m_hgh, 1)
            tokens_lo()

            nb = dve.value_load(plan[0:1, 0:1], min_val=NG, max_val=NG + 1)
            with dve.Fori(0, nb) as b:
                def act_lo(x):
                    dve.wait_ge(m_ach, b * NE + (x + 1))
                    tt_(acl[:, x % 2], tp[:, 0:FF].rearrange("p (r n) -> p r n", r=2), ach[:, x % 2].bitcast(F32), ALU.subtract)\
                        .then_inc(m_acl, 1)

                def tokens_added(t, base):
                    dve.wait_ge(m_sc, base + (t + 1))
                    tt_(x1[:, t, :], x1[:, t, :], pj[:, 1, :], ALU.add).then_inc(m_add, 1)
                for i, (kind, x, h) in enumerate(MOE):
                    if kind == "g" and h == 1 and x >= 1:
                        act_lo(x - 1)
                    if i in (2, 4):
                        tokens_added(i // 2 - 1, b * T)
                    split_lo(N_PRE + i + AHEAD, b)
                    if i == 0:
                        dve.wait_ge(m_ptp, b + 1)
                        w.tensor_copy(wc[:], tp[:, 400:400 + NE]).then_inc(m_wc, 1)
                    if i == 12:
                        one_hot(b + 1)
                    if i == 18:
                        dve.wait_ge(m_gat, b + 2)
                        tokens_scaled()
                    if kind == "g" and h == 1:
                        if x == 0:
                            dve.wait_ge(m_wc, b + 1)
                        gu = pj[:, 0, 512 * (x % 2):512 * (x % 2) + 512]
                        dve.wait_ge(m_sig, b * NE + (x + 1))
                        w.scalar_tensor_tensor(out=a1[:], in0=gu[:, 0:FF], scalar=wc[:, x:x + 1], in1=sg[:],
                                               op0=ALU.mult, op1=ALU.mult).then_inc(moe_step, 1)
                        dve.wait_ge(moe_step, b * NE + (x + 1))
                        tt_(ac[:, x % 2, :], a1[:], gu[:, FF:2 * FF], ALU.mult).then_inc(m_act, 1)
                    if kind == "d" and x == NE - 2:
                        act_lo(NE - 1)
                        dve.wait_ge(m_hgh, b + 2)
                        tokens_lo()
                dve.wait_ge(m_yh, b + 2)
                tt_(yl[:], sc[:].rearrange("p a n -> p (a n)"), yh[:].bitcast(F32), ALU.subtract).then_inc(m_yl, 1)
            for t in range(T):
                tokens_added(t, nb * T)

            normalise(xn2, x1, 4, 3)
            chunks_lo(10, 2)
            split_lo(N_PRE + 3, nb)
            for i in range(2):
                dve.wait_ge(pl_sig, i + 1)
                sgm = f8[:, 4 * i:4 * i + 4].rearrange("p c s -> p (c s)").rearrange("p (t n) -> p t n", t=T)
                st.do(tt_(sgm, sgm, pp[:, :, 512 * i:512 * i + 512], ALU.mult))
                xs = x1[:, :, 512 * i:512 * i + 512]
                tt_(xs, xs, sgm, ALU.add).then_inc(o_ready, 1)

        @block.tensor
        def _(pe):
            m = nc.tensor

            def mm3(o, lh, ll, rh, rl, start, stop):
                m.matmul(o, lh, rh, start=start, stop=False, skip_group_check=True)
                m.matmul(o, lh, rl, start=False, stop=False, skip_group_check=True)
                return m.matmul(o, ll, rh, start=False, stop=stop, skip_group_check=True)

            def split(i):
                return [t.rearrange("p (c n) -> p c n", c=4) for t in parts(i)]

            def parts(i):
                return whi[:, i % NSPL, :], wlo[:, i % NRAW, :]

            def ready(i, b=0):
                pe.wait_ge(lo_done, b * PER_BLOCK + (i + 1))

            def pair_free(G):
                pe.wait_ge(pj_read[G % 2], read_count(G) - 1)

            def by_width(i, G, rhs, part, blocks, last):
                wh, wl = split(i)
                for blk in blocks:
                    o = pj[:, G % 2, blk * S:blk * S + S]
                    for c in range(4):
                        cg = 4 * part[0] + c
                        ins = mm3(o, wh[:, c, blk * P:blk * P + P], wl[:, c, blk * P:blk * P + P],
                                  rhs[0][:, cg, :], rhs[1][:, cg, :],
                                  start=(part[0] == 0 and c == 0 and blk % 2 == 0),
                                  stop=(part[0] == part[1] - 1 and c == 3))
                if last:
                    ins.then_inc(piece_used, 1)
                return ins

            def by_token(o, i, t, part, b=0):
                wh, wl = split(i)
                for c in range(4):
                    cg = 4 * part[0] + c
                    ins = mm3(o, ah[:, cg, t * P:t * P + P], al[:, cg, t * P:t * P + P], wh[:, c, :], wl[:, c, :],
                                start=(part[0] == 0 and c == 0), stop=(part[0] == part[1] - 1 and c == 3))
                return ins

            pe.wait_ge(consts, 8)
            pe.wait_ge(small_in, 160)
            pe.wait_ge(ls_done, 1)
            m.transpose(ov[:, 0:80], smt[:], ident[0:80, 0:80]).then_inc(small_pe, 1)

            def transposes(src, done):
                for k in range(4):
                    for c in (2 * k, 2 * k + 1):
                        for t in range(T):
                            q = (c % 4) * S + t * P
                            ins = m.transpose(pj[:, k // 2, q:q + P], src[:, t, c::KC], ident[:])
                    ins.then_inc(done, 1)
            pe.wait_ge(xnd, 1)
            transposes(xn, xt_pe)
            pe.wait_ge(p_in, 16)
            for c in range(2):
                for t in range(T):
                    ins = m.transpose(tp[:, c * S + t * P:c * S + t * P + P], pst[:, t, c::2], ident[:])
            ins.then_inc(pt_pe, 1)
            for h in range(2):
                ready(P_U + h)
                if h == 0:
                    pe.wait_ge(pj_read[0], 1)
                    pe.wait_ge(pj_read[1], 1)
                by_width(P_U + h, G_U, (ah, al), (h, 2), range(4), True)

            def b_and_c_transposed():
                pe.wait_ge(bm_done, 1)
                for r in range(2):
                    for k in range(4):
                        ins = m.transpose(sc[:, r, k * P:k * P + P],
                                          bm[:, r, 4 * k:4 * k + 4].rearrange("p j g h -> p (j g h)"), ident[:])
                ins.then_inc(b_pe, 1)
                pe.wait_ge(col_done, 1)
                pe.wait_ge(ptl_done, 1)
                for r, bank in enumerate((ov, tp)):
                    for k in range(4):
                        ins = m.transpose(bank[:, k * P:k * P + P], cst[:, r, k, :], ident[:])
                ins.then_inc(c_pe, 1)

            def lambda_spread():
                pe.wait_ge(lam_sum, 1)
                pe.wait_ge(bT_done, 2)
                m.matmul(sc[:, 1, 0:1], ones[0:1, :], lams[0:1, 0:1], start=True, stop=True).then_inc(lam_pe, 1)

            def state_inputs(j):
                b, q, k = j % 2, 32 * (j % 4), j // 4
                if j == 0:
                    pe.wait_ge(pj_read[G_U % 2], read_count(G_U))
                if j == 1:
                    pe.wait_ge(lam_done, 1)
                if j >= 2:
                    pe.wait_ge(bu_read, j - 1)
                for r in range(2):
                    ins = m.matmul(sc[:, b, r * S:r * S + S], bT[q:q + 32, r, k, :], uT[q:q + 32, k, :],
                                   start=True, stop=True)
                ins.then_inc(bu_full, 1)

            def state_outputs(j):
                b, q, k = j % 2, 32 * (j % 4), j // 4
                if j == 0:
                    pe.wait_ge(cm_done, 1)
                elif j % 4 == 0:
                    pe.wait_ge(y_read, k)
                pe.wait_ge(rot_done, j + 1)
                for r in range(2):
                    ins = m.matmul(ov[q:q + 32, 0:S], cm[:, r, j, :], so[:, b, r * S:r * S + S],
                                   start=(r == 0), stop=(r == 1), skip_group_check=True)
                ins.then_inc(y_pe, 1)

            def qk_transposes(i, half):
                pe.wait_ge(pj_read[(G_Q + i) % 2], read_count(G_Q + i))
                if 2 * i + half:
                    pe.wait_ge(qt_done, 2 * i + half)
                for q in range(2):
                    for t in range(T):
                        hd = (2 * half + q) * P
                        ins = m.transpose(tp[:, q * S + t * P:q * S + t * P + P], qn[:, t, hd:hd + P], ident[:])
                ins.then_inc(qt_pe, 1)

            for n in range(P_QKV, P_G):
                G = G_Q + (n - P_QKV) // 2
                part = ((n - P_QKV) % 2, 2)
                ready(n)
                if part[0] == 0:
                    pair_free(G)
                for t in range(T):
                    ins = by_token(pj[:, G % 2, 512 * t:512 * t + 512], n, t, part)
                    if t == T - 1:
                        ins.then_inc(piece_used, 1)
                    k = 2 * (n - P_QKV) + t
                    if k == 1:
                        b_and_c_transposed()
                    if k == 5:
                        lambda_spread()
                    if k in TILE_AT:
                        state_inputs(TILE_AT[k])
                    if k in YT_AT:
                        state_outputs(YT_AT[k])
                    if k in QT_AT:
                        qk_transposes(*QT_AT[k])
            state_outputs(ST - 1)

            def scores(h):
                if h == 0:
                    pe.wait_ge(qt_done, 8)
                    pe.wait_ge(bu_read, ST)
                else:
                    pe.wait_ge(max_done, h)
                for mp in range(2):
                    r = slice(DH * mp, DH * mp + DH)
                    m.matmul(sc[:, mp, 0:P], qT[r, h, 0:P], kT[r, h, 0:P], start=True, stop=True)
                    ins = m.matmul(sc[:, mp, P:3 * P], qT[r, h, P:S], kT[r, h, :], start=True, stop=True)
                ins.then_inc(s_full, 1)

            def weights_transposed(h):
                pe.wait_ge(w_done, h + 1)
                if h >= 2:
                    pe.wait_ge(ol_done, h - 1)
                for q in range(3):
                    ins = m.transpose(tp[:, q * P:q * P + P], ww[:, q * P:q * P + P], ident[:])
                ins.then_inc(wt_pe, 1)

            def values(h):
                pe.wait_ge(wt_done, h + 1)
                if h == 0:
                    pe.wait_ge(y_read, 4)
                    pe.wait_ge(pj_read[G_V % 2], read_count(G_V))
                    pe.wait_ge(pj_read[(G_V + 1) % 2], read_count(G_V + 1))
                else:
                    pe.wait_ge(o_done, h)
                e = slice(P * h, P * h + P)
                m.matmul(ov[:, 0:P], wT[:, 0:P], v[:, 0, e], start=True, stop=True)
                m.matmul(ov[:, P:2 * P], wT[:, P:2 * P], v[:, 0, e], start=True, stop=False)
                m.matmul(ov[:, P:2 * P], wT[:, 2 * P:3 * P], v[:, 1, e], start=False, stop=True).then_inc(o_full, 1)

            def outputs_transposed(h):
                pe.wait_ge(o_done, h + 1)
                if h == HEADS - 1:
                    pe.wait_ge(ol_done, h)
                for t in range(T):
                    ins = m.transpose(tp[:, t * P:t * P + P], on[:, t, :], ident[:])
                ins.then_inc(ot_pe, 1)

            for j in range(HEADS + 2):
                n = P_G + j
                ready(n)
                if j < HEADS:
                    G = G_G + j // 2
                    if j % 2 == 0:
                        pair_free(G)
                    by_width(n, G, (ah, al), (j % 2, 2), (0, 1), False)
                    scores(j)
                elif n == P_GLU:
                    pair_free(G_GLU)
                    pe.wait_ge(z_lo, 1)
                    by_width(n, G_GLU, (zh, zl), (0, 1), (0, 1), False)
                if 1 <= j <= HEADS:
                    weights_transposed(j - 1)
                if j < HEADS:
                    by_width(n, G, (ah, al), (j % 2, 2), (2, 3), True)
                elif n == P_GLU:
                    by_width(n, G_GLU, (zh, zl), (0, 1), (2, 3), True)
                else:
                    wh, wl_ = (t.rearrange("p (c n) -> p c n", c=2) for t in parts(n))
                    for t in range(T):
                        pair_free(G_PLE + t)
                        for q in range(2):
                            for c in range(2):
                                ins = mm3(pj[:, (G_PLE + t) % 2, 512 * q:512 * q + 512],
                                          pth[:, c, t * P:t * P + P], ptl[:, c, t * P:t * P + P],
                                          wh[:, c, 512 * q:512 * q + 512], wl_[:, c, 512 * q:512 * q + 512],
                                          start=(c == 0), stop=(c == 1))
                    ins.then_inc(piece_used, 1)
                if 1 <= j <= HEADS:
                    values(j - 1)
                if j >= 2:
                    outputs_transposed(j - 2)

            for i in range(2):
                ready(P_UP + i)
                pair_free(G_UP + i)
                pe.wait_ge(z_lo, 2)
                by_width(P_UP + i, G_UP + i, (zh, zl), (0, 1), range(4), True)
            for n in range(P_AT, P_WO):
                G = G_AT + (n - P_AT) // 2
                ready(n)
                pair_free(G)
                pe.wait_ge(ol_done, HEADS)
                by_width(n, G, (oh, ol), ((n - P_AT) % 2, 2), range(4), True)
            for n in range(P_WO, N_PRE):
                G, h = G_WO + (n - P_WO) // 2, (n - P_WO) % 2
                ready(n)
                pair_free(G)
                pe.wait_ge(al_done, h + 1)
                for t in range(T):
                    ins = by_token(pj[:, G % 2, 512 * t:512 * t + 512], n, t, (h, 2))
                ins.then_inc(piece_used, 1)

            pe.wait_ge(xnd, 2)
            transposes(xn2, xt_pe)
            for i in range(2):
                pe.wait_ge(pj_read[i], read_count(G_WO) + 1)
            pe.wait_ge(wr_done, 1)
            for t in range(T):
                for c in range(KC):
                    ins = m.matmul(ov[:, 64 * t:64 * t + 36], f8[:, c, t * P:t * P + P], wr[:, c, :],
                                   start=(c == 0), stop=(c == KC - 1))
            ins.then_inc(lg_pe, 1)
            pe.wait_ge(grp_done, 1)
            g0, g1 = rt[:, 0, 56:60], rt[:, 1, 56:60]
            m.matmul(ov[:, 128:132], upper[:], g0, start=True, stop=True)
            m.matmul(ov[:, 132:136], ones[:], g0, start=True, stop=False)
            m.matmul(ov[:, 132:136], upper[:], g1, start=False, stop=True)
            m.matmul(ov[:, 136:140], ones[:], g0, start=True, stop=False)
            m.matmul(ov[:, 136:140], ones[:], g1, start=False, stop=True).then_inc(rank_pe, 1)

            def gather():
                for c in range(KC):
                    o = pj[:, 1, c * P:c * P + P]
                    for t in range(T):
                        m.matmul(o, xnh[:, t, c::KC], pm[:, t, :], start=(t == 0), stop=False)
                        ins = m.matmul(o, xnl[:, t, c::KC], pm[:, t, :], start=False, stop=(t == T - 1))
                ins.then_inc(m_gat, 1)
            pe.wait_ge(xnh_done, 1)
            pe.wait_ge(xnl_done, 1)
            pe.wait_ge(m_pm, 1)
            gather()
            pe.wait_ge(wl_done, 1)
            pe.wait_ge(plan_done, 1)
            nb = pe.value_load(plan[0:1, 0:1], min_val=NG, max_val=NG + 1)

            def scatter(t, base):
                if t:
                    pe.wait_ge(m_add, base + t)
                for q in range(2):
                    o = pj[:, 1, 512 * q:512 * q + 512]
                    m.matmul(o, pT[:, t * P:t * P + P], yh[:, 512 * q:512 * q + 512], start=True, stop=False)
                    ins = m.matmul(o, pT[:, t * P:t * P + P], yl[:, 512 * q:512 * q + 512],
                                   start=False, stop=True)
                ins.then_inc(m_sc, 1)
            pe.wait_ge(m_yh, 1)
            with pe.Fori(0, nb) as b:
                pe.wait_ge(m_pt, b + 1)
                for t in range(T):
                    m.transpose(ov[:, t * P:t * P + P], pm[:, t, :].bitcast(F32), ident[:])
                for t in range(T):
                    ins = m.matmul(tp[:, 400:400 + NE], pm[:, t, :].bitcast(F32), wl8[:, t, :],
                                   start=(t == 0), stop=(t == T - 1))
                ins.then_inc(m_ptp, 1)

                def act_transposes(x):
                    pe.wait_ge(m_act, b * NE + (x + 1))
                    if x == 0:
                        pe.wait_ge(m_wc, b + 1)
                    for r in range(2):
                        ins = m.transpose(tp[:, r * P:r * P + P], ac[:, x % 2, r::2], ident[:])
                    ins.then_inc(m_tp, 1)
                for i, (kind, x, h) in enumerate(MOE):
                    ready(N_PRE + i, b)
                    if kind == "g":
                        if i == 0:
                            pe.wait_ge(m_hgl, b + 1)
                        wh, wl_ = (t.rearrange("p (w c n) -> p w c n", w=2, c=4) for t in parts(N_PRE + i))
                        o = pj[:, 0, 512 * (x % 2):512 * (x % 2) + 512].rearrange("p (w n) -> p w n", w=2)
                        for c in range(4):
                            ins = mm3(o, hgh[:, 4 * h + c, :], hgl[:, 4 * h + c, :], wh[:, :, c, :], wl_[:, :, c, :],
                                      start=(h == 0 and c == 0), stop=(h == 1 and c == 3))
                        ins.then_inc(piece_used, 1)
                        if h == 0 and x >= 1:
                            act_transposes(x - 1)
                    else:
                        wh, wl_ = (t.rearrange("p (c n) -> p c n", c=2) for t in parts(N_PRE + i))
                        pe.wait_ge(m_acl, b * NE + (x + 1))
                        for q in range(2):
                            for c in range(2):
                                ins = mm3(sc[:, q, :], ach[:, x % 2, c, :], acl[:, x % 2, c, :],
                                          wh[:, c, 512 * q:512 * q + 512], wl_[:, c, 512 * q:512 * q + 512],
                                          start=(x == 0 and c == 0), stop=(x == NE - 1 and c == 1))
                            if q == 0 and x == NE - 2:
                                act_transposes(NE - 1)
                        ins.then_inc(piece_used, 1)
                    if i == 1:
                        pe.wait_ge(m_yl, b + 1)
                        pe.wait_ge(m_hgf, b + 1)
                        scatter(0, b * T)
                    if i == 3:
                        scatter(1, b * T)
                    if i == 14:
                        pe.wait_ge(m_pm, b + 2)
                        pe.wait_ge(m_add, (b + 1) * T)
                        gather()
            pe.wait_ge(m_yl, nb + 1)
            pe.wait_ge(m_pt, nb + 1)
            pe.wait_ge(m_hgf, nb + 1)
            for t in range(T):
                scatter(t, nb * T)

            pe.wait_ge(xnd, 3)
            transposes(xn2, xt3)
            for i in range(2):
                pe.wait_ge(pj_read[i], read_count(G_WO) + 2)
            for j in range(4):
                ready(N_PRE + j, nb)
                for t in range(T):
                    ins = by_token(pj[:, j // 2, 512 * t:512 * t + 512], N_PRE + j, t, (j % 2, 2))
                ins.then_inc(piece_used, 1)


_INS = ['x', 'p', 'attn_norm_g', 'w_in', 'b_gate', 'q_norm_g', 'k_norm_g', 'lam_qk', 'subln_g', 'w_attn_up',
        'ssm_lam_re', 'ssm_lam_im', 'ssm_log_step', 'ssm_b_re', 'ssm_b_im', 'ssm_c_re', 'ssm_c_im', 'ssm_d',
        'w_glu', 'b_glu', 'w_ssm_up', 'w_out', 'ffn_norm_g', 'w_router_group', 'b_router_group',
        'w_router_expert', 'b_router_expert', 'w_exp_gate', 'w_exp_up', 'w_exp_down',
        'ple_norm_g', 'w_ple_gate', 'w_ple']


def kernel(**inputs):
    import numpy as _np
    import concourse.bacc as _bacc
    from concourse import mybir as _mybir
    from concourse.bass_utils import run_bass_kernel_spmd as _run

    nc = _bacc.Bacc("TRN2", target_bir_lowering=False, num_devices=1)
    arrays, args = {}, {}
    for name in _INS:
        arr = _np.ascontiguousarray(inputs[name])
        arrays[f"in_{name}_dram"] = arr
        args[name] = nc.dram_tensor(f"in_{name}_dram", arr.shape, _mybir.dt.from_np(arr.dtype),
                                    kind="ExternalInput").ap()
    out = nc.dram_tensor("out_0_dram", (1, S, D), _mybir.dt.float32, kind="ExternalOutput").ap()
    build(nc, args, out)
    r = _run(nc, [arrays], core_ids=[0])
    return r.results[0]["out_0_dram"]
```

```python
from contextlib import ExitStack
import math

import numpy as np
import concourse.bass as bass
from concourse import mybir

F32 = mybir.dt.float32
F32R = mybir.dt.float32r
I32 = mybir.dt.int32
ALU = mybir.AluOpType
ACT = mybir.ActivationFunctionType
AX = mybir.AxisListType.X

P = 128
S = 256
T = S // P
D = 1024
KC = D // P
HEADS = 8
DH = 64
SSMW = 512
SG = 32
NST = 64
SH = 16
ST = SG * NST // P
HALF = 128
LEVELS = 7
NG = 4
NE = 8
FF = 256
EPS = 1e-6
LAM_INIT = 0.8 - 0.6 * math.exp(-0.3 * 0)
SCALE = DH ** -0.5
NEG = -1e30
GELU_C = 2.0 * math.sqrt(2.0 / math.pi)
ROUND = 1.5 * 2.0 ** 23
PI2_HI = 6.28125
PI2_MID = 0.0019350051879882812
PI2_LO = 2 * math.pi - PI2_HI - PI2_MID

NRAW = 8
NSPL = 4
AHEAD = 3
PIECE = 2048

P_U = 0
P_QKV = 2
P_G = 14
P_GLU = P_G + 6
P_UP = 23
P_AT = 25
P_WO = 29
P_PLE = 33
N_PRE = 34
PER_BLOCK = 3 * NE
TILE_AT = {6 + j: j for j in range(ST)}
YT_AT = {k + 3: j for k, j in TILE_AT.items()}
HALF_PIECES = 2 * (P_G - P_QKV)
QN_AT = {4 * i + 4: i for i in range(4)}
QT_AT = {4 * i + 8 + h: (i, h) for i in range(4) for h in range(2)}
G_U, G_Q, G_K, G_V, G_G, G_GLU, G_UP, G_AT, G_WO, G_PLE = 0, 1, 3, 5, (7, 8, 9, 11), 10, 12, 14, 16, 18
C_BG, C_LR, C_LI, C_BGLU, C_D, C_SUB, C_QG, C_KG, C_LS = 0, 16, 32, 48, 52, 56, 57, 58, 64


def moe_order():
    order = [("g", 0, 0), ("g", 0, 1)]
    for e in range(NE):
        if e + 1 < NE:
            order += [("g", e + 1, 0), ("g", e + 1, 1)]
        order.append(("d", e, 0))
    return order


MOE = moe_order()


class Steps:

    def __init__(self, eng, sem):
        self.eng, self.sem, self.n, self.base = eng, sem, 0, 0

    def add(self, ins):
        ins.then_inc(self.sem, 1)
        self.n += 1
        return ins

    def wait(self):
        self.eng.wait_ge(self.sem, self.base + self.n)

    def do(self, ins):
        self.add(ins)
        self.wait()


def build(nc, a, out):
    ctx = ExitStack()
    with ctx:
        def sb(name, shape, dt=F32, stack=None):
            return (stack or ctx).enter_context(nc.sbuf_tensor(name, shape, dt))

        def sem(name):
            return ctx.enter_context(nc.semaphore(name))

        ring = ExitStack()
        raw = sb("raw", [P, NRAW, PIECE], stack=ring)
        ring.close()
        wlo = sb("wlo", [P, NRAW, PIECE], F32R)
        whi = sb("whi", [P, NSPL, PIECE], F32R)
        ah = sb("ah", [P, KC, S], F32R)
        al = sb("al", [P, KC, S], F32R)
        pst = sb("pst", [P, T, 256])
        pth = sb("pth", [P, 2, S], F32R)
        ptl = sb("ptl", [P, 2, S], F32R)
        ident = sb("ident", [P, P])
        ones = sb("ones", [P, P])
        upper = sb("upper", [P, P])
        iota = sb("iota", [P, P])
        mask = sb("mask", [P, 2 * P])
        mk = sb("mk", [P, 4])
        half_c = sb("half_c", [P, 64])
        smt = sb("smt", [80, P])
        lst = sb("lst", [80, 2])
        col = sb("col", [P, 80])
        gains = sb("gains", [P, 3, KC])
        subg = sb("subg", [P, 1])
        lamq = sb("lamq", [1, 4 * DH])
        lamp = sb("lamp", [1, 2 * DH])
        lams = sb("lams", [1, 4])
        lam = sb("lam", [P, 1])
        nrm = sb("nrm", [P, 64])
        wr = sb("wr", [P, KC, 36])
        wrb = sb("wrb", [P, 36])
        ss = sb("ss", [P, 24, 16])
        rt = sb("rt", [P, 2, 160])
        slotc = sb("slotc", [P, T, 8])
        ohc = sb("ohc", [P, T, 8])
        wl8 = sb("wl8", [P, T, NE + 1])
        wc = sb("wc", [P, NE + 1])
        cnt = sb("cnt", [P, 8])
        plan = sb("plan", [P, 2], I32)
        att = sb("att", [P, 32])
        oss = sb("oss", [P, 4])
        osq = sb("osq", [P, 2, P])
        desc = sb("desc", [P, NE])

        ph = ExitStack()
        qT = sb("qT", [P, HEADS, S], stack=ph)
        kT = sb("kT", [P, HEADS, S], stack=ph)
        v = sb("v", [P, T, D], stack=ph)
        y = sb("y", [P, 4, S], stack=ph)
        p1 = ExitStack()
        qsq = sb("qsq", [P, T, 512], stack=p1)
        qn = sb("qn", [P, T, 512], stack=p1)
        ptab = sb("ptab", [P, 2, ST, HALF], stack=p1)
        bT = sb("bT", [P, 2, 4, P], stack=p1)
        cm = sb("cm", [P, 2, ST, 32], stack=p1)
        uT = sb("uT", [P, 4, S], stack=p1)
        tt = sb("tt", [P, 2, 512], stack=p1)
        rr = sb("rr", [P, 2, 512], stack=p1)
        so = sb("so", [P, 2, 512], stack=p1)
        pp2 = sb("pp2", [P, 512], stack=p1)
        ini = sb("ini", [P, 4], stack=p1)
        p1.close()
        p2 = ExitStack()
        zh = sb("zh", [P, 4, S], F32R, stack=p2)
        zl = sb("zl", [P, 4, S], F32R, stack=p2)
        gT = sb("gT", [P, 16, S], stack=p2)
        oh = sb("oh", [P, HEADS, S], F32R, stack=p2)
        ol = sb("ol", [P, HEADS, S], F32R, stack=p2)
        sm = sb("sm", [P, 2, 384], stack=p2)
        ee = sb("ee", [P, 2, 384], stack=p2)
        ww = sb("ww", [P, 384], stack=p2)
        wT = sb("wT", [P, 384], stack=p2)
        on = sb("on", [P, 2, P], stack=p2)
        p2.close()
        ph.close()
        p3 = ExitStack()
        f8 = sb("f8", [P, KC, S], stack=p3)
        pp = sb("pp", [P, T, D], stack=p3)
        x1 = sb("x1", [P, T, D], stack=p3)
        xnh = sb("xnh", [P, T, D], F32R, stack=p3)
        xnl = sb("xnl", [P, T, D], F32R, stack=p3)
        xn2 = sb("xn2", [P, T, D], stack=p3)
        hgh = sb("hgh", [P, KC, P], F32R, stack=p3)
        hgl = sb("hgl", [P, KC, P], F32R, stack=p3)
        yh = sb("yh", [P, D], F32R, stack=p3)
        yl = sb("yl", [P, D], F32R, stack=p3)
        pm = sb("pm", [P, T, P], F32R, stack=p3)
        pT = sb("pT", [P, S], F32R, stack=p3)
        sg = sb("sg", [P, FF], stack=p3)
        a1 = sb("a1", [P, FF], stack=p3)
        ac = sb("ac", [P, 2, FF], stack=p3)
        ach = sb("ach", [P, 2, 2, P], F32R, stack=p3)
        acl = sb("acl", [P, 2, 2, P], F32R, stack=p3)
        p3.close()
        xin, xn = qT[:].rearrange("p a b -> p (a b)").rearrange("p (t d) -> p t d", t=T), \
            kT[:].rearrange("p a b -> p (a b)").rearrange("p (t d) -> p t d", t=T)
        cst = v[:, 0, :].rearrange("p (r k n) -> p r k n", r=2, k=4)
        bm = v[:, 1, :].rearrange("p (r j g h) -> p r j g h", r=2, j=ST, g=2)
        pw = osq[:].rearrange("p a n -> p (a n)").rearrange("p (r i j) -> p r i j", r=2, i=LEVELS + 1)
        hgf = f8[:, 0:4].rearrange("p a b -> p (a b)").rearrange("p (c s) -> p c s", c=KC)
        bst = qsq[:].rearrange("p t n -> p (t n)").rearrange("p (r j h) -> p r j h", r=4, j=ST)

        def psum(name, shape):
            return ctx.enter_context(nc.psum_tensor(name, shape, F32))
        pj = psum("pj", [P, 2, 1024])
        sc = psum("sc", [P, 2, 512])
        tp = psum("tp", [P, 512])
        ov = psum("ov", [P, 512])

        xt_banks0 = [pj[:, k // 2, 512 * (k % 2):512 * (k % 2) + 512] for k in range(4)]
        xt_banks = [sc[:, 0, :], sc[:, 1, :], tp[:], ov[:]]

        raw_in = [sem(f"raw_in{i}") for i in range(NRAW)]
        hi_done = sem("hi_done")
        lo_done = sem("lo_done")
        piece_used = sem("piece_used")
        x_in, small_in, vec_in, p_in, xres_in, bc_in, router_in = (
            sem(n) for n in ("x_in", "small_in", "vec_in", "p_in", "xres_in", "bc_in", "router_in"))
        pool_step, act_step, dve_step = sem("pool_step"), sem("act_step"), sem("dve_step")
        moe_step = sem("moe_step")
        consts = sem("consts")
        xsq = sem("xsq")
        xrs = sem("xrs")
        xnd = sem("xnd")
        xt_pe = sem("xt_pe")
        ah_done = sem("ah_done")
        al_done = sem("al_done")
        pj_read = [sem(f"pj_read{i}") for i in range(2)]
        ls_done = sem("ls_done")
        small_pe = sem("small_pe")
        col_done = sem("col_done")
        lam_row, lam_exp, lam_sum, lam_pe, lam_done = (
            sem(n) for n in ("lam_row", "lam_exp", "lam_sum", "lam_pe", "lam_done"))
        dt_done = sem("dt_done")
        th_done = sem("th_done")
        trig = sem("trig")
        pow_done = sem("pow_done")
        re_done, im_done = sem("re_done"), sem("im_done")
        bm_done = sem("bm_done")
        b_pe, c_pe = sem("b_pe"), sem("c_pe")
        bT_done, cm_done = sem("bT_done"), sem("cm_done")
        bu_full = sem("bu_full")
        bu_read = sem("bu_read")
        scan_done = sem("scan_done")
        rot_done = sem("rot_done")
        y_pe = sem("y_pe")
        y_read = sem("y_read")
        qsq_done = sem("qsq_done")
        ssq_done = sem("ssq_done")
        qk_rs = sem("qk_rs")
        qt_pe = sem("qt_pe")
        qt_done = sem("qt_done")
        gelu_in, gelu_sig, z_done, z_hi, z_lo = (
            sem(n) for n in ("gelu_in", "gelu_sig", "z_done", "z_hi", "z_lo"))
        s_full = sem("s_full")
        max_done = sem("max_done")
        e_done = sem("e_done")
        w_done = sem("w_done")
        wt_pe, wt_done = sem("wt_pe"), sem("wt_done")
        o_full = sem("o_full")
        o_sq, o_rs, o_done = sem("o_sq"), sem("o_rs"), sem("o_done")
        ot_pe, oh_done, ol_done = sem("ot_pe"), sem("oh_done"), sem("ol_done")
        g_sig = sem("g_sig")
        glu_sig = sem("glu_sig")
        pt_pe, pth_done, ptl_done = sem("pt_pe"), sem("pth_done"), sem("ptl_done")
        mix_done = sem("mix_done")
        xnh_done, xnl_done = sem("xnh_done"), sem("xnl_done")
        ple_pe = sem("ple_pe")
        f8_done = sem("f8_done")
        wr_done = sem("wr_done")
        lg_pe, lg_in, lg_exp = sem("lg_pe"), sem("lg_in"), sem("lg_exp")
        grp_done, rank_pe, plan_done = sem("grp_done"), sem("rank_pe"), sem("plan_done")
        m_pm = sem("m_pm")
        m_gat = sem("m_gat")
        m_hgf = sem("m_hgf")
        m_hgh, m_hgl = sem("m_hgh"), sem("m_hgl")
        m_ptp = sem("m_ptp")
        m_pt, m_wc = sem("m_pt"), sem("m_wc")
        m_sig, m_act = sem("m_sig"), sem("m_act")
        m_tp, m_ach, m_acl = sem("m_tp"), sem("m_ach"), sem("m_acl")
        m_yh, m_yl = sem("m_yh"), sem("m_yl")
        m_sc, m_add = sem("m_sc"), sem("m_add")
        wl_done = sem("wl_done")
        xt3, pl_sig = sem("xt3"), sem("pl_sig")
        o_ready, o_out = sem("o_ready"), sem("o_out")

        last_piece = {G_U: P_U + 1, G_GLU: P_GLU, G_PLE: P_PLE, G_PLE + 1: P_PLE, G_UP: P_UP, G_UP + 1: P_UP + 1}
        last_piece.update({G_Q + i: P_QKV + 2 * i + 1 for i in range(6)})
        last_piece.update({G: P_G + 2 * i + 1 + (i == 3) for i, G in enumerate(G_G)})
        last_piece.update({G_AT + i: P_AT + 2 * i + 1 for i in range(2)})
        last_piece.update({G_WO + i: P_WO + 2 + i for i in range(2)})

        def level(i, part):
            L = 2 ** i
            c, s = (pw[:, r, i, :].unsqueeze(2).to_broadcast([P, ST, L]) for r in range(2))
            return L, c, s, ptab[:, 0, :, 0:L], ptab[:, 1, :, 0:L], ptab[:, part, :, L:2 * L]

        def full(eng, G):
            eng.wait_ge(piece_used, last_piece[G] + 1)

        def read_count(G):
            return G // 2 + 2

        w_in = a["w_in"][0].rearrange("(p h c) n -> h p c n", h=2, c=4)

        def cols(w, c0):
            return [w[h, :, :, c0:c0 + 512] for h in range(2)]
        glu_w = a["w_glu"][0].rearrange("(c p) n -> p c n", p=P)
        up_w = a["w_ssm_up"][0].rearrange("(c p) n -> p c n", p=P)
        at_w = a["w_attn_up"][0].rearrange("(h c p) n -> h p c n", h=2, p=P)
        wo_w = a["w_out"][0].rearrange("(h c p) n -> h p c n", h=2, p=P)
        pg_w = a["w_ple_gate"][0].rearrange("(p h c) n -> h p c n", h=2, c=4)
        pl_w = a["w_ple"][0].rearrange("(p c) n -> p c n", c=2)
        pre = cols(w_in, 3072)
        for c0 in (0, 512, 1024, 1536, 2048, 2560):
            pre += cols(w_in, c0)
        for g in range(4):
            if g == 3:
                pre.append(glu_w)
            pre += cols(w_in, 3584 + 512 * g)
        pre += [up_w[:, :, 0:512], up_w[:, :, 512:1024]]
        pre += cols(at_w, 0) + cols(at_w, 512)
        pre += [half for pair in zip(cols(wo_w, 0), cols(wo_w, 512)) for half in pair] + [pl_w]
        assert len(pre) == N_PRE
        ple = cols(pg_w, 0) + cols(pg_w, 512)
        wg_e = a["w_exp_gate"][0].rearrange("n e (p h c) f -> (n e) h p (c f)", h=2, c=4)
        wu_e = a["w_exp_up"][0].rearrange("n e (p h c) f -> (n e) h p (c f)", h=2, c=4)
        wd_e = a["w_exp_down"][0].rearrange("n e (p c) d -> (n e) p (c d)", c=2)
        xd = a["x"][0].rearrange("(t p) d -> p t d", p=P)
        outd = out[0].rearrange("(t p) d -> p t d", p=P)

        block = ctx.enter_context(nc.Block())

        @block.sync
        def _(sp):
            def load(i, halves, b=0):
                if i >= NRAW:
                    sp.wait_ge(piece_used, b * PER_BLOCK + (i - NRAW + 1))
                for dst, src in halves(raw[:, i % NRAW, :]):
                    sp.dma_start(dst, src).then_inc(raw_in[i % NRAW], 16)

            def plain(src):
                k = src.shape[1]

                def halves(slot):
                    d = slot.rearrange("p (c n) -> p c n", c=k)
                    return [(d[:, 0:k // 2], src[:, 0:k // 2]), (d[:, k // 2:], src[:, k // 2:])]
                return halves
            for t in range(T):
                sp.dma_start(xin[:, t], xd[:, t]).then_inc(x_in, 16)
            for n in range(N_PRE):
                load(n, plain(pre[n]))
                if n == 0:
                    for i, nm in enumerate(("ssm_b_re", "ssm_b_im")):
                        sp.dma_start(bst[:, i], a[nm][0].rearrange("(j g) s h -> (g s) j h", g=2)).then_inc(bc_in, 16)
                    for i, nm in enumerate(("ssm_c_re", "ssm_c_im")):
                        for d in range(2):
                            sp.dma_start(cst[:, i, :, NST * d:NST * d + NST],
                                         a[nm][0].rearrange("(k g) h s -> (g h) k s", g=8)).then_inc(bc_in, 16)
                    sp.wait_ge(small_in, 160)
                if n == 2:
                    sp.dma_start(pst[:], a["p"][0, 0].rearrange("(t p) d -> p t d", p=P)).then_inc(p_in, 16)
            sp.wait_ge(o_full, HEADS)
            sp.dma_start(x1[:], xd).then_inc(xres_in, 16)

            def block_loads(b, group):
                for i, (kind, e, h) in enumerate(MOE):
                    ex = group * NE + e

                    def halves(slot):
                        d = slot.rearrange("p (w n) -> p w n", w=2)
                        if kind == "g":
                            return [(d[:, w], m[bass.ds(ex, 1), h].rearrange("a p n -> (a p) n"))
                                    for w, m in enumerate((wg_e, wu_e))]
                        s = wd_e[bass.ds(ex, 1)].rearrange("a p (w n) -> (a p) w n", w=2)
                        return [(d[:, w], s[:, w]) for w in range(2)]
                    load(N_PRE + i, halves, b)
            with sp.Fori(0, NG) as b:
                block_loads(b, b)
            sp.wait_ge(plan_done, 1)
            nb = sp.value_load(plan[0:1, 0:1], min_val=NG, max_val=NG + 1)
            gx = sp.value_load(plan[0:1, 1:2], min_val=0, max_val=NG - 1)
            with sp.If(nb > NG):
                block_loads(NG, gx)
            for j in range(4):
                load(N_PRE + j, plain(ple[j]), nb)
            for i in range(2):
                sp.wait_ge(o_ready, i + 1)
                sp.dma_start(outd[:, :, 512 * i:512 * i + 512], x1[:, :, 512 * i:512 * i + 512]).then_inc(o_out, 16)
            sp.wait_ge(o_out, 32)

        @block.gpsimd
        def _(pool):
            g = nc.gpsimd
            st = Steps(pool, pool_step)
            for buf, val in ((ones, 1.0), (half_c, -0.5), (mask, 0.0), (mk, -1.0), (slotc, -1.0), (ohc, 0.0)):
                st.add(g.memset(buf[:], val))
            st.wait()
            g.affine_select(out=ident[:], in_=ones[:], compare_op=ALU.is_equal, fill=0.0, base=0,
                            pattern=[[-1, P]], channel_multiplier=1).then_inc(consts, 1)
            g.affine_select(out=upper[:], in_=ones[:], compare_op=ALU.is_gt, fill=0.0, base=0,
                            pattern=[[1, P]], channel_multiplier=-1).then_inc(consts, 1)
            g.affine_select(out=mask[:, P:], in_=mask[:, P:], compare_op=ALU.is_ge, fill=NEG, base=0,
                            pattern=[[-1, P]], channel_multiplier=1).then_inc(consts, 1)
            g.iota(iota[:], pattern=[[1, P]], base=0, channel_multiplier=0,
                   allow_small_or_imprecise_dtypes=True).then_inc(consts, 1)
            for i, src in enumerate((ones[:, 0:1], ones[:, 0:1], mk[:, 2:3], mk[:, 3:4])):
                sign, cmp = ((-1, ALU.is_gt), (1, ALU.is_ge))[i % 2]
                g.affine_select(out=mk[:, i:i + 1], in_=src, compare_op=cmp, fill=0.0, base=-64 * sign,
                                pattern=[[0, 1]], channel_multiplier=sign).then_inc(consts, 1)

            def inv_root(ap, width, dim, done):
                st.do(g.tensor_scalar(ap, ap, 1.0 / dim, EPS, ALU.mult, ALU.add))
                g.tensor_tensor(ap, ap, half_c[:, 0:width], ALU.pow).then_inc(done, 1)
            pool.wait_ge(xsq, 1)
            inv_root(nrm[:, 0:2], 2, D, xrs)

            def rload(dst, src):
                pool.dma_start(dst, src).then_inc(router_in, 16)
            for i, nm in enumerate(("ffn_norm_g", "ple_norm_g")):
                rload(gains[:, 1 + i, :], a[nm][0].rearrange("(p c) -> p c", c=KC))
            rload(wr[:, :, 0:NG], a["w_router_group"][0].rearrange("(p c) n -> p c n", c=KC))
            for n in range(NG):
                rload(wr[:, :, NG + NE * n:NG + NE * n + NE],
                      a["w_router_expert"][0, n].rearrange("(p c) e -> p c e", c=KC))
            rload(wrb[:, 0:NG], a["b_router_group"][0].partition_broadcast(P))
            rload(wrb[:, NG:36], a["b_router_expert"][0].rearrange("n e -> (n e)").partition_broadcast(P))

            g.memset(ptab[:, 1, :, 0:1], 0.0).then_inc(im_done, 1)
            pool.wait_ge(im_done, 1)
            pool.wait_ge(pow_done, 1)
            for i in range(LEVELS):
                L, c_, s_, re, im, new = level(i, 1)
                t2 = rr[:].rearrange("p a n -> p (a n)")[:, 0:ST * L].rearrange("p (j l) -> p j l", j=ST)
                pool.wait_ge(re_done, i + 1)
                st.add(g.tensor_tensor(new, re, s_, ALU.mult))
                st.do(g.tensor_tensor(t2, im, c_, ALU.mult))
                g.tensor_tensor(new, new, t2, ALU.add).then_inc(im_done, 1)
                pool.wait_ge(im_done, i + 2)

            def rotate_back(j):
                b = j % 2
                pool.wait_ge(scan_done, j + 1)
                if j >= 2:
                    pool.wait_ge(y_pe, j - 1)
                c, s = (ptab[:, i, j, :].unsqueeze(1).to_broadcast([P, 4, HALF]) for i in range(2))
                r4 = rr[:, b, :].rearrange("p (a t) -> p a t", a=4)
                st.add(g.tensor_tensor(so[:, b, :].rearrange("p (a t) -> p a t", a=4), r4, c, ALU.mult))
                st.do(g.tensor_tensor(pp2[:].rearrange("p (a t) -> p a t", a=4), r4, s, ALU.mult))
                g.tensor_tensor(so[:, b, 0:256], so[:, b, 0:256], pp2[:, 256:512], ALU.subtract)
                g.tensor_tensor(so[:, b, 256:512], so[:, b, 256:512], pp2[:, 0:256], ALU.add).then_inc(rot_done, 1)
                pool.wait_ge(rot_done, j + 1)

            for k in range(HALF_PIECES):
                if k in QN_AT:
                    pool.wait_ge(ssq_done, QN_AT[k] + 1)
                    inv_root(nrm[:, 16:32], 16, DH, qk_rs)
                if k in TILE_AT:
                    rotate_back(TILE_AT[k])
            for h in range(HEADS):
                pool.wait_ge(o_sq, h + 1)
                inv_root(oss[:, 0:2], 2, P, o_rs)
            for i in (1, 2):
                pool.wait_ge(xsq, i + 1)
                inv_root(nrm[:, 2 * i:2 * i + 2], 2, D, xrs)
                if i == 1:
                    zeros = mask[:, 0:P]
                    for buf, done in ((yh, m_yh), (yl, m_yl)):
                        g.tensor_copy(buf[:].rearrange("p (c n) -> p c n", c=KC),
                                      zeros.unsqueeze(1).to_broadcast([P, KC, P])).then_inc(done, 1)
                    g.tensor_copy(pT[:].rearrange("p (t n) -> p t n", t=T),
                                  zeros.unsqueeze(1).to_broadcast([P, T, P])).then_inc(m_pt, 1)

        @block.scalar
        def _(act):
            e = nc.scalar
            st = Steps(act, act_step)

            def split_hi(i, b=0):
                act.wait_ge(raw_in[i % NRAW], b * (32 * PER_BLOCK // NRAW) + 32 * (i // NRAW + 1))
                if i >= NSPL:
                    act.wait_ge(piece_used, b * PER_BLOCK + (i - NSPL + 1))
                e.activation(whi[:, i % NSPL, :], raw[:, i % NRAW, :], ACT.Copy).then_inc(hi_done, 1)

            bg = a["b_gate"][0].rearrange("(r n) -> r n", n=P)
            for r0, src in ((C_BG, bg),
                            (C_LR, a["ssm_lam_re"][0].rearrange("(j g) s -> j (g s)", g=2)),
                            (C_LI, a["ssm_lam_im"][0].rearrange("(j g) s -> j (g s)", g=2)),
                            (C_BGLU, a["b_glu"][0].rearrange("(r n) -> r n", n=P)),
                            (C_D, a["ssm_d"][0].rearrange("(r g) h -> r (g h)", g=8)),
                            (C_SUB, a["subln_g"]),
                            (C_QG, a["q_norm_g"].rearrange("o m d -> o (m d)")),
                            (C_KG, a["k_norm_g"].rearrange("o m d -> o (m d)")),
                            (C_KG + 1, bg[0:C_LS - C_KG - 1])):
                act.dma_start(smt[r0:r0 + src.shape[0], :], src).then_inc(small_in, 16)
            act.dma_start(lst[64:80, :], a["ssm_log_step"][0].rearrange("(j g) -> j g", g=2)).then_inc(small_in, 16)
            act.dma_start(gains[:, 0, :], a["attn_norm_g"][0].rearrange("(p c) -> p c", c=KC)).then_inc(vec_in, 16)
            act.dma_start(lamq[:], a["lam_qk"].rearrange("o m d -> o (m d)")).then_inc(vec_in, 16)

            def square_sums(dst, src, k, done):
                for t in range(T):
                    ins = e.activation(dst[:, t], src[:, t], ACT.Square, accum_out=nrm[:, k + t:k + t + 1])
                ins.then_inc(done, 1)
            act.wait_ge(x_in, 32)
            square_sums(xn, xin, 0, xsq)
            split_hi(0)
            act.wait_ge(small_pe, 1)
            e.activation(col[:], ov[:, 0:80], ACT.Copy).then_inc(col_done, 1)
            act.wait_ge(col_done, 1)
            e.activation(subg[:], col[:, C_SUB:C_SUB + 1], ACT.Copy, scale=1.0 - LAM_INIT)
            e.activation(ss[:, 0, :], col[:, C_LS:C_LS + 16], ACT.Exp).then_inc(dt_done, 1)
            act.wait_ge(lam_row, 1)
            e.activation(lams[0:1, 2:4], lams[0:1, 0:2], ACT.Exp).then_inc(lam_exp, 1)
            act.wait_ge(vec_in, 32)

            def chunks_hi(filled, banks, gain):
                for k, bank in enumerate(banks):
                    act.wait_ge(filled, k + 1)
                    for q in range(2):
                        c = 2 * k + q
                        e.activation(ah[:, c, :], bank[:, q * S:q * S + S], ACT.Copy,
                                     scale=gains[:, gain, c:c + 1]).then_inc(ah_done, 1)
            chunks_hi(xt_pe, xt_banks0, 0)
            split_hi(1)
            act.wait_ge(th_done, 1)
            e.activation(ss[:, 3, :], ss[:, 1, :], ACT.Exp)
            e.activation(ss[:, 5, :], ss[:, 4, :], ACT.Sin)
            e.activation(ss[:, 7, :], ss[:, 6, :], ACT.Sin).then_inc(trig, 1)
            act.wait_ge(pt_pe, 1)
            e.activation(pth[:], tp[:].rearrange("p (c s) -> p c s", c=2), ACT.Copy).then_inc(pth_done, 1)

            def u_evac():
                full(act, G_U)
                e.activation(uT[:].rearrange("p k s -> p (k s)"), pj[:, G_U % 2, :], ACT.Copy)\
                    .then_inc(pj_read[G_U % 2], 1)

            def qk_squares(i):
                full(act, G_Q + i)
                if i:
                    act.wait_ge(ssq_done, i)
                else:
                    act.wait_ge(bm_done, 1)
                e.activation(qsq[:].rearrange("p t n -> p (t n)"), pj[:, (G_Q + i) % 2, :], ACT.Square)\
                    .then_inc(qsq_done, 1)

            def qk_norm(i):
                act.wait_ge(qk_rs, i + 1)
                if i:
                    act.wait_ge(qt_pe, 2 * i)
                src, dst = pj[:, (G_Q + i) % 2, :], qn[:].rearrange("p t n -> p (t n)")
                for q in range(16):
                    ins = e.activation(dst[:, DH * q:DH * q + DH], src[:, DH * q:DH * q + DH], ACT.Copy,
                                       scale=nrm[:, 16 + q:17 + q])
                ins.then_inc(pj_read[(G_Q + i) % 2], 1)

            def qt_evac(i, half):
                act.wait_ge(qt_pe, 2 * i + half + 1)
                h0 = 4 * (i % 2) + 2 * half
                gc = C_QG if i < 2 else C_KG
                e.activation((qT if i < 2 else kT)[:, h0:h0 + 2, :].rearrange("p h s -> p (h s)"), tp[:], ACT.Copy,
                             scale=col[:, gc:gc + 1]).then_inc(qt_done, 1)

            def v_evac(i):
                G = G_V + i
                full(act, G)
                e.activation(v[:, :, 512 * i:512 * i + 512], pj[:, G % 2, :].rearrange("p (t n) -> p t n", t=2),
                             ACT.Copy).then_inc(pj_read[G % 2], 1)

            def g_evac(i):
                G = G_G[i]
                full(act, G)
                for b in range(4):
                    ins = e.activation(gT[:, 4 * i + b, :], pj[:, G % 2, b * S:b * S + S], ACT.Identity,
                                       bias=col[:, C_BG + 4 * i + b:C_BG + 4 * i + b + 1])
                ins.then_inc(pj_read[G % 2], 1)

            split_hi(2)
            split_hi(3)
            u_evac()
            split_hi(4)
            for n in range(P_QKV, P_G):
                split_hi(n + AHEAD)
                if n == P_QKV + 1:
                    act.wait_ge(b_pe, 1)
                    for r in range(2):
                        e.activation(bT[:, r], sc[:, r, :].rearrange("p (k n) -> p k n", k=4), ACT.Copy)\
                            .then_inc(bT_done, 1)
                i = (n - P_QKV) // 2
                if n % 2 == 1:
                    if 1 <= i <= 4:
                        qk_norm(i - 1)
                    qk_squares(i) if i < 4 else v_evac(i - 4)
                for k in (2 * (n - P_QKV), 2 * (n - P_QKV) + 1):
                    if k in QT_AT:
                        qt_evac(*QT_AT[k])

            for j in range(HEADS + 3):
                if j < HEADS + 2:
                    split_hi(P_G + j + AHEAD)
                if j >= 3:
                    act.wait_ge(ot_pe, j - 2)
                    e.activation(oh[:, j - 3, :], tp[:, 0:S], ACT.Copy, scale=subg[:, 0:1]).then_inc(oh_done, 1)
                if j in (3, HEADS):
                    act.wait_ge(z_done, 1 if j == 3 else 2)
                    e.activation(zh[:], y[:], ACT.Copy).then_inc(z_hi, 1)
                if 1 <= j <= HEADS:
                    act.wait_ge(wt_pe, j)
                    e.activation(wT[:], tp[:, 0:384], ACT.Copy).then_inc(wt_done, 1)
                if j < HEADS:
                    act.wait_ge(max_done, j + 1)
                    for m in range(2):
                        for qb, (k0, k1) in enumerate(((0, P), (P, 3 * P))):
                            i = 2 * m + qb
                            ins = e.activation(ee[:, m, k0:k1], sm[:, m, k0:k1], ACT.Exp, scale=SCALE,
                                               bias=att[:, 4 + i:5 + i], accum_out=att[:, 8 + i:9 + i])
                    ins.then_inc(e_done, 1)
                if j in (1, 3, 5, 8):
                    g_evac(j // 2 if j < 8 else 3)
                if j == 2:
                    act.wait_ge(gelu_in, 1)
                    e.activation(tt[:], tt[:], ACT.Sigmoid, scale=GELU_C).then_inc(gelu_sig, 1)
                if 1 <= j <= HEADS:
                    act.wait_ge(o_full, j)
                    if j >= 2:
                        act.wait_ge(o_done, j - 1)
                    for qb in range(2):
                        ins = e.activation(osq[:, qb], ov[:, qb * P:qb * P + P], ACT.Square, accum_out=oss[:, qb:qb + 1])
                    ins.then_inc(o_sq, 1)
                if j == HEADS:
                    act.wait_ge(pj_read[G_G[3] % 2], read_count(G_G[3]))
                    e.activation(gT[:, 8:16], gT[:, 8:16], ACT.Sigmoid).then_inc(g_sig, 1)
                    e.activation(gT[:, 0:8], gT[:, 0:8], ACT.Sigmoid).then_inc(g_sig, 1)
                if j == HEADS - 1:
                    full(act, G_GLU)
                    for b in range(4):
                        ins = e.activation(f8[:, b, :], pj[:, G_GLU % 2, b * S:b * S + S], ACT.Sigmoid,
                                           bias=col[:, C_BGLU + b:C_BGLU + b + 1])
                    ins.then_inc(pj_read[G_GLU % 2], 1)
            for n in range(P_UP + 1, N_PRE):
                split_hi(n + AHEAD)
                if n in (P_AT + 2, P_WO):
                    i = 0 if n < P_WO else 1
                    act.wait_ge(mix_done, i + 1)
                    e.activation(ah[:, 4 * i:4 * i + 4, :], gT[:, 4 * i:4 * i + 4, :], ACT.Copy).then_inc(ah_done, 1)

            act.wait_ge(pj_read[0], read_count(G_WO))
            act.wait_ge(pj_read[1], read_count(G_WO + 1))
            square_sums(xn2, x1, 2, xsq)
            for k in (2, 3):
                act.wait_ge(xt_pe, 4 + k + 1)
                e.activation(f8[:, 2 * k:2 * k + 2].rearrange("p c s -> p (c s)"), xt_banks[k], ACT.Copy)\
                    .then_inc(f8_done, 1)
            e.activation(xnh[:], x1[:], ACT.Copy).then_inc(xnh_done, 1)
            act.wait_ge(ple_pe, 1)
            e.activation(pp[:, 1, :], pj[:, (G_PLE + 1) % 2, :], ACT.Copy).then_inc(pj_read[(G_PLE + 1) % 2], 1)
            act.wait_ge(lg_in, 1)
            e.activation(rt[:, :, 48:52], rt[:, :, 44:48], ACT.Exp).then_inc(lg_exp, 1)
            act.wait_ge(lg_in, 2)
            e.activation(rt[:, :, 90:91], rt[:, :, 89:90], ACT.Exp).then_inc(lg_exp, 1)

            full(act, G_PLE)
            e.activation(pp[:, 0, :], pj[:, G_PLE % 2, :], ACT.Copy).then_inc(pj_read[G_PLE % 2], 1)

            def tokens_hi():
                e.activation(hgh[:], hgf, ACT.Copy).then_inc(m_hgh, 1)
            act.wait_ge(m_hgf, 1)
            tokens_hi()
            act.wait_ge(plan_done, 1)
            nb = act.value_load(plan[0:1, 0:1], min_val=NG, max_val=NG + 1)
            with act.Fori(0, nb) as b:
                def act_hi(x):
                    act.wait_ge(m_tp, b * NE + (x + 1))
                    e.activation(ach[:, x % 2], tp[:, 0:FF].rearrange("p (r n) -> p r n", r=2), ACT.Copy).then_inc(m_ach, 1)
                for i, (kind, x, h) in enumerate(MOE):
                    if kind == "g" and h == 1 and x >= 1:
                        act_hi(x - 1)
                    split_hi(N_PRE + i + AHEAD, b)
                    if i == 4:
                        act.wait_ge(m_ptp, b + 1)
                        act.wait_ge(m_sc, (b + 1) * T)
                        e.activation(pT[:], ov[:, 0:S], ACT.Copy).then_inc(m_pt, 1)
                    if kind == "g" and h == 1:
                        act.wait_ge(piece_used, b * PER_BLOCK + (N_PRE + i + 1))
                        if x == 0:
                            act.wait_ge(m_wc, b + 1)
                        e.activation(sg[:], pj[:, 0, 512 * (x % 2):512 * (x % 2) + FF], ACT.Sigmoid,
                                     scale=wc[:, NE:NE + 1])\
                            .then_inc(m_sig, 1)
                    if kind == "d" and x == NE - 2:
                        act_hi(NE - 1)
                        act.wait_ge(m_hgf, b + 2)
                        tokens_hi()
                act.wait_ge(piece_used, b * PER_BLOCK + (N_PRE + PER_BLOCK))
                e.activation(yh[:], sc[:].rearrange("p a n -> p (a n)"), ACT.Copy).then_inc(m_yh, 1)

            act.wait_ge(router_in, 16 * 9)
            act.wait_ge(m_add, (nb + 1) * T)
            chunks_hi(xt3, xt_banks, 2)
            split_hi(N_PRE + 3, nb)
            square_sums(xn2, x1, 4, xsq)
            act.wait_ge(xrs, 3)
            for i in range(2):
                act.wait_ge(piece_used, nb * PER_BLOCK + (N_PRE + 2 * i + 2))
                for t in range(T):
                    ins = e.activation(f8[:, 4 * i + 2 * t:4 * i + 2 * t + 2].rearrange("p c s -> p (c s)"),
                                       pj[:, i, 512 * t:512 * t + 512], ACT.Sigmoid, scale=nrm[:, 4 + t:5 + t])
                ins.then_inc(pl_sig, 1)

        @block.vector
        def _(dve):
            w = nc.vector
            st = Steps(dve, dve_step)

            def split_lo(i, b=0):
                dve.wait_ge(hi_done, b * PER_BLOCK + (i + 1))
                w.tensor_tensor(wlo[:, i % NRAW, :], raw[:, i % NRAW, :], whi[:, i % NSPL, :].bitcast(F32),
                                ALU.subtract).then_inc(lo_done, 1)
            dve.wait_ge(small_in, 160)
            w.tensor_copy(smt[64:80, :].rearrange("p (g s) -> p g s", g=2),
                          lst[64:80, :].unsqueeze(2).to_broadcast([16, 2, NST])).then_inc(ls_done, 1)
            dve.wait_ge(vec_in, 32)
            lq = lamq[:].rearrange("o (a b d) -> o a b d", a=2, b=2)
            lp = lamp[:].rearrange("o (a d) -> o a d", a=2)
            st.do(w.tensor_tensor(lp, lq[:, :, 0], lq[:, :, 1], ALU.mult))
            w.reduce_sum(lams[0:1, 0:2], lp, AX).then_inc(lam_row, 1)

            dve.wait_ge(xrs, 1)
            for t in range(T):
                ins = w.tensor_scalar(xn[:, t], xin[:, t], nrm[:, t:t + 1], None, ALU.mult)
            ins.then_inc(xnd, 1)
            split_lo(0)
            dve.wait_ge(lam_exp, 1)
            st.do(w.tensor_tensor(lams[0:1, 0:1], lams[0:1, 2:3], lams[0:1, 3:4], ALU.subtract))
            w.tensor_scalar(lams[0:1, 0:1], lams[0:1, 0:1], LAM_INIT, None, ALU.add).then_inc(lam_sum, 1)

            def chunks_lo(base, banks, gain, done):
                for k, bank in enumerate(banks):
                    dve.wait_ge(ah_done, base + 2 * k + 2)
                    for q in range(2):
                        c = 2 * k + q
                        ins = w.scalar_tensor_tensor(
                            out=al[:, c, :], in0=bank[:, q * S:q * S + S], scalar=gains[:, gain, c:c + 1],
                            in1=ah[:, c, :].bitcast(F32), op0=ALU.mult, op1=ALU.subtract)
                    if k % 2:
                        ins.then_inc(done[k // 2], 1)
            chunks_lo(0, xt_banks0, 0, pj_read)
            split_lo(1)

            def V(i):
                return ss[:, i, :]

            def tt_(o, x, z, op):
                return w.tensor_tensor(o, x, z, op)
            dve.wait_ge(dt_done, 1)
            lr, li = col[:, C_LR:C_LR + 16], col[:, C_LI:C_LI + 16]
            st.add(tt_(V(1), lr, V(0), ALU.mult))
            st.do(tt_(V(2), li, V(0), ALU.mult))
            st.do(w.tensor_scalar(V(8), V(2), 1.0 / (2 * math.pi), None, ALU.mult))
            st.do(w.tensor_scalar(V(8), V(8), ROUND, None, ALU.add))
            st.do(w.tensor_scalar(V(8), V(8), -ROUND, None, ALU.add))
            for part in (PI2_HI, PI2_MID, PI2_LO):
                st.do(w.scalar_tensor_tensor(out=V(2), in0=V(8), scalar=-part, in1=V(2), op0=ALU.mult, op1=ALU.add))
            st.do(w.tensor_scalar(V(4), V(2), 3.1415925, -3.1415925, ALU.min, ALU.max))
            st.do(w.tensor_scalar(V(6), V(4), -1.0, None, ALU.mult))
            st.do(tt_(V(6), V(6), V(4), ALU.max))
            w.tensor_scalar(V(6), V(6), -1.0, math.pi / 2, ALU.mult, ALU.add).then_inc(th_done, 1)
            split_lo(2)
            st.add(tt_(V(8), lr, lr, ALU.mult))
            st.do(tt_(V(9), li, li, ALU.mult))
            st.do(tt_(V(8), V(8), V(9), ALU.add))
            st.do(w.reciprocal(V(8), V(8)))
            dve.wait_ge(trig, 1)
            w.memset(ptab[:, 0, :, 0:1], 1.0).then_inc(re_done, 1)
            st.add(w.tensor_copy(pw[:, 0, 0, :], V(7)))
            st.do(w.tensor_copy(pw[:, 1, 0, :], V(5)))
            for i in range(LEVELS):
                c, s = pw[:, 0, i, :], pw[:, 1, i, :]
                st.add(tt_(V(18), c, c, ALU.mult))
                st.add(tt_(V(19), s, s, ALU.mult))
                st.do(tt_(V(20), c, s, ALU.mult))
                st.add(tt_(pw[:, 0, i + 1, :], V(18), V(19), ALU.subtract))
                ins = w.tensor_scalar(pw[:, 1, i + 1, :], V(20), 2.0, None, ALU.mult)
                st.do(ins)
            w.tensor_copy(ini[:, 0:1], pw[:, 1, LEVELS, 0:1]).then_inc(pow_done, 1)
            split_lo(3)
            st.add(tt_(V(10), V(3), V(7), ALU.mult))
            st.do(tt_(V(11), V(3), V(5), ALU.mult))
            st.do(w.tensor_scalar(V(10), V(10), -1.0, None, ALU.add))
            st.add(tt_(V(12), V(10), lr, ALU.mult))
            st.add(tt_(V(13), V(11), li, ALU.mult))
            st.add(tt_(V(14), V(11), lr, ALU.mult))
            st.do(tt_(V(15), V(10), li, ALU.mult))
            st.add(tt_(V(12), V(12), V(13), ALU.add))
            st.do(tt_(V(14), V(14), V(15), ALU.subtract))
            st.add(tt_(V(12), V(12), V(8), ALU.mult))
            st.do(tt_(V(14), V(14), V(8), ALU.mult))

            dve.wait_ge(bc_in, 96)
            dve.wait_ge(consts, 8)

            def spread(col_):
                return col_.unsqueeze(2).to_broadcast([P, ST, SH])
            st.add(tt_(bst[:, 2], bst[:, 0], spread(V(12)), ALU.mult))
            st.add(tt_(bm[:, 0, :, 0, :], bst[:, 1], spread(V(14)), ALU.mult))
            st.add(tt_(bst[:, 3], bst[:, 1], spread(V(12)), ALU.mult))
            st.do(tt_(bm[:, 0, :, 1, :], bst[:, 0], spread(V(14)), ALU.mult))
            st.add(tt_(bst[:, 2], bst[:, 2], bm[:, 0, :, 0, :], ALU.subtract))
            st.do(tt_(bst[:, 3], bst[:, 3], bm[:, 0, :, 1, :], ALU.add))
            for r in range(2):
                for gl in range(2):
                    ins = w.tensor_scalar(bm[:, r, :, gl, :], bst[:, 2 + r], mk[:, gl:gl + 1], None, ALU.mult)
            ins.then_inc(bm_done, 1)
            dve.wait_ge(pth_done, 1)
            tt_(ptl[:], tp[:].rearrange("p (c s) -> p c s", c=2), pth[:].bitcast(F32), ALU.subtract)\
                .then_inc(ptl_done, 1)

            def head_sums(i):
                dve.wait_ge(qsq_done, i + 1)
                if i:
                    dve.wait_ge(pj_read[(G_Q + i - 1) % 2], read_count(G_Q + i - 1))
                w.reduce_sum(nrm[:, 16:32], qsq[:].rearrange("p t (s d) -> p (t s) d", d=DH), AX)\
                    .then_inc(ssq_done, 1)
            for i in range(LEVELS):
                if i == LEVELS - 1:
                    head_sums(0)
                L, c_, s_, re, im, new = level(i, 0)
                t1 = tt[:].rearrange("p a n -> p (a n)")[:, 0:ST * L].rearrange("p (j l) -> p j l", j=ST)
                dve.wait_ge(im_done, i + 1)
                st.add(tt_(new, re, c_, ALU.mult))
                st.do(tt_(t1, im, s_, ALU.mult))
                tt_(new, new, t1, ALU.subtract).then_inc(re_done, 1)
                dve.wait_ge(re_done, i + 2)
                if i >= 3:
                    split_lo(P_QKV + i - 1)
            dve.wait_ge(im_done, LEVELS + 1)

            dve.wait_ge(c_pe, 1)
            for r, bank in enumerate((ov, tp)):
                src = bank[:].rearrange("p (j g h) -> p j g h", j=ST, g=2)
                dst = cm[:, r].rearrange("p j (g h) -> p j g h", g=2)
                for gl in range(2):
                    ins = w.tensor_scalar(dst[:, :, gl, :], src[:, :, gl, :], mk[:, 2 * r + gl:2 * r + gl + 1],
                                          None, ALU.mult)
            ins.then_inc(cm_done, 1)
            dve.wait_ge(lam_pe, 1)
            w.tensor_copy(lam[:], sc[:, 1, 0:1]).then_inc(lam_done, 1)

            def scan_tile(j):
                b = j % 2
                dve.wait_ge(bu_full, j + 1)
                if j >= 2:
                    dve.wait_ge(rot_done, j - 1)
                c, s = (ptab[:, i, j, :].unsqueeze(1).to_broadcast([P, 4, HALF]) for i in range(2))
                bank = sc[:, b, :].rearrange("p (a t) -> p a t", a=4)
                t1, t2 = tt[:, 0, :], tt[:, 1, :]
                w.tensor_tensor(t1.rearrange("p (a t) -> p a t", a=4), bank, c, ALU.mult)
                w.tensor_tensor(t2.rearrange("p (a t) -> p a t", a=4), bank, s, ALU.mult).then_inc(bu_read, 1)
                dve.wait_ge(bu_read, j + 1)
                st.add(tt_(t1[:, 0:256], t1[:, 0:256], t2[:, 256:512], ALU.add))
                st.do(tt_(t1[:, 256:512], t1[:, 256:512], t2[:, 0:256], ALU.subtract))
                mag = ss[:, 3, j:j + 1].to_broadcast([P, HALF])
                r = rr[:, b, :]
                for k in (0, 256):
                    ins = st.add(w.tensor_tensor_scan(r[:, k:k + HALF], mag, t1[:, k:k + HALF], 0.0, ALU.mult, ALU.add))
                st.wait()
                c1, s1 = pw[:, 0, LEVELS, j:j + 1], pw[:, 1, LEVELS, j:j + 1]
                re, im = r[:, HALF - 1:HALF], r[:, 256 + HALF - 1:256 + HALF]
                st.add(tt_(ini[:, 0:1], im, s1, ALU.mult))
                st.do(tt_(ini[:, 1:2], re, s1, ALU.mult))
                st.add(w.scalar_tensor_tensor(out=ini[:, 2:3], in0=re, scalar=c1, in1=ini[:, 0:1],
                                              op0=ALU.mult, op1=ALU.subtract))
                st.do(w.scalar_tensor_tensor(out=ini[:, 3:4], in0=im, scalar=c1, in1=ini[:, 1:2],
                                             op0=ALU.mult, op1=ALU.add))
                for n, k in enumerate((0, 256)):
                    ins = w.tensor_tensor_scan(r[:, k + HALF:k + 2 * HALF], mag, t1[:, k + HALF:k + 2 * HALF],
                                               ini[:, 2 + n:3 + n], ALU.mult, ALU.add)
                ins.then_inc(scan_done, 1)
                dve.wait_ge(scan_done, j + 1)

            def y_evac(c):
                dve.wait_ge(y_pe, 4 * c + 4)
                dve.wait_ge(pj_read[G_U % 2], read_count(G_U))
                w.scalar_tensor_tensor(out=y[:, c, :], in0=uT[:, c, :], scalar=col[:, C_D + c:C_D + c + 1],
                                       in1=ov[:, 0:S], op0=ALU.mult, op1=ALU.add).then_inc(y_read, 1)

            for k in range(5, max(YT_AT) + 1):
                if k in QN_AT:
                    head_sums(QN_AT[k])
                if k in TILE_AT:
                    scan_tile(TILE_AT[k])
                if YT_AT.get(k, 0) % 4 == 3:
                    y_evac(YT_AT[k] // 4)
                if k % 2 == 0 and 6 <= k < HALF_PIECES:
                    split_lo(P_QKV + k // 2 + AHEAD)

            yf, tf = y[:].rearrange("p k s -> p (k s)"), tt[:].rearrange("p a n -> p (a n)")

            def gelu_argument():
                dve.wait_ge(y_read, 4)
                st.do(tt_(tf, yf, yf, ALU.mult))
                st.do(w.tensor_scalar(tf, tf, 0.044715, 1.0, ALU.mult, ALU.add))
                tt_(tf, tf, yf, ALU.mult).then_inc(gelu_in, 1)

            def gelu_product():
                dve.wait_ge(gelu_sig, 1)
                tt_(yf, yf, tf, ALU.mult).then_inc(z_done, 1)

            for j in range(HEADS + 3):
                if j >= 3:
                    dve.wait_ge(oh_done, j - 2)
                    w.scalar_tensor_tensor(out=ol[:, j - 3, :], in0=tp[:, 0:S], scalar=subg[:, 0:1],
                                           in1=oh[:, j - 3, :].bitcast(F32), op0=ALU.mult, op1=ALU.subtract)\
                        .then_inc(ol_done, 1)
                if j == 3:
                    gelu_product()
                if j == HEADS:
                    dve.wait_ge(pj_read[G_GLU % 2], read_count(G_GLU))
                    tt_(y[:], y[:], f8[:, 0:4, :], ALU.mult).then_inc(z_done, 1)
                if j < HEADS:
                    dve.wait_ge(s_full, j + 1)
                    for m in range(2):
                        for qb, (k0, k1) in enumerate(((0, P), (P, 3 * P))):
                            ins = st.add(w.tensor_tensor_reduce(
                                out=sm[:, m, k0:k1], in0=sc[:, m, k0:k1], in1=mask[:, 2 * P - (k1 - k0):2 * P],
                                scale=1.0, scalar=-3e38, op0=ALU.add, op1=ALU.max,
                                accum_out=att[:, 2 * m + qb:2 * m + qb + 1]))
                    st.wait()
                    w.tensor_scalar(att[:, 4:8], att[:, 0:4], -SCALE, None, ALU.mult).then_inc(max_done, 1)
                if j < HEADS + 2:
                    split_lo(P_G + j + AHEAD)
                if j < HEADS:
                    dve.wait_ge(e_done, j + 1)
                    if j == 0:
                        dve.wait_ge(lam_done, 1)
                    st.do(w.reciprocal(att[:, 12:16], att[:, 8:12]))
                    st.do(w.tensor_scalar(att[:, 16:18], att[:, 14:16], lam[:, 0:1], -1.0, ALU.mult, ALU.mult))
                    if j:
                        dve.wait_ge(wt_pe, j)
                    for qb, (k0, k1) in enumerate(((0, P), (P, 3 * P))):
                        st.add(w.tensor_scalar(ww[:, k0:k1], ee[:, 0, k0:k1], att[:, 12 + qb:13 + qb], None, ALU.mult))
                    st.wait()
                    for qb, (k0, k1) in enumerate(((0, P), (P, 3 * P))):
                        ins = w.scalar_tensor_tensor(out=ww[:, k0:k1], in0=ee[:, 1, k0:k1],
                                                     scalar=att[:, 16 + qb:17 + qb], in1=ww[:, k0:k1],
                                                     op0=ALU.mult, op1=ALU.add)
                    ins.then_inc(w_done, 1)
                if 1 <= j <= HEADS:
                    dve.wait_ge(o_rs, j)
                    if j >= 2:
                        dve.wait_ge(ot_pe, j - 1)
                    for qb in range(2):
                        ins = w.tensor_scalar(on[:, qb, :], ov[:, qb * P:qb * P + P], oss[:, qb:qb + 1], None, ALU.mult)
                    ins.then_inc(o_done, 1)
                if j == 1:
                    gelu_argument()
                if j in (4, HEADS):
                    dve.wait_ge(z_hi, 1 if j == 4 else 2)
                    tt_(zl[:], y[:], zh[:].bitcast(F32), ALU.subtract).then_inc(z_lo, 1)

            def pair(i, G):
                full(dve, G)
                return pj[:, G % 2, :].rearrange("p (c s) -> p c s", c=4)
            for n in range(P_UP + 1, N_PRE):
                if n == P_PLE:
                    dve.wait_ge(xres_in, 16)
                    for i in range(2):
                        G = G_WO + i
                        full(dve, G)
                        xs = x1[:, :, 512 * i:512 * i + 512]
                        tt_(xs, xs, pj[:, G % 2, :].rearrange("p (t n) -> p t n", t=T), ALU.add)\
                            .then_inc(pj_read[G % 2], 1)
                split_lo(n + AHEAD)
                if n in (P_UP + 1, P_UP + 2):
                    i = n - P_UP - 1
                    dve.wait_ge(g_sig, 2)
                    tt_(gT[:, 8 + 4 * i:12 + 4 * i], gT[:, 8 + 4 * i:12 + 4 * i], pair(i, G_UP + i), ALU.mult)\
                        .then_inc(pj_read[(G_UP + i) % 2], 1)
                if n in (P_AT + 2, P_WO):
                    i = 0 if n < P_WO else 1
                    tt_(gT[:, 4 * i:4 * i + 4], gT[:, 4 * i:4 * i + 4], pair(i, G_AT + i), ALU.mult)\
                        .then_inc(pj_read[(G_AT + i) % 2], 1)
                    dve.wait_ge(pj_read[(G_AT + i) % 2], read_count(G_AT + i))
                    dve.wait_ge(pj_read[(G_UP + i) % 2], read_count(G_UP + i))
                    tt_(gT[:, 4 * i:4 * i + 4], gT[:, 4 * i:4 * i + 4], gT[:, 8 + 4 * i:12 + 4 * i], ALU.add)\
                        .then_inc(mix_done, 1)
                    dve.wait_ge(ah_done, 9 + i)
                    tt_(al[:, 4 * i:4 * i + 4], gT[:, 4 * i:4 * i + 4], ah[:, 4 * i:4 * i + 4].bitcast(F32),
                        ALU.subtract).then_inc(al_done, 1)
                if n == P_WO:
                    dve.wait_ge(router_in, 16 * 9)
                    tt_(wr[:], wr[:], gains[:, 1, :].unsqueeze(2).to_broadcast([P, KC, 36]), ALU.mult)\
                        .then_inc(wr_done, 1)

            for k in range(2):
                dve.wait_ge(xt_pe, 4 + k + 1)
                w.tensor_copy(f8[:, 2 * k:2 * k + 2].rearrange("p c s -> p (c s)"), xt_banks[k]).then_inc(f8_done, 1)
            dve.wait_ge(xnh_done, 1)
            tt_(xnl[:], x1[:], xnh[:].bitcast(F32), ALU.subtract).then_inc(xnl_done, 1)
            dve.wait_ge(lg_pe, 1)
            dve.wait_ge(xrs, 2)

            def R(k0, k1):
                return rt[:, :, k0:k1]

            def wide(k, n):
                return rt[:, :, k:k + 1].to_broadcast([P, T, n])
            logits = ov[:, 0:128].rearrange("p (t n) -> p t n", t=T)[:, :, 0:36]
            for t in range(T):
                st.add(w.scalar_tensor_tensor(out=rt[:, t, 0:36], in0=logits[:, t, :], scalar=nrm[:, 2 + t:3 + t],
                                              in1=wrb[:], op0=ALU.mult, op1=ALU.add))
            st.wait()
            st.add(w.tensor_scalar(desc[:], iota[:, 0:NE], -1.0, float(NE), ALU.mult, ALU.add))
            st.do(w.reduce_max(R(36, 37), R(0, 4), AX))

            def first_max(vals, k_max, n, dst):
                st.do(tt_(dst, vals, wide(k_max, n), ALU.is_equal))
                st.do(tt_(dst, dst, desc[:, 0:n].unsqueeze(1).to_broadcast([P, T, n]), ALU.mult))
                st.do(w.reduce_max(R(37, 38), dst, AX))
                return tt_(dst, dst, wide(37, n), ALU.is_equal)
            tt_(R(44, 48), R(0, 4), wide(36, 4), ALU.subtract).then_inc(lg_in, 1)
            first_max(R(0, 4), 36, NG, R(56, 60)).then_inc(grp_done, 1)
            dve.wait_ge(grp_done, 1)
            le = R(4, 36).rearrange("p t (n e) -> p t n e", n=NG)
            prod = R(96, 128).rearrange("p t (n e) -> p t n e", n=NG)
            st.do(tt_(prod, le, R(56, 60).unsqueeze(3).to_broadcast([P, T, NG, NE]), ALU.mult))
            st.do(w.reduce_sum(R(60, 68), prod.rearrange("p t n e -> p t e n"), AX))
            st.do(w.reduce_max(R(68, 69), R(60, 68), AX))
            st.do(first_max(R(60, 68), 68, NE, R(72, 80)))
            st.do(w.scalar_tensor_tensor(out=R(60, 68), in0=R(72, 80), scalar=NEG, in1=R(60, 68),
                                         op0=ALU.mult, op1=ALU.add))
            st.do(w.reduce_max(R(69, 70), R(60, 68), AX))
            st.do(first_max(R(60, 68), 69, NE, R(80, 88)))
            tt_(R(89, 90), R(69, 70), R(68, 69), ALU.subtract).then_inc(lg_in, 1)

            dve.wait_ge(rank_pe, 1)
            ranks = ov[:, 128:136].rearrange("p (t n) -> p t n", t=T)
            st.do(tt_(R(40, 44), ranks, R(56, 60), ALU.mult))
            st.add(w.tensor_scalar(cnt[:, 0:4], ov[:, 136:140], float(P), None, ALU.is_gt))
            st.do(w.reduce_sum(R(95, 96), R(40, 44), AX))
            st.add(w.tensor_copy(slotc[:, :, 0:NG], wide(95, NG)))
            st.add(w.tensor_copy(ohc[:, :, 0:NG], R(56, 60)))
            st.add(w.tensor_scalar(slotc[:, :, NG:NG + 1], R(95, 96), -float(P), None, ALU.add))
            st.add(w.tensor_scalar(ohc[:, :, NG:NG + 1], R(95, 96), float(P), None, ALU.is_ge))
            st.add(w.reduce_sum(cnt[:, 4:5], cnt[:, 0:4], AX))
            st.do(tt_(cnt[:, 0:4], cnt[:, 0:4], iota[:, 0:4], ALU.mult))
            st.add(w.tensor_scalar(cnt[:, 4:5], cnt[:, 4:5], float(NG), None, ALU.add))
            st.do(w.reduce_sum(cnt[:, 5:6], cnt[:, 0:4], AX))
            w.tensor_copy(plan[:], cnt[:, 4:6]).then_inc(plan_done, 1)

            def one_hot(b):
                for t in range(T):
                    ins = w.tensor_scalar(pm[:, t, :], iota[:], slotc[:, t, bass.ds(b, 1)], ohc[:, t, bass.ds(b, 1)],
                                          ALU.is_equal, ALU.mult)
                ins.then_inc(m_pm, 1)

            def tokens_scaled():
                tt_(hgf, pj[:, 1, :].rearrange("p (c s) -> p c s", c=KC),
                    gains[:, 1, :].unsqueeze(2).to_broadcast([P, KC, P]), ALU.mult).then_inc(m_hgf, 1)

            def tokens_lo():
                tt_(hgl[:], hgf, hgh[:].bitcast(F32), ALU.subtract).then_inc(m_hgl, 1)
            one_hot(0)
            dve.wait_ge(lg_exp, 2)
            st.do(w.reduce_sum(R(52, 53), R(48, 52), AX))
            st.add(w.reciprocal(R(53, 54), R(52, 53)))
            st.do(w.tensor_scalar(R(91, 92), R(90, 91), 1.0, None, ALU.add))
            st.do(w.reciprocal(R(92, 93), R(91, 92)))
            st.do(tt_(R(93, 94), R(92, 93), R(53, 54), ALU.mult))
            for t in range(T):
                r = nrm[:, 2 + t:3 + t]
                st.add(w.tensor_scalar(rt[:, t, 93:94], rt[:, t, 93:94], r, r, ALU.mult, ALU.mult))
            st.add(w.tensor_copy(wl8[:, :, NE:NE + 1], nrm[:, 2:4].unsqueeze(2)))
            st.wait()
            st.do(tt_(R(94, 95), R(93, 94), R(90, 91), ALU.mult))
            for t in range(T):
                st.add(w.tensor_scalar(wl8[:, t, 0:NE], rt[:, t, 72:80], rt[:, t, 93:94], None, ALU.mult))
            st.wait()
            for t in range(T):
                ins = w.scalar_tensor_tensor(out=wl8[:, t, 0:NE], in0=rt[:, t, 80:88], scalar=rt[:, t, 94:95],
                                             in1=wl8[:, t, 0:NE], op0=ALU.mult, op1=ALU.add)
            ins.then_inc(wl_done, 1)
            dve.wait_ge(m_gat, 1)
            tokens_scaled()
            dve.wait_ge(m_hgh, 1)
            tokens_lo()

            nb = dve.value_load(plan[0:1, 0:1], min_val=NG, max_val=NG + 1)
            with dve.Fori(0, nb) as b:
                def act_lo(x):
                    dve.wait_ge(m_ach, b * NE + (x + 1))
                    tt_(acl[:, x % 2], tp[:, 0:FF].rearrange("p (r n) -> p r n", r=2), ach[:, x % 2].bitcast(F32), ALU.subtract)\
                        .then_inc(m_acl, 1)

                def tokens_added(t, base, pair=1):
                    dve.wait_ge(m_sc, base + (t + 1))
                    tt_(x1[:, t, :], x1[:, t, :], pj[:, pair, :], ALU.add).then_inc(m_add, 1)
                for i, (kind, x, h) in enumerate(MOE):
                    if kind == "g" and h == 1 and x >= 1:
                        act_lo(x - 1)
                    if i in (2, 4):
                        tokens_added(i // 2 - 1, b * T)
                    split_lo(N_PRE + i + AHEAD, b)
                    if i == 0:
                        dve.wait_ge(m_ptp, b + 1)
                        w.tensor_copy(wc[:], tp[:, 400:400 + NE + 1]).then_inc(m_wc, 1)
                    if i == 12:
                        one_hot(b + 1)
                    if i == 18:
                        dve.wait_ge(m_gat, b + 2)
                        tokens_scaled()
                    if kind == "g" and h == 1:
                        if x == 0:
                            dve.wait_ge(m_wc, b + 1)
                        gu = pj[:, 0, 512 * (x % 2):512 * (x % 2) + 512]
                        dve.wait_ge(m_sig, b * NE + (x + 1))
                        w.scalar_tensor_tensor(out=a1[:], in0=gu[:, 0:FF], scalar=wc[:, x:x + 1], in1=sg[:],
                                               op0=ALU.mult, op1=ALU.mult).then_inc(moe_step, 1)
                        dve.wait_ge(moe_step, b * NE + (x + 1))
                        tt_(ac[:, x % 2, :], a1[:], gu[:, FF:2 * FF], ALU.mult).then_inc(m_act, 1)
                    if kind == "d" and x == NE - 2:
                        act_lo(NE - 1)
                        dve.wait_ge(m_hgh, b + 2)
                        tokens_lo()
                dve.wait_ge(m_yh, b + 2)
                tt_(yl[:], sc[:].rearrange("p a n -> p (a n)"), yh[:].bitcast(F32), ALU.subtract).then_inc(m_yl, 1)
            for t in range(T):
                tokens_added(t, nb * T, t)

            chunks_lo(10, xt_banks, 2, [al_done, al_done])
            split_lo(N_PRE + 3, nb)
            for i in range(2):
                dve.wait_ge(pl_sig, i + 1)
                sgm = f8[:, 4 * i:4 * i + 4].rearrange("p c s -> p (c s)").rearrange("p (t n) -> p t n", t=T)
                st.do(tt_(sgm, sgm, pp[:, :, 512 * i:512 * i + 512], ALU.mult))
                xs = x1[:, :, 512 * i:512 * i + 512]
                tt_(xs, xs, sgm, ALU.add).then_inc(o_ready, 1)

        @block.tensor
        def _(pe):
            m = nc.tensor

            def mm3(o, lh, ll, rh, rl, start, stop):
                m.matmul(o, lh, rh, start=start, stop=False, skip_group_check=True)
                m.matmul(o, lh, rl, start=False, stop=False, skip_group_check=True)
                return m.matmul(o, ll, rh, start=False, stop=stop, skip_group_check=True)

            def split(i):
                return [t.rearrange("p (c n) -> p c n", c=4) for t in parts(i)]

            def parts(i):
                return whi[:, i % NSPL, :], wlo[:, i % NRAW, :]

            def ready(i, b=0):
                pe.wait_ge(lo_done, b * PER_BLOCK + (i + 1))

            def pair_free(G):
                pe.wait_ge(pj_read[G % 2], read_count(G) - 1)

            def by_width(i, G, rhs, part, blocks, last):
                wh, wl = split(i)
                for blk in blocks:
                    o = pj[:, G % 2, blk * S:blk * S + S]
                    for c in range(4):
                        cg = 4 * part[0] + c
                        ins = mm3(o, wh[:, c, blk * P:blk * P + P], wl[:, c, blk * P:blk * P + P],
                                  rhs[0][:, cg, :], rhs[1][:, cg, :],
                                  start=(part[0] == 0 and c == 0 and blk % 2 == 0),
                                  stop=(part[0] == part[1] - 1 and c == 3))
                if last:
                    ins.then_inc(piece_used, 1)
                return ins

            def by_token(o, i, t, part, b=0):
                wh, wl = split(i)
                for c in range(4):
                    cg = 4 * part[0] + c
                    ins = mm3(o, ah[:, cg, t * P:t * P + P], al[:, cg, t * P:t * P + P], wh[:, c, :], wl[:, c, :],
                                start=(part[0] == 0 and c == 0), stop=(part[0] == part[1] - 1 and c == 3))
                return ins

            pe.wait_ge(consts, 8)
            pe.wait_ge(small_in, 160)
            pe.wait_ge(ls_done, 1)
            m.transpose(ov[:, 0:80], smt[:], ident[0:80, 0:80]).then_inc(small_pe, 1)

            def transposes(src, banks, done):
                for k, bank in enumerate(banks):
                    for q in range(2):
                        for t in range(T):
                            ins = m.transpose(bank[:, q * S + t * P:q * S + t * P + P], src[:, t, 2 * k + q::KC],
                                              ident[:])
                    ins.then_inc(done, 1)
            pe.wait_ge(xnd, 1)
            transposes(xn, xt_banks0, xt_pe)
            pe.wait_ge(p_in, 16)
            for c in range(2):
                for t in range(T):
                    ins = m.transpose(tp[:, c * S + t * P:c * S + t * P + P], pst[:, t, c::2], ident[:])
            ins.then_inc(pt_pe, 1)
            for h in range(2):
                ready(P_U + h)
                if h == 0:
                    pe.wait_ge(pj_read[0], 1)
                    pe.wait_ge(pj_read[1], 1)
                by_width(P_U + h, G_U, (ah, al), (h, 2), range(4), True)

            def b_and_c_transposed():
                pe.wait_ge(bm_done, 1)
                for r in range(2):
                    for k in range(4):
                        ins = m.transpose(sc[:, r, k * P:k * P + P],
                                          bm[:, r, 4 * k:4 * k + 4].rearrange("p j g h -> p (j g h)"), ident[:])
                ins.then_inc(b_pe, 1)
                pe.wait_ge(col_done, 1)
                pe.wait_ge(ptl_done, 1)
                for r, bank in enumerate((ov, tp)):
                    for k in range(4):
                        ins = m.transpose(bank[:, k * P:k * P + P], cst[:, r, k, :], ident[:])
                ins.then_inc(c_pe, 1)

            def lambda_spread():
                pe.wait_ge(lam_sum, 1)
                pe.wait_ge(bT_done, 2)
                m.matmul(sc[:, 1, 0:1], ones[0:1, :], lams[0:1, 0:1], start=True, stop=True).then_inc(lam_pe, 1)

            def state_inputs(j):
                b, q, k = j % 2, 32 * (j % 4), j // 4
                if j == 0:
                    pe.wait_ge(pj_read[G_U % 2], read_count(G_U))
                if j == 1:
                    pe.wait_ge(lam_done, 1)
                if j >= 2:
                    pe.wait_ge(bu_read, j - 1)
                for r in range(2):
                    ins = m.matmul(sc[:, b, r * S:r * S + S], bT[q:q + 32, r, k, :], uT[q:q + 32, k, :],
                                   start=True, stop=True)
                ins.then_inc(bu_full, 1)

            def state_outputs(j):
                b, q, k = j % 2, 32 * (j % 4), j // 4
                if j == 0:
                    pe.wait_ge(cm_done, 1)
                elif j % 4 == 0:
                    pe.wait_ge(y_read, k)
                pe.wait_ge(rot_done, j + 1)
                for r in range(2):
                    ins = m.matmul(ov[q:q + 32, 0:S], cm[:, r, j, :], so[:, b, r * S:r * S + S],
                                   start=(r == 0), stop=(r == 1), skip_group_check=True)
                ins.then_inc(y_pe, 1)

            def qk_transposes(i, half):
                pe.wait_ge(pj_read[(G_Q + i) % 2], read_count(G_Q + i))
                if 2 * i + half:
                    pe.wait_ge(qt_done, 2 * i + half)
                for q in range(2):
                    for t in range(T):
                        hd = (2 * half + q) * P
                        ins = m.transpose(tp[:, q * S + t * P:q * S + t * P + P], qn[:, t, hd:hd + P], ident[:])
                ins.then_inc(qt_pe, 1)

            for n in range(P_QKV, P_G):
                G = G_Q + (n - P_QKV) // 2
                part = ((n - P_QKV) % 2, 2)
                ready(n)
                if part[0] == 0:
                    pair_free(G)
                for t in range(T):
                    ins = by_token(pj[:, G % 2, 512 * t:512 * t + 512], n, t, part)
                    if t == T - 1:
                        ins.then_inc(piece_used, 1)
                    k = 2 * (n - P_QKV) + t
                    if k == 2:
                        b_and_c_transposed()
                    if k == 5:
                        lambda_spread()
                    if k in TILE_AT:
                        state_inputs(TILE_AT[k])
                    if k in YT_AT:
                        state_outputs(YT_AT[k])
                    if k in QT_AT:
                        qk_transposes(*QT_AT[k])
            state_outputs(ST - 1)

            def scores(h):
                if h == 0:
                    pe.wait_ge(qt_done, 8)
                    pe.wait_ge(bu_read, ST)
                else:
                    pe.wait_ge(max_done, h)
                for mp in range(2):
                    r = slice(DH * mp, DH * mp + DH)
                    m.matmul(sc[:, mp, 0:P], qT[r, h, 0:P], kT[r, h, 0:P], start=True, stop=True)
                    ins = m.matmul(sc[:, mp, P:3 * P], qT[r, h, P:S], kT[r, h, :], start=True, stop=True)
                ins.then_inc(s_full, 1)

            def weights_transposed(h):
                pe.wait_ge(w_done, h + 1)
                if h >= 2:
                    pe.wait_ge(ol_done, h - 1)
                for q in range(3):
                    ins = m.transpose(tp[:, q * P:q * P + P], ww[:, q * P:q * P + P], ident[:])
                ins.then_inc(wt_pe, 1)

            def values(h):
                pe.wait_ge(wt_done, h + 1)
                if h == 0:
                    pe.wait_ge(y_read, 4)
                    pe.wait_ge(pj_read[G_V % 2], read_count(G_V))
                    pe.wait_ge(pj_read[(G_V + 1) % 2], read_count(G_V + 1))
                else:
                    pe.wait_ge(o_done, h)
                e = slice(P * h, P * h + P)
                m.matmul(ov[:, 0:P], wT[:, 0:P], v[:, 0, e], start=True, stop=True)
                m.matmul(ov[:, P:2 * P], wT[:, P:2 * P], v[:, 0, e], start=True, stop=False)
                m.matmul(ov[:, P:2 * P], wT[:, 2 * P:3 * P], v[:, 1, e], start=False, stop=True).then_inc(o_full, 1)

            def outputs_transposed(h):
                pe.wait_ge(o_done, h + 1)
                if h == HEADS - 1:
                    pe.wait_ge(ol_done, h)
                for t in range(T):
                    ins = m.transpose(tp[:, t * P:t * P + P], on[:, t, :], ident[:])
                ins.then_inc(ot_pe, 1)

            for j in range(HEADS + 2):
                n = P_G + j
                ready(n)
                if n == P_GLU:
                    G, rhs, part = G_GLU, (zh, zl), (0, 1)
                    pe.wait_ge(z_lo, 1)
                elif n == P_UP:
                    G, rhs, part = G_UP, (zh, zl), (0, 1)
                    pe.wait_ge(z_lo, 2)
                else:
                    i = j - (n > P_GLU)
                    G, rhs, part = G_G[i // 2], (ah, al), (i % 2, 2)
                if part[0] == 0:
                    pair_free(G)
                by_width(n, G, rhs, part, (0, 1), False)
                if j < HEADS:
                    scores(j)
                if 1 <= j <= HEADS:
                    weights_transposed(j - 1)
                by_width(n, G, rhs, part, (2, 3), True)
                if 1 <= j <= HEADS:
                    values(j - 1)
                if j >= 2:
                    outputs_transposed(j - 2)

            ready(P_UP + 1)
            pair_free(G_UP + 1)
            by_width(P_UP + 1, G_UP + 1, (zh, zl), (0, 1), range(4), True)
            for n in range(P_AT, P_WO):
                G = G_AT + (n - P_AT) // 2
                ready(n)
                pair_free(G)
                pe.wait_ge(ol_done, HEADS)
                by_width(n, G, (oh, ol), ((n - P_AT) % 2, 2), range(4), True)
            for n in range(P_WO, P_PLE):
                G, h = G_WO + (n - P_WO) % 2, (n - P_WO) // 2
                ready(n)
                if h == 0:
                    pair_free(G)
                pe.wait_ge(al_done, h + 1)
                for t in range(T):
                    ins = by_token(pj[:, G % 2, 512 * t:512 * t + 512], n, t, (h, 2))
                ins.then_inc(piece_used, 1)

            for i in range(2):
                pe.wait_ge(pj_read[i], read_count(G_WO))
            transposes(x1, xt_banks, xt_pe)
            pe.wait_ge(f8_done, 4)
            pe.wait_ge(wr_done, 1)
            for t in range(T):
                for c in range(KC):
                    ins = m.matmul(ov[:, 64 * t:64 * t + 36], f8[:, c, t * P:t * P + P], wr[:, c, :],
                                   start=(c == 0), stop=(c == KC - 1))
            ins.then_inc(lg_pe, 1)

            def embedding(t):
                wh, wl_ = (part.rearrange("p (c n) -> p c n", c=2) for part in parts(P_PLE))
                for q in range(2):
                    for c in range(2):
                        ins = mm3(pj[:, (G_PLE + t) % 2, 512 * q:512 * q + 512],
                                  pth[:, c, t * P:t * P + P], ptl[:, c, t * P:t * P + P],
                                  wh[:, c, 512 * q:512 * q + 512], wl_[:, c, 512 * q:512 * q + 512],
                                  start=(c == 0), stop=(c == 1))
                return ins
            ready(P_PLE)
            embedding(1).then_inc(ple_pe, 1)
            pe.wait_ge(grp_done, 1)
            g0, g1 = rt[:, 0, 56:60], rt[:, 1, 56:60]
            m.matmul(ov[:, 128:132], upper[:], g0, start=True, stop=True)
            m.matmul(ov[:, 132:136], ones[:], g0, start=True, stop=False)
            m.matmul(ov[:, 132:136], upper[:], g1, start=False, stop=True)
            m.matmul(ov[:, 136:140], ones[:], g0, start=True, stop=False)
            m.matmul(ov[:, 136:140], ones[:], g1, start=False, stop=True).then_inc(rank_pe, 1)

            def gather():
                for c in range(KC):
                    o = pj[:, 1, c * P:c * P + P]
                    for t in range(T):
                        m.matmul(o, xnh[:, t, c::KC], pm[:, t, :], start=(t == 0), stop=False)
                        ins = m.matmul(o, xnl[:, t, c::KC], pm[:, t, :], start=False, stop=(t == T - 1))
                ins.then_inc(m_gat, 1)
            ins = embedding(0)
            ins.then_inc(piece_used, 1)
            pe.wait_ge(xnh_done, 1)
            pe.wait_ge(xnl_done, 1)
            pe.wait_ge(m_pm, 1)
            pe.wait_ge(pj_read[(G_PLE + 1) % 2], read_count(G_PLE + 1))
            gather()
            pe.wait_ge(wl_done, 1)
            pe.wait_ge(pj_read[G_PLE % 2], read_count(G_PLE))
            pe.wait_ge(plan_done, 1)
            nb = pe.value_load(plan[0:1, 0:1], min_val=NG, max_val=NG + 1)

            def scatter(t, pair=1):
                for q in range(2):
                    o = pj[:, pair, 512 * q:512 * q + 512]
                    m.matmul(o, pT[:, t * P:t * P + P], yh[:, 512 * q:512 * q + 512], start=True, stop=False)
                    ins = m.matmul(o, pT[:, t * P:t * P + P], yl[:, 512 * q:512 * q + 512],
                                   start=False, stop=True)
                ins.then_inc(m_sc, 1)
            pe.wait_ge(m_yh, 1)
            with pe.Fori(0, nb) as b:
                pe.wait_ge(m_pt, b + 1)
                for t in range(T):
                    m.transpose(ov[:, t * P:t * P + P], pm[:, t, :].bitcast(F32), ident[:])
                for t in range(T):
                    ins = m.matmul(tp[:, 400:400 + NE + 1], pm[:, t, :].bitcast(F32), wl8[:, t, :],
                                   start=(t == 0), stop=(t == T - 1))
                ins.then_inc(m_ptp, 1)

                def act_transposes(x):
                    pe.wait_ge(m_act, b * NE + (x + 1))
                    if x == 0:
                        pe.wait_ge(m_wc, b + 1)
                    for r in range(2):
                        ins = m.transpose(tp[:, r * P:r * P + P], ac[:, x % 2, r::2], ident[:])
                    ins.then_inc(m_tp, 1)
                for i, (kind, x, h) in enumerate(MOE):
                    ready(N_PRE + i, b)
                    if kind == "g":
                        if i == 0:
                            pe.wait_ge(m_hgl, b + 1)
                        wh, wl_ = (t.rearrange("p (w c n) -> p w c n", w=2, c=4) for t in parts(N_PRE + i))
                        o = pj[:, 0, 512 * (x % 2):512 * (x % 2) + 512].rearrange("p (w n) -> p w n", w=2)
                        for c in range(4):
                            ins = mm3(o, hgh[:, 4 * h + c, :], hgl[:, 4 * h + c, :], wh[:, :, c, :], wl_[:, :, c, :],
                                      start=(h == 0 and c == 0), stop=(h == 1 and c == 3))
                        ins.then_inc(piece_used, 1)
                        if h == 0 and x >= 1:
                            act_transposes(x - 1)
                    else:
                        wh, wl_ = (t.rearrange("p (c n) -> p c n", c=2) for t in parts(N_PRE + i))
                        pe.wait_ge(m_acl, b * NE + (x + 1))
                        for q in range(2):
                            for c in range(2):
                                ins = mm3(sc[:, q, :], ach[:, x % 2, c, :], acl[:, x % 2, c, :],
                                          wh[:, c, 512 * q:512 * q + 512], wl_[:, c, 512 * q:512 * q + 512],
                                          start=(x == 0 and c == 0), stop=(x == NE - 1 and c == 1))
                            if q == 0 and x == NE - 2:
                                act_transposes(NE - 1)
                        ins.then_inc(piece_used, 1)
                    if i == 1:
                        pe.wait_ge(m_yl, b + 1)
                        pe.wait_ge(m_hgf, b + 1)
                        scatter(0)
                    if i == 3:
                        pe.wait_ge(m_add, b * T + 1)
                        scatter(1)
                    if i == 14:
                        pe.wait_ge(m_pm, b + 2)
                        pe.wait_ge(m_add, (b + 1) * T)
                        gather()
            pe.wait_ge(m_yl, nb + 1)
            pe.wait_ge(m_pt, nb + 1)
            pe.wait_ge(m_hgf, nb + 1)
            for t in range(T):
                scatter(t, t)

            pe.wait_ge(m_add, (nb + 1) * T)
            transposes(x1, xt_banks, xt3)
            for j in range(4):
                ready(N_PRE + j, nb)
                if j < 2:
                    pe.wait_ge(al_done, 3 + j)
                for t in range(T):
                    ins = by_token(pj[:, j // 2, 512 * t:512 * t + 512], N_PRE + j, t, (j % 2, 2))
                ins.then_inc(piece_used, 1)


_INS = ['x', 'p', 'attn_norm_g', 'w_in', 'b_gate', 'q_norm_g', 'k_norm_g', 'lam_qk', 'subln_g', 'w_attn_up',
        'ssm_lam_re', 'ssm_lam_im', 'ssm_log_step', 'ssm_b_re', 'ssm_b_im', 'ssm_c_re', 'ssm_c_im', 'ssm_d',
        'w_glu', 'b_glu', 'w_ssm_up', 'w_out', 'ffn_norm_g', 'w_router_group', 'b_router_group',
        'w_router_expert', 'b_router_expert', 'w_exp_gate', 'w_exp_up', 'w_exp_down',
        'ple_norm_g', 'w_ple_gate', 'w_ple']


def kernel(**inputs):
    import numpy as _np
    import concourse.bacc as _bacc
    from concourse import mybir as _mybir
    from concourse.bass_utils import run_bass_kernel_spmd as _run

    nc = _bacc.Bacc("TRN2", target_bir_lowering=False, num_devices=1)
    arrays, args = {}, {}
    for name in _INS:
        arr = _np.ascontiguousarray(inputs[name])
        arrays[f"in_{name}_dram"] = arr
        args[name] = nc.dram_tensor(f"in_{name}_dram", arr.shape, _mybir.dt.from_np(arr.dtype),
                                    kind="ExternalInput").ap()
    out = nc.dram_tensor("out_0_dram", (1, S, D), _mybir.dt.float32, kind="ExternalOutput").ap()
    build(nc, args, out)
    r = _run(nc, [arrays], core_ids=[0])
    return r.results[0]["out_0_dram"]
```

```python
from contextlib import ExitStack
import math

import numpy as np
import concourse.bass as bass
from concourse import mybir

F32 = mybir.dt.float32
F32R = mybir.dt.float32r
I32 = mybir.dt.int32
ALU = mybir.AluOpType
ACT = mybir.ActivationFunctionType
AX = mybir.AxisListType.X

P = 128
S = 256
T = S // P
D = 1024
KC = D // P
HEADS = 8
DH = 64
SSMW = 512
SG = 32
NST = 64
SH = 16
ST = SG * NST // P
HALF = 128
LEVELS = 7
NG = 4
NE = 8
FF = 256
EPS = 1e-6
LAM_INIT = 0.8 - 0.6 * math.exp(-0.3 * 0)
SCALE = DH ** -0.5
NEG = -1e30
GELU_C = 2.0 * math.sqrt(2.0 / math.pi)
ROUND = 1.5 * 2.0 ** 23
PI2_HI = 6.28125
PI2_MID = 0.0019350051879882812
PI2_LO = 2 * math.pi - PI2_HI - PI2_MID

NRAW = 8
NSPL = 4
LO_BY_POOL = (1,)
AHEAD = 3
PIECE = 2048

P_U = 0
P_QKV = 2
P_G = 14
P_GLU = P_G + 6
P_UP = 23
P_AT = 25
P_WO = 29
P_PLE = 33
N_PRE = 34
PER_BLOCK = 3 * NE
TILES_AT = {6 + j: (j, j + 1) for j in range(0, ST, 2)}
YT_AT = {9 + j: j for j in range(ST)}
HALF_PIECES = 2 * (P_G - P_QKV)
QN_AT = {4 * i + 4: i for i in range(4)}
QT_AT = {4 * i + 8 + h: (i, h) for i in range(4) for h in range(2)}
G_U, G_Q, G_K, G_V, G_G, G_GLU, G_UP, G_AT, G_WO, G_PLE = 0, 1, 3, 5, (7, 8, 9, 11), 10, 12, 14, 16, 18
C_BG, C_LR, C_LI, C_BGLU, C_D, C_SUB, C_QG, C_KG, C_LS = 0, 16, 32, 48, 52, 56, 57, 58, 64


def moe_order():
    order = [("g", 0, 0), ("g", 0, 1)]
    for e in range(NE):
        if e + 1 < NE:
            order += [("g", e + 1, 0), ("g", e + 1, 1)]
        order.append(("d", e, 0))
    return order


MOE = moe_order()


class Steps:

    def __init__(self, eng, sem):
        self.eng, self.sem, self.n, self.base = eng, sem, 0, 0

    def add(self, ins):
        ins.then_inc(self.sem, 1)
        self.n += 1
        return ins

    def wait(self):
        self.eng.wait_ge(self.sem, self.base + self.n)

    def do(self, ins):
        self.add(ins)
        self.wait()


def build(nc, a, out):
    ctx = ExitStack()
    with ctx:
        def sb(name, shape, dt=F32, stack=None):
            return (stack or ctx).enter_context(nc.sbuf_tensor(name, shape, dt))

        def sem(name):
            return ctx.enter_context(nc.semaphore(name))

        ring = ExitStack()
        raw = sb("raw", [P, NRAW, PIECE], stack=ring)
        ring.close()
        wlo = sb("wlo", [P, NRAW, PIECE], F32R)
        whi = sb("whi", [P, NSPL, PIECE], F32R)
        ah = sb("ah", [P, KC, S], F32R)
        al = sb("al", [P, KC, S], F32R)
        pst = sb("pst", [P, T, 256])
        pth = sb("pth", [P, 2, S], F32R)
        ptl = sb("ptl", [P, 2, S], F32R)
        ident = sb("ident", [P, P])
        ones = sb("ones", [P, P])
        upper = sb("upper", [P, P])
        iota = sb("iota", [P, P])
        mask = sb("mask", [P, 2 * P])
        mk = sb("mk", [P, 4])
        half_c = sb("half_c", [P, 64])
        smt = sb("smt", [80, P])
        lst = sb("lst", [80, 2])
        col = sb("col", [P, 80])
        gains = sb("gains", [P, 3, KC])
        subg = sb("subg", [P, 1])
        lamq = sb("lamq", [1, 4 * DH])
        lamp = sb("lamp", [1, 2 * DH])
        lams = sb("lams", [1, 4])
        lam = sb("lam", [P, 1])
        nrm = sb("nrm", [P, 64])
        wr = sb("wr", [P, KC, 36])
        wrb = sb("wrb", [P, 36])
        ss = sb("ss", [P, 24, 16])
        rt = sb("rt", [P, 2, 160])
        slotc = sb("slotc", [P, T, 8])
        ohc = sb("ohc", [P, T, 8])
        wl8 = sb("wl8", [P, T, NE + 1])
        wc = sb("wc", [P, NE + 1])
        cnt = sb("cnt", [P, 8])
        plan = sb("plan", [P, 2], I32)
        att = sb("att", [P, 32])
        oss = sb("oss", [P, 4])
        osq = sb("osq", [P, 2, P])
        desc = sb("desc", [P, NE])

        ph = ExitStack()
        qT = sb("qT", [P, HEADS, S], stack=ph)
        kT = sb("kT", [P, HEADS, S], stack=ph)
        v = sb("v", [P, T, D], stack=ph)
        y = sb("y", [P, 4, S], stack=ph)
        p1 = ExitStack()
        rq = sb("rq", [P, 2, 512], stack=p1)
        qn = sb("qn", [P, T, 512], stack=p1)
        ptab = sb("ptab", [P, 2, ST, HALF], stack=p1)
        bT = sb("bT", [P, 2, 4, P], stack=p1)
        cm = sb("cm", [P, 2, ST, 32], stack=p1)
        uT = sb("uT", [P, 4, S], stack=p1)
        tt = sb("tt", [P, 2, 512], stack=p1)
        rr = sb("rr", [P, 2, 512], stack=p1)
        so = sb("so", [P, 2, 512], stack=p1)
        pp2 = sb("pp2", [P, 512], stack=p1)
        ini = sb("ini", [P, 2, 4], stack=p1)
        p1.close()
        p2 = ExitStack()
        zh = sb("zh", [P, 4, S], F32R, stack=p2)
        zl = sb("zl", [P, 4, S], F32R, stack=p2)
        gT = sb("gT", [P, 16, S], stack=p2)
        oh = sb("oh", [P, HEADS, S], F32R, stack=p2)
        ol = sb("ol", [P, HEADS, S], F32R, stack=p2)
        sm = sb("sm", [P, 2, 384], stack=p2)
        ee = sb("ee", [P, 2, 384], stack=p2)
        ww = sb("ww", [P, 384], stack=p2)
        wT = sb("wT", [P, 384], stack=p2)
        on = sb("on", [P, 2, P], stack=p2)
        p2.close()
        ph.close()
        p3 = ExitStack()
        f8 = sb("f8", [P, KC, S], stack=p3)
        pp = sb("pp", [P, T, D], stack=p3)
        x1 = sb("x1", [P, T, D], stack=p3)
        xnh = sb("xnh", [P, T, D], F32R, stack=p3)
        xnl = sb("xnl", [P, T, D], F32R, stack=p3)
        xn2 = sb("xn2", [P, T, D], stack=p3)
        hgh = sb("hgh", [P, KC, P], F32R, stack=p3)
        hgl = sb("hgl", [P, KC, P], F32R, stack=p3)
        yh = sb("yh", [P, D], F32R, stack=p3)
        yl = sb("yl", [P, D], F32R, stack=p3)
        pm = sb("pm", [P, T, P], F32R, stack=p3)
        pT = sb("pT", [P, S], F32R, stack=p3)
        sg = sb("sg", [P, FF], stack=p3)
        a1 = sb("a1", [P, FF], stack=p3)
        ac = sb("ac", [P, 2, FF], stack=p3)
        ach = sb("ach", [P, 2, 2, P], F32R, stack=p3)
        acl = sb("acl", [P, 2, 2, P], F32R, stack=p3)
        p3.close()
        xin, xn = qT[:].rearrange("p a b -> p (a b)").rearrange("p (t d) -> p t d", t=T), \
            kT[:].rearrange("p a b -> p (a b)").rearrange("p (t d) -> p t d", t=T)
        cst = v[:, 0, :].rearrange("p (r k n) -> p r k n", r=2, k=4)
        bm = v[:, 1, :].rearrange("p (r j g h) -> p r j g h", r=2, j=ST, g=2)
        scans = [rr[:, 0, :], rr[:, 1, :], rq[:, 0, :], rq[:, 1, :]]
        pw = osq[:].rearrange("p a n -> p (a n)").rearrange("p (r i j) -> p r i j", r=2, i=LEVELS + 1)
        hgf = f8[:, 0:4].rearrange("p a b -> p (a b)").rearrange("p (c s) -> p c s", c=KC)
        bst = rq[:].rearrange("p t n -> p (t n)").rearrange("p (r j h) -> p r j h", r=4, j=ST)

        def psum(name, shape):
            return ctx.enter_context(nc.psum_tensor(name, shape, F32))
        pj = psum("pj", [P, 2, 1024])
        sc = psum("sc", [P, 2, 512])
        tp = psum("tp", [P, 512])
        ov = psum("ov", [P, 512])

        xt_banks0 = [pj[:, k // 2, 512 * (k % 2):512 * (k % 2) + 512] for k in range(4)]
        xt_banks = [sc[:, 0, :], sc[:, 1, :], tp[:], ov[:]]

        raw_in = [sem(f"raw_in{i}") for i in range(NRAW)]
        hi_done = sem("hi_done")
        lo_done = sem("lo_done")
        lo_pool = sem("lo_pool")
        piece_used = sem("piece_used")
        x_in, small_in, vec_in, p_in, xres_in, bc_in, router_in = (
            sem(n) for n in ("x_in", "small_in", "vec_in", "p_in", "xres_in", "bc_in", "router_in"))
        pool_step, act_step, dve_step = sem("pool_step"), sem("act_step"), sem("dve_step")
        moe_step = sem("moe_step")
        consts = sem("consts")
        xsq = sem("xsq")
        xrs = sem("xrs")
        xnd = sem("xnd")
        xt_pe = sem("xt_pe")
        ah_done = sem("ah_done")
        al_done = sem("al_done")
        pj_read = [sem(f"pj_read{i}") for i in range(2)]
        ls_done = sem("ls_done")
        small_pe = sem("small_pe")
        col_done = sem("col_done")
        lam_row, lam_exp, lam_sum, lam_pe, lam_done = (
            sem(n) for n in ("lam_row", "lam_exp", "lam_sum", "lam_pe", "lam_done"))
        dt_done = sem("dt_done")
        th_done = sem("th_done")
        trig = sem("trig")
        pow_done = sem("pow_done")
        re_done, im_done = sem("re_done"), sem("im_done")
        bm_done = sem("bm_done")
        b_pe, c_pe = sem("b_pe"), sem("c_pe")
        bT_done, cm_done = sem("bT_done"), sem("cm_done")
        bu_full = sem("bu_full")
        bu_read = sem("bu_read")
        scan_done = sem("scan_done")
        rot_done = sem("rot_done")
        last_rot = sem("last_rot")
        y_pe = sem("y_pe")
        y_read = sem("y_read")
        ssq_done = sem("ssq_done")
        qk_rs = sem("qk_rs")
        qt_pe = sem("qt_pe")
        qt_done = sem("qt_done")
        gelu_in, gelu_sig, z_done, z_hi, z_lo = (
            sem(n) for n in ("gelu_in", "gelu_sig", "z_done", "z_hi", "z_lo"))
        s_full = sem("s_full")
        max_done = sem("max_done")
        e_done = sem("e_done")
        w_done = sem("w_done")
        wt_pe, wt_done = sem("wt_pe"), sem("wt_done")
        o_full = sem("o_full")
        o_sq, o_rs, o_done = sem("o_sq"), sem("o_rs"), sem("o_done")
        ot_pe, oh_done, ol_done = sem("ot_pe"), sem("oh_done"), sem("ol_done")
        g_sig = sem("g_sig")
        pt_pe, pth_done, ptl_done = sem("pt_pe"), sem("pth_done"), sem("ptl_done")
        mix_done = sem("mix_done")
        xnh_done, xnl_done = sem("xnh_done"), sem("xnl_done")
        ple_pe = sem("ple_pe")
        f8_done = sem("f8_done")
        wr_done = sem("wr_done")
        lg_pe, lg_in, lg_exp = sem("lg_pe"), sem("lg_in"), sem("lg_exp")
        grp_done, rank_pe, plan_done = sem("grp_done"), sem("rank_pe"), sem("plan_done")
        m_pm = sem("m_pm")
        m_gat = sem("m_gat")
        m_hgf = sem("m_hgf")
        m_hgh, m_hgl = sem("m_hgh"), sem("m_hgl")
        m_ptp = sem("m_ptp")
        m_pt, m_wc = sem("m_pt"), sem("m_wc")
        m_sig, m_act = sem("m_sig"), sem("m_act")
        m_tp, m_ach, m_acl = sem("m_tp"), sem("m_ach"), sem("m_acl")
        m_yh, m_yl = sem("m_yh"), sem("m_yl")
        y_first = sem("y_first")
        m_sc, m_add = sem("m_sc"), sem("m_add")
        wl_done = sem("wl_done")
        xt3 = sem("xt3")
        gate_pe, pl_sig = sem("gate_pe"), sem("pl_sig")
        o_ready, o_out = sem("o_ready"), sem("o_out")

        last_piece = {G_U: P_U + 1, G_GLU: P_GLU, G_PLE: P_PLE, G_PLE + 1: P_PLE, G_UP: P_UP, G_UP + 1: P_UP + 1}
        last_piece.update({G_Q + i: P_QKV + 2 * i + 1 for i in range(6)})
        last_piece.update({G: P_G + 2 * i + 1 + (i == 3) for i, G in enumerate(G_G)})
        last_piece.update({G_AT + i: P_AT + 2 * i + 1 for i in range(2)})
        last_piece.update({G_WO + i: P_WO + 2 + i for i in range(2)})

        def level(i, part):
            L = 2 ** i
            c, s = (pw[:, r, i, :].unsqueeze(2).to_broadcast([P, ST, L]) for r in range(2))
            return L, c, s, ptab[:, 0, :, 0:L], ptab[:, 1, :, 0:L], ptab[:, part, :, L:2 * L]

        def full(eng, G):
            eng.wait_ge(piece_used, last_piece[G] + 1)

        def read_count(G):
            return G // 2 + 2

        w_in = a["w_in"][0].rearrange("(p h c) n -> h p c n", h=2, c=4)

        def cols(w, c0):
            return [w[h, :, :, c0:c0 + 512] for h in range(2)]
        glu_w = a["w_glu"][0].rearrange("(c p) n -> p c n", p=P)
        up_w = a["w_ssm_up"][0].rearrange("(c p) n -> p c n", p=P)
        at_w = a["w_attn_up"][0].rearrange("(h c p) n -> h p c n", h=2, p=P)
        wo_w = a["w_out"][0].rearrange("(h c p) n -> h p c n", h=2, p=P)
        pg_w = a["w_ple_gate"][0].rearrange("(p h c) n -> h p c n", h=2, c=4)
        pl_w = a["w_ple"][0].rearrange("(p c) n -> p c n", c=2)
        pre = cols(w_in, 3072)
        for c0 in (0, 512, 1024, 1536, 2048, 2560):
            pre += cols(w_in, c0)
        for g in range(4):
            if g == 3:
                pre.append(glu_w)
            pre += cols(w_in, 3584 + 512 * g)
        pre += [up_w[:, :, 0:512], up_w[:, :, 512:1024]]
        pre += cols(at_w, 0) + cols(at_w, 512)
        pre += [half for pair in zip(cols(wo_w, 0), cols(wo_w, 512)) for half in pair] + [pl_w]
        assert len(pre) == N_PRE
        ple = cols(pg_w, 0) + cols(pg_w, 512)
        wg_e = a["w_exp_gate"][0].rearrange("n e (p h c) f -> (n e) h p (c f)", h=2, c=4)
        wu_e = a["w_exp_up"][0].rearrange("n e (p h c) f -> (n e) h p (c f)", h=2, c=4)
        wd_e = a["w_exp_down"][0].rearrange("n e (p c) d -> (n e) p (c d)", c=2)
        bg = a["b_gate"][0].rearrange("(r n) -> r n", n=P)
        SMALL = ((C_BG, bg),
                 (C_LR, a["ssm_lam_re"][0].rearrange("(j g) s -> j (g s)", g=2)),
                 (C_LI, a["ssm_lam_im"][0].rearrange("(j g) s -> j (g s)", g=2)),
                 (C_BGLU, a["b_glu"][0].rearrange("(r n) -> r n", n=P)),
                 (C_D, a["ssm_d"][0].rearrange("(r g) h -> r (g h)", g=8)),
                 (C_SUB, a["subln_g"]),
                 (C_QG, a["q_norm_g"].rearrange("o m d -> o (m d)")),
                 (C_KG, a["k_norm_g"].rearrange("o m d -> o (m d)")),
                 (C_KG + 1, bg[0:C_LS - C_KG - 1]))
        xd = a["x"][0].rearrange("(t p) d -> p t d", p=P)
        outd = out[0].rearrange("(t p) d -> p t d", p=P)

        block = ctx.enter_context(nc.Block())

        @block.sync
        def _(sp):
            def load(i, halves, b=0):
                if i >= NRAW:
                    sp.wait_ge(piece_used, b * PER_BLOCK + (i - NRAW + 1))
                for dst, src in halves(raw[:, i % NRAW, :]):
                    sp.dma_start(dst, src).then_inc(raw_in[i % NRAW], 16)

            def plain(src):
                k = src.shape[1]

                def halves(slot):
                    d = slot.rearrange("p (c n) -> p c n", c=k)
                    return [(d[:, 0:k // 2], src[:, 0:k // 2]), (d[:, k // 2:], src[:, k // 2:])]
                return halves
            for t in range(T):
                sp.dma_start(xin[:, t], xd[:, t]).then_inc(x_in, 16)
            sp.dma_start(gains[:, 0, :], a["attn_norm_g"][0].rearrange("(p c) -> p c", c=KC)).then_inc(vec_in, 16)
            sp.dma_start(lamq[:], a["lam_qk"].rearrange("o m d -> o (m d)")).then_inc(vec_in, 16)
            for r0, src in SMALL[0:4]:
                sp.dma_start(smt[r0:r0 + src.shape[0], :], src).then_inc(small_in, 16)
            for n in range(N_PRE):
                load(n, plain(pre[n]))
                if n == 1:
                    sp.dma_start(pst[:], a["p"][0, 0].rearrange("(t p) d -> p t d", p=P)).then_inc(p_in, 16)
                    for i, nm in enumerate(("ssm_b_re", "ssm_b_im")):
                        sp.dma_start(bst[:, i], a[nm][0].rearrange("(j g) s h -> (g s) j h", g=2)).then_inc(bc_in, 16)
                    for i, nm in enumerate(("ssm_c_re", "ssm_c_im")):
                        for d in range(2):
                            sp.dma_start(cst[:, i, :, NST * d:NST * d + NST],
                                         a[nm][0].rearrange("(k g) h s -> (g h) k s", g=8)).then_inc(bc_in, 16)
            sp.wait_ge(o_full, HEADS)
            sp.dma_start(x1[:], xd).then_inc(xres_in, 16)

            def block_loads(b, group):
                for i, (kind, e, h) in enumerate(MOE):
                    ex = group * NE + e

                    def halves(slot):
                        d = slot.rearrange("p (w n) -> p w n", w=2)
                        if kind == "g":
                            return [(d[:, w], m[bass.ds(ex, 1), h].rearrange("a p n -> (a p) n"))
                                    for w, m in enumerate((wg_e, wu_e))]
                        s = wd_e[bass.ds(ex, 1)].rearrange("a p (w n) -> (a p) w n", w=2)
                        return [(d[:, w], s[:, w]) for w in range(2)]
                    load(N_PRE + i, halves, b)
            with sp.Fori(0, NG) as b:
                block_loads(b, b)
            sp.wait_ge(plan_done, 1)
            nb = sp.value_load(plan[0:1, 0:1], min_val=NG, max_val=NG + 1)
            gx = sp.value_load(plan[0:1, 1:2], min_val=0, max_val=NG - 1)
            with sp.If(nb > NG):
                block_loads(NG, gx)
            for j in range(4):
                load(N_PRE + j, plain(ple[j]), nb)
            for i in range(2):
                for t in range(T):
                    sp.wait_ge(o_ready, T * i + t + 1)
                    c = slice(512 * i, 512 * i + 512)
                    sp.dma_start(outd[:, t, c], x1[:, t, c]).then_inc(o_out, 16)
            sp.wait_ge(o_out, 2 * T * 16)

        @block.gpsimd
        def _(pool):
            g = nc.gpsimd
            st = Steps(pool, pool_step)
            for buf, val in ((ones, 1.0), (half_c, -0.5), (mask, 0.0), (mk, -1.0), (slotc, -1.0), (ohc, 0.0)):
                st.add(g.memset(buf[:], val))
            st.wait()
            g.affine_select(out=ident[:], in_=ones[:], compare_op=ALU.is_equal, fill=0.0, base=0,
                            pattern=[[-1, P]], channel_multiplier=1).then_inc(consts, 1)
            g.affine_select(out=upper[:], in_=ones[:], compare_op=ALU.is_gt, fill=0.0, base=0,
                            pattern=[[1, P]], channel_multiplier=-1).then_inc(consts, 1)
            g.affine_select(out=mask[:, P:], in_=mask[:, P:], compare_op=ALU.is_ge, fill=NEG, base=0,
                            pattern=[[-1, P]], channel_multiplier=1).then_inc(consts, 1)
            g.iota(iota[:], pattern=[[1, P]], base=0, channel_multiplier=0,
                   allow_small_or_imprecise_dtypes=True).then_inc(consts, 1)
            for i, src in enumerate((ones[:, 0:1], ones[:, 0:1], mk[:, 2:3], mk[:, 3:4])):
                sign, cmp = ((-1, ALU.is_gt), (1, ALU.is_ge))[i % 2]
                g.affine_select(out=mk[:, i:i + 1], in_=src, compare_op=cmp, fill=0.0, base=-64 * sign,
                                pattern=[[0, 1]], channel_multiplier=sign).then_inc(consts, 1)

            def inv_root(ap, width, dim, done):
                st.do(g.tensor_scalar(ap, ap, 1.0 / dim, EPS, ALU.mult, ALU.add))
                g.tensor_tensor(ap, ap, half_c[:, 0:width], ALU.pow).then_inc(done, 1)
            pool.wait_ge(xsq, 1)
            inv_root(nrm[:, 0:2], 2, D, xrs)

            def split_lo(i):
                pool.wait_ge(hi_done, i + 1)
                g.tensor_tensor(wlo[:, i % NRAW, :], raw[:, i % NRAW, :], whi[:, i % NSPL, :].bitcast(F32),
                                ALU.subtract).then_inc(lo_pool, 1)

            def rload(dst, src):
                pool.dma_start(dst, src).then_inc(router_in, 16)
            for i, nm in enumerate(("ffn_norm_g", "ple_norm_g")):
                rload(gains[:, 1 + i, :], a[nm][0].rearrange("(p c) -> p c", c=KC))
            rload(wr[:, :, 0:NG], a["w_router_group"][0].rearrange("(p c) n -> p c n", c=KC))
            for n in range(NG):
                rload(wr[:, :, NG + NE * n:NG + NE * n + NE],
                      a["w_router_expert"][0, n].rearrange("(p c) e -> p c e", c=KC))
            rload(wrb[:, 0:NG], a["b_router_group"][0].partition_broadcast(P))
            rload(wrb[:, NG:36], a["b_router_expert"][0].rearrange("n e -> (n e)").partition_broadcast(P))

            for i in LO_BY_POOL:
                split_lo(i)

            g.memset(ptab[:, 1, :, 0:1], 0.0).then_inc(im_done, 1)
            pool.wait_ge(im_done, 1)
            pool.wait_ge(pow_done, 1)
            for i in range(LEVELS):
                L, c_, s_, re, im, new = level(i, 1)
                t2 = rr[:].rearrange("p a n -> p (a n)")[:, 0:ST * L].rearrange("p (j l) -> p j l", j=ST)
                pool.wait_ge(re_done, i + 1)
                st.add(g.tensor_tensor(new, re, s_, ALU.mult))
                st.do(g.tensor_tensor(t2, im, c_, ALU.mult))
                g.tensor_tensor(new, new, t2, ALU.add).then_inc(im_done, 1)
                pool.wait_ge(im_done, i + 2)

            def rotate_back(j):
                b = j % 2
                pool.wait_ge(scan_done, j + 1)
                if j >= 2:
                    pool.wait_ge(y_pe, j - 1)
                c, s = (ptab[:, i, j, :].unsqueeze(1).to_broadcast([P, 4, HALF]) for i in range(2))
                r4 = scans[j % 4].rearrange("p (a t) -> p a t", a=4)
                st.add(g.tensor_tensor(so[:, b, :].rearrange("p (a t) -> p a t", a=4), r4, c, ALU.mult))
                st.do(g.tensor_tensor(pp2[:].rearrange("p (a t) -> p a t", a=4), r4, s, ALU.mult))
                g.tensor_tensor(so[:, b, 0:256], so[:, b, 0:256], pp2[:, 256:512], ALU.subtract)
                g.tensor_tensor(so[:, b, 256:512], so[:, b, 256:512], pp2[:, 0:256], ALU.add).then_inc(rot_done, 1)
                pool.wait_ge(rot_done, j + 1)

            for k in range(HALF_PIECES):
                if k in QN_AT:
                    pool.wait_ge(ssq_done, QN_AT[k] + 1)
                    inv_root(nrm[:, 16:32], 16, DH, qk_rs)
                for j in TILES_AT.get(k, ()):
                    if j < ST - 1:
                        rotate_back(j)
            for h in range(HEADS):
                pool.wait_ge(o_sq, h + 1)
                inv_root(oss[:, 0:2], 2, P, o_rs)
            for i in (1, 2):
                pool.wait_ge(xsq, i + 1)
                inv_root(nrm[:, 2 * i:2 * i + 2], 2, D, xrs)
                if i == 1:
                    zeros = mask[:, 0:P]
                    for buf, done in ((yh, m_yh), (yl, m_yl)):
                        for q in range(2):
                            g.tensor_copy(buf[:, 512 * q:512 * q + 512].rearrange("p (c n) -> p c n", c=4),
                                          zeros.unsqueeze(1).to_broadcast([P, 4, P])).then_inc(done, 1)
                    g.tensor_copy(pT[:].rearrange("p (t n) -> p t n", t=T),
                                  zeros.unsqueeze(1).to_broadcast([P, T, P])).then_inc(m_pt, 1)

        @block.scalar
        def _(act):
            e = nc.scalar
            st = Steps(act, act_step)

            def split_hi(i, b=0):
                act.wait_ge(raw_in[i % NRAW], b * (32 * PER_BLOCK // NRAW) + 32 * (i // NRAW + 1))
                if i >= NSPL:
                    act.wait_ge(piece_used, b * PER_BLOCK + (i - NSPL + 1))
                e.activation(whi[:, i % NSPL, :], raw[:, i % NRAW, :], ACT.Copy).then_inc(hi_done, 1)

            for r0, src in SMALL[4:]:
                act.dma_start(smt[r0:r0 + src.shape[0], :], src).then_inc(small_in, 16)
            act.dma_start(lst[64:80, :], a["ssm_log_step"][0].rearrange("(j g) -> j g", g=2)).then_inc(small_in, 16)

            def square_sums(dst, src, k, done):
                for t in range(T):
                    ins = e.activation(dst[:, t], src[:, t], ACT.Square, accum_out=nrm[:, k + t:k + t + 1])
                ins.then_inc(done, 1)
            act.wait_ge(x_in, 32)
            square_sums(xn, xin, 0, xsq)
            split_hi(0)
            act.wait_ge(small_pe, 1)
            e.activation(col[:], ov[:, 0:80], ACT.Copy).then_inc(col_done, 1)
            act.wait_ge(col_done, 1)
            e.activation(subg[:], col[:, C_SUB:C_SUB + 1], ACT.Copy, scale=1.0 - LAM_INIT)
            e.activation(ss[:, 0, :], col[:, C_LS:C_LS + 16], ACT.Exp).then_inc(dt_done, 1)
            act.wait_ge(lam_row, 1)
            e.activation(lams[0:1, 2:4], lams[0:1, 0:2], ACT.Exp).then_inc(lam_exp, 1)
            act.wait_ge(vec_in, 32)

            def chunks_hi(filled, banks, gain):
                for k, bank in enumerate(banks):
                    act.wait_ge(filled, k + 1)
                    for q in range(2):
                        c = 2 * k + q
                        e.activation(ah[:, c, :], bank[:, q * S:q * S + S], ACT.Copy,
                                     scale=gains[:, gain, c:c + 1]).then_inc(ah_done, 1)
            chunks_hi(xt_pe, xt_banks0, 0)
            split_hi(1)
            act.wait_ge(th_done, 1)
            e.activation(ss[:, 3, :], ss[:, 1, :], ACT.Exp)
            e.activation(ss[:, 5, :], ss[:, 4, :], ACT.Sin)
            e.activation(ss[:, 7, :], ss[:, 6, :], ACT.Sin).then_inc(trig, 1)
            act.wait_ge(pt_pe, 1)
            e.activation(pth[:], tp[:].rearrange("p (c s) -> p c s", c=2), ACT.Copy).then_inc(pth_done, 1)

            def u_evac():
                full(act, G_U)
                e.activation(uT[:].rearrange("p k s -> p (k s)"), pj[:, G_U % 2, :], ACT.Copy)\
                    .then_inc(pj_read[G_U % 2], 1)

            def qk_squares(i):
                full(act, G_Q + i)
                if i:
                    act.wait_ge(pj_read[(G_Q + i - 1) % 2], read_count(G_Q + i - 1))
                else:
                    act.wait_ge(pt_pe, 1)
                for q in range(16):
                    ins = e.activation(pst[:].rearrange("p t n -> p (t n)")[:, DH * (q % 8):DH * (q % 8) + DH],
                                       pj[:, (G_Q + i) % 2, DH * q:DH * q + DH], ACT.Square,
                                       accum_out=nrm[:, 16 + q:17 + q])
                    if q == 7:
                        st.do(ins)
                ins.then_inc(ssq_done, 1)

            def qk_norm(i):
                act.wait_ge(qk_rs, i + 1)
                if i:
                    act.wait_ge(qt_pe, 2 * i)
                src, dst = pj[:, (G_Q + i) % 2, :], qn[:].rearrange("p t n -> p (t n)")
                for q in range(16):
                    ins = e.activation(dst[:, DH * q:DH * q + DH], src[:, DH * q:DH * q + DH], ACT.Copy,
                                       scale=nrm[:, 16 + q:17 + q])
                ins.then_inc(pj_read[(G_Q + i) % 2], 1)

            def qt_evac(i, half):
                act.wait_ge(qt_pe, 2 * i + half + 1)
                h0 = 4 * (i % 2) + 2 * half
                gc = C_QG if i < 2 else C_KG
                e.activation((qT if i < 2 else kT)[:, h0:h0 + 2, :].rearrange("p h s -> p (h s)"), tp[:], ACT.Copy,
                             scale=col[:, gc:gc + 1]).then_inc(qt_done, 1)

            def v_evac(i):
                G = G_V + i
                full(act, G)
                e.activation(v[:, :, 512 * i:512 * i + 512], pj[:, G % 2, :].rearrange("p (t n) -> p t n", t=2),
                             ACT.Copy).then_inc(pj_read[G % 2], 1)

            def g_evac(i):
                G = G_G[i]
                full(act, G)
                for b in range(4):
                    ins = e.activation(gT[:, 4 * i + b, :], pj[:, G % 2, b * S:b * S + S], ACT.Identity,
                                       bias=col[:, C_BG + 4 * i + b:C_BG + 4 * i + b + 1])
                ins.then_inc(pj_read[G % 2], 1)

            split_hi(2)
            split_hi(3)
            u_evac()
            split_hi(4)
            for n in range(P_QKV, P_G):
                split_hi(n + AHEAD)
                if n == P_QKV + 1:
                    act.wait_ge(b_pe, 1)
                    for r in range(2):
                        e.activation(bT[:, r], sc[:, r, :].rearrange("p (k n) -> p k n", k=4), ACT.Copy)\
                            .then_inc(bT_done, 1)
                i = (n - P_QKV) // 2
                if n % 2 == 1:
                    if 1 <= i <= 4:
                        qk_norm(i - 1)
                    qk_squares(i) if i < 4 else v_evac(i - 4)
                for k in (2 * (n - P_QKV), 2 * (n - P_QKV) + 1):
                    if k in QT_AT:
                        qt_evac(*QT_AT[k])

            for j in range(HEADS + 3):
                if j >= 3:
                    act.wait_ge(ot_pe, j - 2)
                    e.activation(oh[:, j - 3, :], tp[:, 0:S], ACT.Copy, scale=subg[:, 0:1]).then_inc(oh_done, 1)
                if j < HEADS + 2:
                    split_hi(P_G + j + AHEAD)
                if j == 0:
                    act.wait_ge(gelu_in, 1)
                    e.activation(tt[:], tt[:], ACT.Sigmoid, scale=GELU_C).then_inc(gelu_sig, 1)
                if j in (1, HEADS):
                    act.wait_ge(z_done, 1 if j == 1 else 2)
                    e.activation(zh[:], y[:], ACT.Copy).then_inc(z_hi, 1)
                if 1 <= j <= HEADS:
                    act.wait_ge(wt_pe, j)
                    e.activation(wT[:], tp[:, 0:384], ACT.Copy).then_inc(wt_done, 1)
                if j < HEADS:
                    act.wait_ge(max_done, j + 1)
                    for m in range(2):
                        for qb, (k0, k1) in enumerate(((0, P), (P, 3 * P))):
                            i = 2 * m + qb
                            ins = e.activation(ee[:, m, k0:k1], sm[:, m, k0:k1], ACT.Exp, scale=SCALE,
                                               bias=att[:, 4 + i:5 + i], accum_out=att[:, 8 + i:9 + i])
                    ins.then_inc(e_done, 1)
                if j in (1, 3, 5, 8):
                    g_evac(j // 2 if j < 8 else 3)
                if 1 <= j <= HEADS:
                    act.wait_ge(o_full, j)
                    if j >= 2:
                        act.wait_ge(o_done, j - 1)
                    for qb in range(2):
                        ins = e.activation(osq[:, qb], ov[:, qb * P:qb * P + P], ACT.Square, accum_out=oss[:, qb:qb + 1])
                    ins.then_inc(o_sq, 1)
                if j == HEADS:
                    act.wait_ge(pj_read[G_G[3] % 2], read_count(G_G[3]))
                    e.activation(gT[:, 8:16], gT[:, 8:16], ACT.Sigmoid).then_inc(g_sig, 1)
                    e.activation(gT[:, 0:8], gT[:, 0:8], ACT.Sigmoid).then_inc(g_sig, 1)
                if j == HEADS - 1:
                    full(act, G_GLU)
                    for b in range(4):
                        ins = e.activation(f8[:, b, :], pj[:, G_GLU % 2, b * S:b * S + S], ACT.Sigmoid,
                                           bias=col[:, C_BGLU + b:C_BGLU + b + 1])
                    ins.then_inc(pj_read[G_GLU % 2], 1)
            for n in range(P_UP + 1, N_PRE):
                split_hi(n + AHEAD)
                if n in (P_AT + 2, P_WO):
                    i = 0 if n < P_WO else 1
                    act.wait_ge(mix_done, i + 1)
                    e.activation(ah[:, 4 * i:4 * i + 4, :], gT[:, 4 * i:4 * i + 4, :], ACT.Copy).then_inc(ah_done, 1)

            act.wait_ge(pj_read[0], read_count(G_WO))
            act.wait_ge(pj_read[1], read_count(G_WO + 1))
            for k in (2, 3):
                act.wait_ge(xt_pe, 4 + k + 1)
                e.activation(f8[:, 2 * k:2 * k + 2].rearrange("p c s -> p (c s)"), xt_banks[k], ACT.Copy)\
                    .then_inc(f8_done, 1)
            square_sums(xn2, x1, 2, xsq)
            e.activation(xnh[:], x1[:], ACT.Copy).then_inc(xnh_done, 1)
            act.wait_ge(ple_pe, 1)
            e.activation(pp[:, 1, :], pj[:, (G_PLE + 1) % 2, :], ACT.Copy).then_inc(pj_read[(G_PLE + 1) % 2], 1)
            act.wait_ge(lg_in, 1)
            e.activation(rt[:, :, 48:52], rt[:, :, 44:48], ACT.Exp).then_inc(lg_exp, 1)
            act.wait_ge(lg_in, 2)
            e.activation(rt[:, :, 90:91], rt[:, :, 89:90], ACT.Exp).then_inc(lg_exp, 1)

            full(act, G_PLE)
            e.activation(pp[:, 0, :], pj[:, G_PLE % 2, :], ACT.Copy).then_inc(pj_read[G_PLE % 2], 1)

            def tokens_hi(base):
                for h in range(2):
                    act.wait_ge(m_hgf, base + (h + 1))
                    c = slice(KC // 2 * h, KC // 2 * h + KC // 2)
                    e.activation(hgh[:, c], hgf[:, c], ACT.Copy).then_inc(m_hgh, 1)
            tokens_hi(0)
            act.wait_ge(plan_done, 1)
            nb = act.value_load(plan[0:1, 0:1], min_val=NG, max_val=NG + 1)
            with act.Fori(0, nb) as b:
                def act_hi(x):
                    act.wait_ge(m_tp, b * NE + (x + 1))
                    e.activation(ach[:, x % 2], tp[:, 0:FF].rearrange("p (r n) -> p r n", r=2), ACT.Copy).then_inc(m_ach, 1)
                for i, (kind, x, h) in enumerate(MOE):
                    if kind == "g" and h == 1 and x >= 1:
                        act_hi(x - 1)
                    split_hi(N_PRE + i + AHEAD, b)
                    if i == 4:
                        act.wait_ge(m_ptp, b + 1)
                        act.wait_ge(m_sc, (b + 1) * T)
                        e.activation(pT[:], ov[:, 0:S], ACT.Copy).then_inc(m_pt, 1)
                    if kind == "g" and h == 1:
                        act.wait_ge(piece_used, b * PER_BLOCK + (N_PRE + i + 1))
                        if x == 0:
                            act.wait_ge(m_wc, b + 1)
                        e.activation(sg[:], pj[:, 0, 512 * (x % 2):512 * (x % 2) + FF], ACT.Sigmoid,
                                     scale=wc[:, NE:NE + 1])\
                            .then_inc(m_sig, 1)
                    if kind == "d" and x == NE - 2:
                        act_hi(NE - 1)
                        tokens_hi(b * 2 + 2)
                for q in range(2):
                    if q == 0:
                        act.wait_ge(y_first, b + 1)
                    else:
                        act.wait_ge(piece_used, b * PER_BLOCK + (N_PRE + PER_BLOCK))
                    e.activation(yh[:, 512 * q:512 * q + 512], sc[:, q, :], ACT.Copy).then_inc(m_yh, 1)

            act.wait_ge(router_in, 16 * 9)
            act.wait_ge(m_add, (nb + 1) * T)
            chunks_hi(xt3, xt_banks, 2)
            split_hi(N_PRE + 3, nb)
            square_sums(xn2, x1, 4, xsq)
            act.wait_ge(xrs, 3)
            for i in range(2):
                for t in range(T):
                    act.wait_ge(gate_pe, T * i + t + 1)
                    e.activation(f8[:, 4 * i + 2 * t:4 * i + 2 * t + 2].rearrange("p c s -> p (c s)"),
                                 pj[:, i, 512 * t:512 * t + 512], ACT.Sigmoid, scale=nrm[:, 4 + t:5 + t])\
                        .then_inc(pl_sig, 1)

        @block.vector
        def _(dve):
            w = nc.vector
            st = Steps(dve, dve_step)

            def split_lo(i, b=0):
                dve.wait_ge(hi_done, b * PER_BLOCK + (i + 1))
                w.tensor_tensor(wlo[:, i % NRAW, :], raw[:, i % NRAW, :], whi[:, i % NSPL, :].bitcast(F32),
                                ALU.subtract).then_inc(lo_done, 1)
            dve.wait_ge(small_in, 160)
            w.tensor_copy(smt[64:80, :].rearrange("p (g s) -> p g s", g=2),
                          lst[64:80, :].unsqueeze(2).to_broadcast([16, 2, NST])).then_inc(ls_done, 1)
            dve.wait_ge(vec_in, 32)
            lq = lamq[:].rearrange("o (a b d) -> o a b d", a=2, b=2)
            lp = lamp[:].rearrange("o (a d) -> o a d", a=2)
            st.do(w.tensor_tensor(lp, lq[:, :, 0], lq[:, :, 1], ALU.mult))
            w.reduce_sum(lams[0:1, 0:2], lp, AX).then_inc(lam_row, 1)

            dve.wait_ge(xrs, 1)
            for t in range(T):
                ins = w.tensor_scalar(xn[:, t], xin[:, t], nrm[:, t:t + 1], None, ALU.mult)
            ins.then_inc(xnd, 1)
            split_lo(0)
            dve.wait_ge(lam_exp, 1)
            st.do(w.tensor_tensor(lams[0:1, 0:1], lams[0:1, 2:3], lams[0:1, 3:4], ALU.subtract))
            w.tensor_scalar(lams[0:1, 0:1], lams[0:1, 0:1], LAM_INIT, None, ALU.add).then_inc(lam_sum, 1)

            def chunks_lo(base, banks, gain, done):
                for k, bank in enumerate(banks):
                    dve.wait_ge(ah_done, base + 2 * k + 2)
                    for q in range(2):
                        c = 2 * k + q
                        ins = w.scalar_tensor_tensor(
                            out=al[:, c, :], in0=bank[:, q * S:q * S + S], scalar=gains[:, gain, c:c + 1],
                            in1=ah[:, c, :].bitcast(F32), op0=ALU.mult, op1=ALU.subtract)
                    if k % 2:
                        ins.then_inc(done[k // 2], 1)
            chunks_lo(0, xt_banks0, 0, pj_read)

            def V(i):
                return ss[:, i, :]

            def tt_(o, x, z, op):
                return w.tensor_tensor(o, x, z, op)
            dve.wait_ge(dt_done, 1)
            lr, li = col[:, C_LR:C_LR + 16], col[:, C_LI:C_LI + 16]
            st.add(tt_(V(1), lr, V(0), ALU.mult))
            st.do(tt_(V(2), li, V(0), ALU.mult))
            st.do(w.tensor_scalar(V(8), V(2), 1.0 / (2 * math.pi), None, ALU.mult))
            st.do(w.tensor_scalar(V(8), V(8), ROUND, None, ALU.add))
            st.do(w.tensor_scalar(V(8), V(8), -ROUND, None, ALU.add))
            for part in (PI2_HI, PI2_MID, PI2_LO):
                st.do(w.scalar_tensor_tensor(out=V(2), in0=V(8), scalar=-part, in1=V(2), op0=ALU.mult, op1=ALU.add))
            st.do(w.tensor_scalar(V(4), V(2), 3.1415925, -3.1415925, ALU.min, ALU.max))
            st.do(w.tensor_scalar(V(6), V(4), -1.0, None, ALU.mult))
            st.do(tt_(V(6), V(6), V(4), ALU.max))
            w.tensor_scalar(V(6), V(6), -1.0, math.pi / 2, ALU.mult, ALU.add).then_inc(th_done, 1)
            st.add(tt_(V(8), lr, lr, ALU.mult))
            st.do(tt_(V(9), li, li, ALU.mult))
            st.do(tt_(V(8), V(8), V(9), ALU.add))
            st.do(w.reciprocal(V(8), V(8)))
            dve.wait_ge(trig, 1)
            w.memset(ptab[:, 0, :, 0:1], 1.0).then_inc(re_done, 1)
            st.add(w.tensor_copy(pw[:, 0, 0, :], V(7)))
            st.do(w.tensor_copy(pw[:, 1, 0, :], V(5)))
            for i in range(LEVELS):
                c, s = pw[:, 0, i, :], pw[:, 1, i, :]
                st.add(tt_(V(18), c, c, ALU.mult))
                st.add(tt_(V(19), s, s, ALU.mult))
                st.do(tt_(V(20), c, s, ALU.mult))
                st.add(tt_(pw[:, 0, i + 1, :], V(18), V(19), ALU.subtract))
                ins = w.tensor_scalar(pw[:, 1, i + 1, :], V(20), 2.0, None, ALU.mult)
                st.do(ins)
            w.tensor_copy(ini[:, 0, 0:1], pw[:, 1, LEVELS, 0:1]).then_inc(pow_done, 1)
            split_lo(2)
            st.add(tt_(V(10), V(3), V(7), ALU.mult))
            st.do(tt_(V(11), V(3), V(5), ALU.mult))
            st.do(w.tensor_scalar(V(10), V(10), -1.0, None, ALU.add))
            st.add(tt_(V(12), V(10), lr, ALU.mult))
            st.add(tt_(V(13), V(11), li, ALU.mult))
            st.add(tt_(V(14), V(11), lr, ALU.mult))
            st.do(tt_(V(15), V(10), li, ALU.mult))
            st.add(tt_(V(12), V(12), V(13), ALU.add))
            st.do(tt_(V(14), V(14), V(15), ALU.subtract))
            st.add(tt_(V(12), V(12), V(8), ALU.mult))
            st.do(tt_(V(14), V(14), V(8), ALU.mult))

            split_lo(3)

            dve.wait_ge(bc_in, 96)
            dve.wait_ge(consts, 8)

            def spread(col_):
                return col_.unsqueeze(2).to_broadcast([P, ST, SH])
            st.add(tt_(bst[:, 2], bst[:, 0], spread(V(12)), ALU.mult))
            st.add(tt_(bm[:, 0, :, 0, :], bst[:, 1], spread(V(14)), ALU.mult))
            st.add(tt_(bst[:, 3], bst[:, 1], spread(V(12)), ALU.mult))
            st.do(tt_(bm[:, 0, :, 1, :], bst[:, 0], spread(V(14)), ALU.mult))
            st.add(tt_(bst[:, 2], bst[:, 2], bm[:, 0, :, 0, :], ALU.subtract))
            st.do(tt_(bst[:, 3], bst[:, 3], bm[:, 0, :, 1, :], ALU.add))
            for r in range(2):
                for gl in range(2):
                    ins = w.tensor_scalar(bm[:, r, :, gl, :], bst[:, 2 + r], mk[:, gl:gl + 1], None, ALU.mult)
            ins.then_inc(bm_done, 1)
            dve.wait_ge(pth_done, 1)
            tt_(ptl[:], tp[:].rearrange("p (c s) -> p c s", c=2), pth[:].bitcast(F32), ALU.subtract)\
                .then_inc(ptl_done, 1)

            for i in range(LEVELS):
                L, c_, s_, re, im, new = level(i, 0)
                t1 = tt[:].rearrange("p a n -> p (a n)")[:, 0:ST * L].rearrange("p (j l) -> p j l", j=ST)
                dve.wait_ge(im_done, i + 1)
                st.add(tt_(new, re, c_, ALU.mult))
                st.do(tt_(t1, im, s_, ALU.mult))
                tt_(new, new, t1, ALU.subtract).then_inc(re_done, 1)
                dve.wait_ge(re_done, i + 2)
                if i >= 3:
                    split_lo(P_QKV + i - 1)
            dve.wait_ge(im_done, LEVELS + 1)

            dve.wait_ge(c_pe, 1)
            for r, bank in enumerate((ov, tp)):
                src = bank[:].rearrange("p (j g h) -> p j g h", j=ST, g=2)
                dst = cm[:, r].rearrange("p j (g h) -> p j g h", g=2)
                for gl in range(2):
                    ins = w.tensor_scalar(dst[:, :, gl, :], src[:, :, gl, :], mk[:, 2 * r + gl:2 * r + gl + 1],
                                          None, ALU.mult)
            ins.then_inc(cm_done, 1)
            dve.wait_ge(lam_pe, 1)
            w.tensor_copy(lam[:], sc[:, 1, 0:1]).then_inc(lam_done, 1)

            def scan_pair(tiles, y_chunk):
                mark = {}

                def turns(ops):
                    for j in tiles:
                        if j in mark:
                            dve.wait_ge(dve_step, mark[j])
                        ops(j)
                        mark[j] = st.n

                def rotate(j):
                    b = j % 2
                    dve.wait_ge(bu_full, j + 1)
                    if j >= 4:
                        dve.wait_ge(rot_done, j - 3)
                    c, s = (ptab[:, i, j, :].unsqueeze(1).to_broadcast([P, 4, HALF]) for i in range(2))
                    bank = sc[:, b, :].rearrange("p (a t) -> p a t", a=4)
                    r, t2 = scans[j % 4], tt[:, b, :]
                    st.add(w.tensor_tensor(t2.rearrange("p (a t) -> p a t", a=4), bank, s, ALU.mult))
                    w.tensor_tensor(r.rearrange("p (a t) -> p a t", a=4), bank, c, ALU.mult).then_inc(bu_read, 1)

                def add_parts(j):
                    r, t2 = scans[j % 4], tt[:, j % 2, :]
                    dve.wait_ge(bu_read, j + 1)
                    st.add(tt_(r[:, 0:256], r[:, 0:256], t2[:, 256:512], ALU.add))
                    st.add(tt_(r[:, 256:512], r[:, 256:512], t2[:, 0:256], ALU.subtract))

                def scan(j, half):
                    r = scans[j % 4]
                    mag = ss[:, 3, j:j + 1].to_broadcast([P, HALF])
                    for n in range(2):
                        x = r[:, 256 * n + HALF * half:256 * n + HALF * half + HALF]
                        first = ini[:, j % 2, 2 + n:3 + n] if half else 0.0
                        ins = w.tensor_tensor_scan(x, mag, x, first, ALU.mult, ALU.add)
                        if not half:
                            st.add(ins)
                    if half:
                        ins.then_inc(scan_done, 1)

                def last(j):
                    r = scans[j % 4]
                    return r[:, HALF - 1:HALF], r[:, 256 + HALF - 1:256 + HALF], \
                        pw[:, 0, LEVELS, j:j + 1], pw[:, 1, LEVELS, j:j + 1], ini[:, j % 2, :]

                def frame_products(j):
                    re, im, c1, s1, x = last(j)
                    st.add(tt_(x[:, 0:1], im, s1, ALU.mult))
                    st.add(tt_(x[:, 1:2], re, s1, ALU.mult))

                def frame_sums(j):
                    re, im, c1, s1, x = last(j)
                    st.add(w.scalar_tensor_tensor(out=x[:, 2:3], in0=re, scalar=c1, in1=x[:, 0:1],
                                                  op0=ALU.mult, op1=ALU.subtract))
                    st.add(w.scalar_tensor_tensor(out=x[:, 3:4], in0=im, scalar=c1, in1=x[:, 1:2],
                                                  op0=ALU.mult, op1=ALU.add))
                turns(rotate)
                turns(add_parts)
                if y_chunk is not None:
                    y_evac(y_chunk)
                for ops in (lambda j: scan(j, 0), frame_products, frame_sums, lambda j: scan(j, 1)):
                    turns(ops)
                dve.wait_ge(scan_done, tiles[0] + 1)
                dve.wait_ge(scan_done, tiles[1] + 1)

            def y_evac(c):
                dve.wait_ge(y_pe, 4 * c + 4)
                dve.wait_ge(pj_read[G_U % 2], read_count(G_U))
                w.scalar_tensor_tensor(out=y[:, c, :], in0=uT[:, c, :], scalar=col[:, C_D + c:C_D + c + 1],
                                       in1=ov[:, 0:S], op0=ALU.mult, op1=ALU.add).then_inc(y_read, 1)

            def last_rotated_back():
                c, s = (ptab[:, i, ST - 1, :].unsqueeze(1).to_broadcast([P, 4, HALF]) for i in range(2))
                r4 = scans[(ST - 1) % 4].rearrange("p (a t) -> p a t", a=4)
                st.add(tt_(tt[:, 0, :].rearrange("p (a t) -> p a t", a=4), r4, c, ALU.mult))
                st.do(tt_(tt[:, 1, :].rearrange("p (a t) -> p a t", a=4), r4, s, ALU.mult))
                st.add(tt_(tt[:, 0, 0:256], tt[:, 0, 0:256], tt[:, 1, 256:512], ALU.subtract))
                tt_(tt[:, 0, 256:512], tt[:, 0, 256:512], tt[:, 1, 0:256], ALU.add).then_inc(last_rot, 1)

            for k in range(5, max(YT_AT) + 1):
                c = YT_AT[k] // 4 if YT_AT.get(k, 0) % 4 == 3 else None
                if k in TILES_AT:
                    scan_pair(TILES_AT[k], c)
                    if k == max(TILES_AT):
                        last_rotated_back()
                elif c is not None:
                    y_evac(c)
                if k % 2 == 0 and 6 <= k < HALF_PIECES:
                    split_lo(P_QKV + k // 2 + AHEAD)

            yf, tf = y[:].rearrange("p k s -> p (k s)"), tt[:].rearrange("p a n -> p (a n)")

            def gelu_argument():
                dve.wait_ge(y_read, 4)
                st.do(tt_(tf, yf, yf, ALU.mult))
                st.do(w.tensor_scalar(tf, tf, 0.044715, 1.0, ALU.mult, ALU.add))
                tt_(tf, tf, yf, ALU.mult).then_inc(gelu_in, 1)

            def gelu_product():
                dve.wait_ge(gelu_sig, 1)
                tt_(yf, yf, tf, ALU.mult).then_inc(z_done, 1)

            for j in range(HEADS + 3):
                if j >= 3:
                    dve.wait_ge(oh_done, j - 2)
                    w.scalar_tensor_tensor(out=ol[:, j - 3, :], in0=tp[:, 0:S], scalar=subg[:, 0:1],
                                           in1=oh[:, j - 3, :].bitcast(F32), op0=ALU.mult, op1=ALU.subtract)\
                        .then_inc(ol_done, 1)
                if j == 0:
                    gelu_argument()
                if j == HEADS:
                    dve.wait_ge(pj_read[G_GLU % 2], read_count(G_GLU))
                    tt_(y[:], y[:], f8[:, 0:4, :], ALU.mult).then_inc(z_done, 1)
                if j < HEADS:
                    dve.wait_ge(s_full, j + 1)
                    for m in range(2):
                        for qb, (k0, k1) in enumerate(((0, P), (P, 3 * P))):
                            ins = st.add(w.tensor_tensor_reduce(
                                out=sm[:, m, k0:k1], in0=sc[:, m, k0:k1], in1=mask[:, 2 * P - (k1 - k0):2 * P],
                                scale=1.0, scalar=-3e38, op0=ALU.add, op1=ALU.max,
                                accum_out=att[:, 2 * m + qb:2 * m + qb + 1]))
                    st.wait()
                    w.tensor_scalar(att[:, 4:8], att[:, 0:4], -SCALE, None, ALU.mult).then_inc(max_done, 1)
                if j < HEADS + 2:
                    split_lo(P_G + j + AHEAD)
                if j == 0:
                    gelu_product()
                if j in (1, HEADS):
                    dve.wait_ge(z_hi, 1 if j == 1 else 2)
                    tt_(zl[:], y[:], zh[:].bitcast(F32), ALU.subtract).then_inc(z_lo, 1)
                if j < HEADS:
                    dve.wait_ge(e_done, j + 1)
                    if j == 0:
                        dve.wait_ge(lam_done, 1)
                    st.do(w.reciprocal(att[:, 12:16], att[:, 8:12]))
                    st.do(w.tensor_scalar(att[:, 16:18], att[:, 14:16], lam[:, 0:1], -1.0, ALU.mult, ALU.mult))
                    if j:
                        dve.wait_ge(wt_pe, j)
                    for qb, (k0, k1) in enumerate(((0, P), (P, 3 * P))):
                        st.add(w.tensor_scalar(ww[:, k0:k1], ee[:, 0, k0:k1], att[:, 12 + qb:13 + qb], None, ALU.mult))
                    st.wait()
                    for qb, (k0, k1) in enumerate(((0, P), (P, 3 * P))):
                        ins = w.scalar_tensor_tensor(out=ww[:, k0:k1], in0=ee[:, 1, k0:k1],
                                                     scalar=att[:, 16 + qb:17 + qb], in1=ww[:, k0:k1],
                                                     op0=ALU.mult, op1=ALU.add)
                    ins.then_inc(w_done, 1)
                if 1 <= j <= HEADS:
                    dve.wait_ge(o_rs, j)
                    if j >= 2:
                        dve.wait_ge(ot_pe, j - 1)
                    for qb in range(2):
                        ins = w.tensor_scalar(on[:, qb, :], ov[:, qb * P:qb * P + P], oss[:, qb:qb + 1], None, ALU.mult)
                    ins.then_inc(o_done, 1)

            def pair(i, G):
                full(dve, G)
                return pj[:, G % 2, :].rearrange("p (c s) -> p c s", c=4)
            for n in range(P_UP + 1, N_PRE):
                if n == P_PLE:
                    dve.wait_ge(xres_in, 16)
                    for i in range(2):
                        G = G_WO + i
                        full(dve, G)
                        xs = x1[:, :, 512 * i:512 * i + 512]
                        tt_(xs, xs, pj[:, G % 2, :].rearrange("p (t n) -> p t n", t=T), ALU.add)\
                            .then_inc(pj_read[G % 2], 1)
                    for k in range(2):
                        dve.wait_ge(xt_pe, 4 + k + 1)
                        w.tensor_copy(f8[:, 2 * k:2 * k + 2].rearrange("p c s -> p (c s)"), xt_banks[k])\
                            .then_inc(f8_done, 1)
                split_lo(n + AHEAD)
                if n in (P_UP + 1, P_UP + 2):
                    i = n - P_UP - 1
                    dve.wait_ge(g_sig, 2)
                    tt_(gT[:, 8 + 4 * i:12 + 4 * i], gT[:, 8 + 4 * i:12 + 4 * i], pair(i, G_UP + i), ALU.mult)\
                        .then_inc(pj_read[(G_UP + i) % 2], 1)
                if n in (P_AT + 2, P_WO):
                    i = 0 if n < P_WO else 1
                    tt_(gT[:, 4 * i:4 * i + 4], gT[:, 4 * i:4 * i + 4], pair(i, G_AT + i), ALU.mult)\
                        .then_inc(pj_read[(G_AT + i) % 2], 1)
                    dve.wait_ge(pj_read[(G_AT + i) % 2], read_count(G_AT + i))
                    dve.wait_ge(pj_read[(G_UP + i) % 2], read_count(G_UP + i))
                    tt_(gT[:, 4 * i:4 * i + 4], gT[:, 4 * i:4 * i + 4], gT[:, 8 + 4 * i:12 + 4 * i], ALU.add)\
                        .then_inc(mix_done, 1)
                    dve.wait_ge(ah_done, 9 + i)
                    tt_(al[:, 4 * i:4 * i + 4], gT[:, 4 * i:4 * i + 4], ah[:, 4 * i:4 * i + 4].bitcast(F32),
                        ALU.subtract).then_inc(al_done, 1)
                if n == P_WO:
                    dve.wait_ge(router_in, 16 * 9)
                    tt_(wr[:], wr[:], gains[:, 1, :].unsqueeze(2).to_broadcast([P, KC, 36]), ALU.mult)\
                        .then_inc(wr_done, 1)

            dve.wait_ge(lg_pe, 1)
            dve.wait_ge(xrs, 2)

            def R(k0, k1):
                return rt[:, :, k0:k1]

            def wide(k, n):
                return rt[:, :, k:k + 1].to_broadcast([P, T, n])
            logits = ov[:, 0:128].rearrange("p (t n) -> p t n", t=T)[:, :, 0:36]
            for t in range(T):
                st.add(w.scalar_tensor_tensor(out=rt[:, t, 0:36], in0=logits[:, t, :], scalar=nrm[:, 2 + t:3 + t],
                                              in1=wrb[:], op0=ALU.mult, op1=ALU.add))
            st.wait()
            st.add(w.tensor_scalar(desc[:], iota[:, 0:NE], -1.0, float(NE), ALU.mult, ALU.add))
            st.do(w.reduce_max(R(36, 37), R(0, 4), AX))

            def first_max(vals, k_max, n, dst):
                st.do(tt_(dst, vals, wide(k_max, n), ALU.is_equal))
                st.do(tt_(dst, dst, desc[:, 0:n].unsqueeze(1).to_broadcast([P, T, n]), ALU.mult))
                st.do(w.reduce_max(R(37, 38), dst, AX))
                return tt_(dst, dst, wide(37, n), ALU.is_equal)
            tt_(R(44, 48), R(0, 4), wide(36, 4), ALU.subtract).then_inc(lg_in, 1)
            first_max(R(0, 4), 36, NG, R(56, 60)).then_inc(grp_done, 1)
            dve.wait_ge(grp_done, 1)
            dve.wait_ge(xnh_done, 1)
            tt_(xnl[:], x1[:], xnh[:].bitcast(F32), ALU.subtract).then_inc(xnl_done, 1)

            dve.wait_ge(rank_pe, 1)
            ranks = ov[:, 128:136].rearrange("p (t n) -> p t n", t=T)
            st.do(tt_(R(40, 44), ranks, R(56, 60), ALU.mult))
            st.add(w.tensor_scalar(cnt[:, 0:4], ov[:, 136:140], float(P), None, ALU.is_gt))
            st.do(w.reduce_sum(R(95, 96), R(40, 44), AX))
            st.add(w.tensor_copy(slotc[:, :, 0:NG], wide(95, NG)))
            st.add(w.tensor_copy(ohc[:, :, 0:NG], R(56, 60)))
            st.add(w.tensor_scalar(slotc[:, :, NG:NG + 1], R(95, 96), -float(P), None, ALU.add))
            st.add(w.tensor_scalar(ohc[:, :, NG:NG + 1], R(95, 96), float(P), None, ALU.is_ge))
            st.add(w.reduce_sum(cnt[:, 4:5], cnt[:, 0:4], AX))
            st.do(tt_(cnt[:, 0:4], cnt[:, 0:4], iota[:, 0:4], ALU.mult))
            st.add(w.tensor_scalar(cnt[:, 4:5], cnt[:, 4:5], float(NG), None, ALU.add))
            st.do(w.reduce_sum(cnt[:, 5:6], cnt[:, 0:4], AX))
            w.tensor_copy(plan[:], cnt[:, 4:6]).then_inc(plan_done, 1)

            def one_hot(b):
                for t in range(T):
                    ins = w.tensor_scalar(pm[:, t, :], iota[:], slotc[:, t, bass.ds(b, 1)], ohc[:, t, bass.ds(b, 1)],
                                          ALU.is_equal, ALU.mult)
                ins.then_inc(m_pm, 1)

            def tokens_scaled(base):
                for h in range(2):
                    dve.wait_ge(m_gat, base + (h + 1))
                    c = slice(KC // 2 * h, KC // 2 * h + KC // 2)
                    tt_(hgf[:, c], pj[:, 1, 512 * h:512 * h + 512].rearrange("p (c s) -> p c s", c=KC // 2),
                        gains[:, 1, c].unsqueeze(2).to_broadcast([P, KC // 2, P]), ALU.mult).then_inc(m_hgf, 1)

            def tokens_lo(base):
                for h in range(2):
                    dve.wait_ge(m_hgh, base + (h + 1))
                    c = slice(KC // 2 * h, KC // 2 * h + KC // 2)
                    tt_(hgl[:, c], hgf[:, c], hgh[:, c].bitcast(F32), ALU.subtract).then_inc(m_hgl, 1)
            one_hot(0)

            le = R(4, 36).rearrange("p t (n e) -> p t n e", n=NG)
            prod = R(96, 128).rearrange("p t (n e) -> p t n e", n=NG)
            st.do(tt_(prod, le, R(56, 60).unsqueeze(3).to_broadcast([P, T, NG, NE]), ALU.mult))
            st.do(w.reduce_sum(R(60, 68), prod.rearrange("p t n e -> p t e n"), AX))
            st.do(w.reduce_max(R(68, 69), R(60, 68), AX))
            st.do(first_max(R(60, 68), 68, NE, R(72, 80)))
            st.do(w.scalar_tensor_tensor(out=R(60, 68), in0=R(72, 80), scalar=NEG, in1=R(60, 68),
                                         op0=ALU.mult, op1=ALU.add))
            st.do(w.reduce_max(R(69, 70), R(60, 68), AX))
            st.do(first_max(R(60, 68), 69, NE, R(80, 88)))
            tt_(R(89, 90), R(69, 70), R(68, 69), ALU.subtract).then_inc(lg_in, 1)
            dve.wait_ge(lg_exp, 2)
            st.do(w.reduce_sum(R(52, 53), R(48, 52), AX))
            st.add(w.reciprocal(R(53, 54), R(52, 53)))
            st.do(w.tensor_scalar(R(91, 92), R(90, 91), 1.0, None, ALU.add))
            st.do(w.reciprocal(R(92, 93), R(91, 92)))
            st.do(tt_(R(93, 94), R(92, 93), R(53, 54), ALU.mult))
            for t in range(T):
                r = nrm[:, 2 + t:3 + t]
                st.add(w.tensor_scalar(rt[:, t, 93:94], rt[:, t, 93:94], r, r, ALU.mult, ALU.mult))
            st.add(w.tensor_copy(wl8[:, :, NE:NE + 1], nrm[:, 2:4].unsqueeze(2)))
            st.wait()
            st.do(tt_(R(94, 95), R(93, 94), R(90, 91), ALU.mult))
            for t in range(T):
                st.add(w.tensor_scalar(wl8[:, t, 0:NE], rt[:, t, 72:80], rt[:, t, 93:94], None, ALU.mult))
            st.wait()
            for t in range(T):
                ins = w.scalar_tensor_tensor(out=wl8[:, t, 0:NE], in0=rt[:, t, 80:88], scalar=rt[:, t, 94:95],
                                             in1=wl8[:, t, 0:NE], op0=ALU.mult, op1=ALU.add)
            ins.then_inc(wl_done, 1)
            tokens_scaled(0)
            tokens_lo(0)

            nb = dve.value_load(plan[0:1, 0:1], min_val=NG, max_val=NG + 1)
            with dve.Fori(0, nb) as b:
                def act_lo(x):
                    dve.wait_ge(m_ach, b * NE + (x + 1))
                    tt_(acl[:, x % 2], tp[:, 0:FF].rearrange("p (r n) -> p r n", r=2), ach[:, x % 2].bitcast(F32), ALU.subtract)\
                        .then_inc(m_acl, 1)

                def tokens_added(t, base, pair=1):
                    dve.wait_ge(m_sc, base + (t + 1))
                    tt_(x1[:, t, :], x1[:, t, :], pj[:, pair, :], ALU.add).then_inc(m_add, 1)
                for i, (kind, x, h) in enumerate(MOE):
                    if kind == "g" and h == 1 and x >= 1:
                        act_lo(x - 1)
                    if kind == "d" and x == NE - 2:
                        act_lo(NE - 1)
                    if i in (2, 4):
                        tokens_added(i // 2 - 1, b * T)
                    last = kind == "g" and h == 1 and x == NE - 1
                    if not last:
                        split_lo(N_PRE + i + AHEAD, b)
                    if i == 0:
                        dve.wait_ge(m_ptp, b + 1)
                        w.tensor_copy(wc[:], ov[:, 400:400 + NE + 1]).then_inc(m_wc, 1)
                    if i == 12:
                        one_hot(b + 1)
                    if i == 18:
                        tokens_scaled(b * 2 + 2)
                    if kind == "g" and h == 1:
                        if x == 0:
                            dve.wait_ge(m_wc, b + 1)
                        gu = pj[:, 0, 512 * (x % 2):512 * (x % 2) + 512]
                        dve.wait_ge(m_sig, b * NE + (x + 1))
                        w.scalar_tensor_tensor(out=a1[:], in0=gu[:, 0:FF], scalar=wc[:, x:x + 1], in1=sg[:],
                                               op0=ALU.mult, op1=ALU.mult).then_inc(moe_step, 1)
                        dve.wait_ge(moe_step, b * NE + (x + 1))
                        tt_(ac[:, x % 2, :], a1[:], gu[:, FF:2 * FF], ALU.mult).then_inc(m_act, 1)
                    if last:
                        split_lo(N_PRE + i + AHEAD, b)
                    if kind == "d" and x == NE - 2:
                        tokens_lo(b * 2 + 2)
                for q in range(2):
                    dve.wait_ge(m_yh, b * 2 + (q + 3))
                    tt_(yl[:, 512 * q:512 * q + 512], sc[:, q, :], yh[:, 512 * q:512 * q + 512].bitcast(F32),
                        ALU.subtract).then_inc(m_yl, 1)
            for t in range(T):
                tokens_added(t, nb * T, t)

            chunks_lo(10, xt_banks, 2, [al_done, al_done])
            split_lo(N_PRE + 3, nb)
            for i in range(2):
                for t in range(T):
                    dve.wait_ge(pl_sig, T * i + t + 1)
                    sgm = f8[:, 4 * i + 2 * t:4 * i + 2 * t + 2].rearrange("p c s -> p (c s)")
                    st.do(tt_(sgm, sgm, pp[:, t, 512 * i:512 * i + 512], ALU.mult))
                    xs = x1[:, t, 512 * i:512 * i + 512]
                    tt_(xs, xs, sgm, ALU.add).then_inc(o_ready, 1)

        @block.tensor
        def _(pe):
            m = nc.tensor

            def mm3(o, lh, ll, rh, rl, start, stop):
                m.matmul(o, lh, rh, start=start, stop=False, skip_group_check=True)
                m.matmul(o, lh, rl, start=False, stop=False, skip_group_check=True)
                return m.matmul(o, ll, rh, start=False, stop=stop, skip_group_check=True)

            def split(i):
                return [t.rearrange("p (c n) -> p c n", c=4) for t in parts(i)]

            def parts(i):
                return whi[:, i % NSPL, :], wlo[:, i % NRAW, :]

            def ready(i, b=0):
                if i in LO_BY_POOL:
                    pe.wait_ge(lo_pool, i)
                else:
                    pe.wait_ge(lo_done, b * PER_BLOCK + (i + 1 - (len(LO_BY_POOL) if i else 0)))

            def pair_free(G):
                pe.wait_ge(pj_read[G % 2], read_count(G) - 1)

            def by_width(i, G, rhs, part, blocks, last):
                wh, wl = split(i)
                for blk in blocks:
                    o = pj[:, G % 2, blk * S:blk * S + S]
                    for c in range(4):
                        cg = 4 * part[0] + c
                        ins = mm3(o, wh[:, c, blk * P:blk * P + P], wl[:, c, blk * P:blk * P + P],
                                  rhs[0][:, cg, :], rhs[1][:, cg, :],
                                  start=(part[0] == 0 and c == 0 and blk % 2 == 0),
                                  stop=(part[0] == part[1] - 1 and c == 3))
                if last:
                    ins.then_inc(piece_used, 1)
                return ins

            def by_token(o, i, t, part, b=0):
                wh, wl = split(i)
                for c in range(4):
                    cg = 4 * part[0] + c
                    ins = mm3(o, ah[:, cg, t * P:t * P + P], al[:, cg, t * P:t * P + P], wh[:, c, :], wl[:, c, :],
                                start=(part[0] == 0 and c == 0), stop=(part[0] == part[1] - 1 and c == 3))
                return ins

            pe.wait_ge(consts, 8)
            pe.wait_ge(small_in, 160)
            pe.wait_ge(ls_done, 1)
            m.transpose(ov[:, 0:80], smt[:], ident[0:80, 0:80]).then_inc(small_pe, 1)

            def transposes(src, banks, done):
                for k, bank in enumerate(banks):
                    for q in range(2):
                        for t in range(T):
                            ins = m.transpose(bank[:, q * S + t * P:q * S + t * P + P], src[:, t, 2 * k + q::KC],
                                              ident[:])
                    ins.then_inc(done, 1)
            pe.wait_ge(xnd, 1)
            transposes(xn, xt_banks0, xt_pe)
            pe.wait_ge(p_in, 16)
            for c in range(2):
                for t in range(T):
                    ins = m.transpose(tp[:, c * S + t * P:c * S + t * P + P], pst[:, t, c::2], ident[:])
            ins.then_inc(pt_pe, 1)
            for h in range(2):
                ready(P_U + h)
                if h == 0:
                    pe.wait_ge(pj_read[0], 1)
                    pe.wait_ge(pj_read[1], 1)
                by_width(P_U + h, G_U, (ah, al), (h, 2), range(4), True)

            def b_and_c_transposed():
                pe.wait_ge(bm_done, 1)
                for r in range(2):
                    for k in range(4):
                        ins = m.transpose(sc[:, r, k * P:k * P + P],
                                          bm[:, r, 4 * k:4 * k + 4].rearrange("p j g h -> p (j g h)"), ident[:])
                ins.then_inc(b_pe, 1)
                pe.wait_ge(col_done, 1)
                pe.wait_ge(ptl_done, 1)
                for r, bank in enumerate((ov, tp)):
                    for k in range(4):
                        ins = m.transpose(bank[:, k * P:k * P + P], cst[:, r, k, :], ident[:])
                ins.then_inc(c_pe, 1)

            def lambda_spread():
                pe.wait_ge(lam_sum, 1)
                pe.wait_ge(bT_done, 2)
                m.matmul(sc[:, 1, 0:1], ones[0:1, :], lams[0:1, 0:1], start=True, stop=True).then_inc(lam_pe, 1)

            def state_inputs(j):
                b, q, k = j % 2, 32 * (j % 4), j // 4
                if j == 0:
                    pe.wait_ge(pj_read[G_U % 2], read_count(G_U))
                if j == 1:
                    pe.wait_ge(lam_done, 1)
                if j >= 2:
                    pe.wait_ge(bu_read, j - 1)
                for r in range(2):
                    ins = m.matmul(sc[:, b, r * S:r * S + S], bT[q:q + 32, r, k, :], uT[q:q + 32, k, :],
                                   start=True, stop=True)
                ins.then_inc(bu_full, 1)

            def state_outputs(j):
                b, q, k = j % 2, 32 * (j % 4), j // 4
                if j == 0:
                    pe.wait_ge(cm_done, 1)
                elif j % 4 == 0:
                    pe.wait_ge(y_read, k)
                if j < ST - 1:
                    pe.wait_ge(rot_done, j + 1)
                    states = so[:, b, :]
                else:
                    pe.wait_ge(last_rot, 1)
                    states = tt[:, 0, :]
                for r in range(2):
                    ins = m.matmul(ov[q:q + 32, 0:S], cm[:, r, j, :], states[:, r * S:r * S + S],
                                   start=(r == 0), stop=(r == 1), skip_group_check=True)
                ins.then_inc(y_pe, 1)

            def qk_transposes(i, half):
                pe.wait_ge(pj_read[(G_Q + i) % 2], read_count(G_Q + i))
                if 2 * i + half:
                    pe.wait_ge(qt_done, 2 * i + half)
                for q in range(2):
                    for t in range(T):
                        hd = (2 * half + q) * P
                        ins = m.transpose(tp[:, q * S + t * P:q * S + t * P + P], qn[:, t, hd:hd + P], ident[:])
                ins.then_inc(qt_pe, 1)

            for n in range(P_QKV, P_G):
                G = G_Q + (n - P_QKV) // 2
                part = ((n - P_QKV) % 2, 2)
                ready(n)
                if part[0] == 0:
                    pair_free(G)
                for t in range(T):
                    ins = by_token(pj[:, G % 2, 512 * t:512 * t + 512], n, t, part)
                    if t == T - 1:
                        ins.then_inc(piece_used, 1)
                    k = 2 * (n - P_QKV) + t
                    if k == 2:
                        b_and_c_transposed()
                    if k == 5:
                        lambda_spread()
                    for j in TILES_AT.get(k, ()):
                        state_inputs(j)
                    if k in YT_AT:
                        state_outputs(YT_AT[k])
                    if k in QT_AT:
                        qk_transposes(*QT_AT[k])
            state_outputs(ST - 1)

            def scores(h):
                if h == 0:
                    pe.wait_ge(qt_done, 8)
                    pe.wait_ge(bu_read, ST)
                else:
                    pe.wait_ge(max_done, h)
                for mp in range(2):
                    r = slice(DH * mp, DH * mp + DH)
                    m.matmul(sc[:, mp, 0:P], qT[r, h, 0:P], kT[r, h, 0:P], start=True, stop=True)
                    ins = m.matmul(sc[:, mp, P:3 * P], qT[r, h, P:S], kT[r, h, :], start=True, stop=True)
                ins.then_inc(s_full, 1)

            def weights_transposed(h):
                pe.wait_ge(w_done, h + 1)
                if h >= 2:
                    pe.wait_ge(ol_done, h - 1)
                for q in range(3):
                    ins = m.transpose(tp[:, q * P:q * P + P], ww[:, q * P:q * P + P], ident[:])
                ins.then_inc(wt_pe, 1)

            def values(h):
                pe.wait_ge(wt_done, h + 1)
                if h == 0:
                    pe.wait_ge(y_read, 4)
                    pe.wait_ge(pj_read[G_V % 2], read_count(G_V))
                    pe.wait_ge(pj_read[(G_V + 1) % 2], read_count(G_V + 1))
                else:
                    pe.wait_ge(o_done, h)
                e = slice(P * h, P * h + P)
                m.matmul(ov[:, 0:P], wT[:, 0:P], v[:, 0, e], start=True, stop=True)
                m.matmul(ov[:, P:2 * P], wT[:, P:2 * P], v[:, 0, e], start=True, stop=False)
                m.matmul(ov[:, P:2 * P], wT[:, 2 * P:3 * P], v[:, 1, e], start=False, stop=True).then_inc(o_full, 1)

            def outputs_transposed(h):
                pe.wait_ge(o_done, h + 1)
                if h == HEADS - 1:
                    pe.wait_ge(ol_done, h)
                for t in range(T):
                    ins = m.transpose(tp[:, t * P:t * P + P], on[:, t, :], ident[:])
                ins.then_inc(ot_pe, 1)

            for j in range(HEADS + 2):
                n = P_G + j
                ready(n)
                if n == P_GLU:
                    G, rhs, part = G_GLU, (zh, zl), (0, 1)
                    pe.wait_ge(z_lo, 1)
                elif n == P_UP:
                    G, rhs, part = G_UP, (zh, zl), (0, 1)
                    pe.wait_ge(z_lo, 2)
                else:
                    i = j - (n > P_GLU)
                    G, rhs, part = G_G[i // 2], (ah, al), (i % 2, 2)
                if part[0] == 0:
                    pair_free(G)
                by_width(n, G, rhs, part, (0, 1), False)
                if j < HEADS:
                    scores(j)
                if 1 <= j <= HEADS:
                    weights_transposed(j - 1)
                by_width(n, G, rhs, part, (2, 3), True)
                if 1 <= j <= HEADS:
                    values(j - 1)
                if j >= 2:
                    outputs_transposed(j - 2)

            ready(P_UP + 1)
            pair_free(G_UP + 1)
            by_width(P_UP + 1, G_UP + 1, (zh, zl), (0, 1), range(4), True)
            for n in range(P_AT, P_WO):
                G = G_AT + (n - P_AT) // 2
                ready(n)
                pair_free(G)
                pe.wait_ge(ol_done, HEADS)
                by_width(n, G, (oh, ol), ((n - P_AT) % 2, 2), range(4), True)
            for n in range(P_WO, P_PLE):
                G, h = G_WO + (n - P_WO) % 2, (n - P_WO) // 2
                ready(n)
                if h == 0:
                    pair_free(G)
                pe.wait_ge(al_done, h + 1)
                for t in range(T):
                    ins = by_token(pj[:, G % 2, 512 * t:512 * t + 512], n, t, (h, 2))
                ins.then_inc(piece_used, 1)

            for i in range(2):
                pe.wait_ge(pj_read[i], read_count(G_WO))
            transposes(x1, xt_banks, xt_pe)

            def embedding(t):
                wh, wl_ = (part.rearrange("p (c n) -> p c n", c=2) for part in parts(P_PLE))
                for q in range(2):
                    for c in range(2):
                        ins = mm3(pj[:, (G_PLE + t) % 2, 512 * q:512 * q + 512],
                                  pth[:, c, t * P:t * P + P], ptl[:, c, t * P:t * P + P],
                                  wh[:, c, 512 * q:512 * q + 512], wl_[:, c, 512 * q:512 * q + 512],
                                  start=(c == 0), stop=(c == 1))
                return ins
            ready(P_PLE)
            embedding(1).then_inc(ple_pe, 1)
            pe.wait_ge(f8_done, 4)
            pe.wait_ge(wr_done, 1)
            for t in range(T):
                for c in range(KC):
                    ins = m.matmul(ov[:, 64 * t:64 * t + 36], f8[:, c, t * P:t * P + P], wr[:, c, :],
                                   start=(c == 0), stop=(c == KC - 1))
            ins.then_inc(lg_pe, 1)
            embedding(0).then_inc(piece_used, 1)

            pe.wait_ge(grp_done, 1)
            g0, g1 = rt[:, 0, 56:60], rt[:, 1, 56:60]
            m.matmul(ov[:, 128:132], upper[:], g0, start=True, stop=True)
            m.matmul(ov[:, 132:136], ones[:], g0, start=True, stop=False)
            m.matmul(ov[:, 132:136], upper[:], g1, start=False, stop=True)
            m.matmul(ov[:, 136:140], ones[:], g0, start=True, stop=False)
            m.matmul(ov[:, 136:140], ones[:], g1, start=False, stop=True).then_inc(rank_pe, 1)

            def gather():
                for c in range(KC):
                    o = pj[:, 1, c * P:c * P + P]
                    for t in range(T):
                        m.matmul(o, xnh[:, t, c::KC], pm[:, t, :], start=(t == 0), stop=False)
                        ins = m.matmul(o, xnl[:, t, c::KC], pm[:, t, :], start=False, stop=(t == T - 1))
                    if c % (KC // 2) == KC // 2 - 1:
                        ins.then_inc(m_gat, 1)
            pe.wait_ge(xnh_done, 1)
            pe.wait_ge(xnl_done, 1)
            pe.wait_ge(m_pm, 1)
            pe.wait_ge(pj_read[(G_PLE + 1) % 2], read_count(G_PLE + 1))
            gather()
            pe.wait_ge(wl_done, 1)
            pe.wait_ge(pj_read[G_PLE % 2], read_count(G_PLE))
            pe.wait_ge(plan_done, 1)
            nb = pe.value_load(plan[0:1, 0:1], min_val=NG, max_val=NG + 1)

            def scatter(t, pair=1, halves=None):
                for q in range(2):
                    if halves is not None:
                        pe.wait_ge(m_yl, halves + (q + 1))
                    o = pj[:, pair, 512 * q:512 * q + 512]
                    m.matmul(o, pT[:, t * P:t * P + P], yh[:, 512 * q:512 * q + 512], start=True, stop=False)
                    ins = m.matmul(o, pT[:, t * P:t * P + P], yl[:, 512 * q:512 * q + 512],
                                   start=False, stop=True)
                ins.then_inc(m_sc, 1)

            def slots_to_tokens():
                for t in range(T):
                    m.transpose(ov[:, t * P:t * P + P], pm[:, t, :].bitcast(F32), ident[:])
                for t in range(T):
                    ins = m.matmul(ov[:, 400:400 + NE + 1], pm[:, t, :].bitcast(F32), wl8[:, t, :],
                                   start=(t == 0), stop=(t == T - 1))
                ins.then_inc(m_ptp, 1)
            slots_to_tokens()
            pe.wait_ge(m_yh, 2)
            pe.wait_ge(m_pt, 1)
            with pe.Fori(0, nb) as b:
                def act_transposes(x):
                    pe.wait_ge(m_act, b * NE + (x + 1))
                    if x == 0:
                        pe.wait_ge(m_wc, b + 1)
                    for r in range(2):
                        ins = m.transpose(tp[:, r * P:r * P + P], ac[:, x % 2, r::2], ident[:])
                    ins.then_inc(m_tp, 1)
                for i, (kind, x, h) in enumerate(MOE):
                    ready(N_PRE + i, b)
                    if kind == "g":
                        if x == 0:
                            pe.wait_ge(m_hgl, b * 2 + (h + 1))
                        wh, wl_ = (t.rearrange("p (w c n) -> p w c n", w=2, c=4) for t in parts(N_PRE + i))
                        o = pj[:, 0, 512 * (x % 2):512 * (x % 2) + 512].rearrange("p (w n) -> p w n", w=2)
                        for c in range(4):
                            ins = mm3(o, hgh[:, 4 * h + c, :], hgl[:, 4 * h + c, :], wh[:, :, c, :], wl_[:, :, c, :],
                                      start=(h == 0 and c == 0), stop=(h == 1 and c == 3))
                        ins.then_inc(piece_used, 1)
                        if h == 0 and x >= 1:
                            act_transposes(x - 1)
                    else:
                        wh, wl_ = (t.rearrange("p (c n) -> p c n", c=2) for t in parts(N_PRE + i))
                        if x == NE - 1:
                            act_transposes(x)
                            pe.wait_ge(m_pt, b + 2)
                            slots_to_tokens()
                        pe.wait_ge(m_acl, b * NE + (x + 1))
                        for q in range(2):
                            for c in range(2):
                                ins = mm3(sc[:, q, :], ach[:, x % 2, c, :], acl[:, x % 2, c, :],
                                          wh[:, c, 512 * q:512 * q + 512], wl_[:, c, 512 * q:512 * q + 512],
                                          start=(x == 0 and c == 0), stop=(x == NE - 1 and c == 1))
                            if x == NE - 1 and q == 0:
                                ins.then_inc(y_first, 1)
                        ins.then_inc(piece_used, 1)
                    if i == 1:
                        pe.wait_ge(m_yl, b * 2 + 2)
                        pe.wait_ge(m_hgf, b * 2 + 2)
                        scatter(0)
                    if i == 3:
                        pe.wait_ge(m_add, b * T + 1)
                        scatter(1)
                    if i == 14:
                        pe.wait_ge(m_pm, b + 2)
                        pe.wait_ge(m_add, (b + 1) * T)
                        gather()
            pe.wait_ge(m_pt, nb + 1)
            pe.wait_ge(m_hgf, nb * 2 + 2)
            for t in range(T):
                scatter(t, t, nb * 2)

            pe.wait_ge(m_add, (nb + 1) * T)
            transposes(x1, xt_banks, xt3)
            for j in range(4):
                ready(N_PRE + j, nb)
                if j < 2:
                    pe.wait_ge(al_done, 3 + j)
                for t in range(T):
                    ins = by_token(pj[:, j // 2, 512 * t:512 * t + 512], N_PRE + j, t, (j % 2, 2))
                    if j % 2:
                        ins.then_inc(gate_pe, 1)
                if j % 2 == 0:
                    ins.then_inc(piece_used, 1)


_INS = ['x', 'p', 'attn_norm_g', 'w_in', 'b_gate', 'q_norm_g', 'k_norm_g', 'lam_qk', 'subln_g', 'w_attn_up',
        'ssm_lam_re', 'ssm_lam_im', 'ssm_log_step', 'ssm_b_re', 'ssm_b_im', 'ssm_c_re', 'ssm_c_im', 'ssm_d',
        'w_glu', 'b_glu', 'w_ssm_up', 'w_out', 'ffn_norm_g', 'w_router_group', 'b_router_group',
        'w_router_expert', 'b_router_expert', 'w_exp_gate', 'w_exp_up', 'w_exp_down',
        'ple_norm_g', 'w_ple_gate', 'w_ple']


def kernel(**inputs):
    import numpy as _np
    import concourse.bacc as _bacc
    from concourse import mybir as _mybir
    from concourse.bass_utils import run_bass_kernel_spmd as _run

    nc = _bacc.Bacc("TRN2", target_bir_lowering=False, num_devices=1)
    arrays, args = {}, {}
    for name in _INS:
        arr = _np.ascontiguousarray(inputs[name])
        arrays[f"in_{name}_dram"] = arr
        args[name] = nc.dram_tensor(f"in_{name}_dram", arr.shape, _mybir.dt.from_np(arr.dtype),
                                    kind="ExternalInput").ap()
    out = nc.dram_tensor("out_0_dram", (1, S, D), _mybir.dt.float32, kind="ExternalOutput").ap()
    build(nc, args, out)
    r = _run(nc, [arrays], core_ids=[0])
    return r.results[0]["out_0_dram"]
```
